# Optimizing a Trainium2 kernel written in Bass

```python
import jax, jax.numpy as jnp
from jax import lax
import numpy as np
import math

D_MODEL = 1024
BATCH = 1
SEQ = 512
DEPTH = 2

N_HEADS = 16
HEAD_DIM = D_MODEL // N_HEADS
HD = N_HEADS * HEAD_DIM
D_FF = ((8 * D_MODEL + 3 * 256 - 1) // (3 * 256)) * 256
PLE_DIM = 256
BLOCK_Q = 128
N_A = DEPTH // 2
N_B = DEPTH - N_A
EPS = 1e-6


def rms_norm(x, g):
    xf = x.astype(jnp.float32)
    y = xf * lax.rsqrt(jnp.mean(xf * xf, axis=-1, keepdims=True) + EPS)
    return (y * g.astype(jnp.float32)).astype(x.dtype)

def split_heads(t):
    b, s, _ = t.shape
    return t.reshape(b, s, N_HEADS, HEAD_DIM).transpose(0, 2, 1, 3)

def merge_heads(t):
    b, h, s, d = t.shape
    return t.transpose(0, 2, 1, 3).reshape(b, s, h * d)

def to_blocks(t):
    b, h, s = t.shape[:3]
    t = t.reshape((b, h, s // BLOCK_Q, BLOCK_Q) + t.shape[3:])
    return jnp.moveaxis(t, 2, 0)

def from_blocks(t):
    t = jnp.moveaxis(t, 0, 2)
    b, h, nb, bq, d = t.shape
    return t.reshape(b, h, nb * bq, d)

def stick_breaking_attention(q, k, v):
    s_len = q.shape[2]
    nb = s_len // BLOCK_Q
    kpos = jnp.arange(s_len)
    scale = HEAD_DIM ** -0.5

    def block(args):
        qb, i = args
        tpos = i * BLOCK_Q + jnp.arange(BLOCK_Q)
        z = jnp.einsum('bhqd,bhkd->bhqk', qb, k).astype(jnp.float32) * scale
        strict = kpos[None, :] < tpos[:, None]
        log_one_minus = jnp.where(strict, -jax.nn.softplus(z), 0.0)
        later = lax.cumsum(log_one_minus, axis=3, reverse=True) - log_one_minus
        w = jnp.where(strict, jnp.exp(jax.nn.log_sigmoid(z) + later), 0.0)
        return jnp.einsum('bhqk,bhkd->bhqd', w.astype(v.dtype), v)

    out = lax.map(block, (to_blocks(q), jnp.arange(nb)))
    return from_blocks(out)

def forgetting_attention(q, k, v, f_cum):
    s_len = q.shape[2]
    nb = s_len // BLOCK_Q
    kpos = jnp.arange(s_len)
    scale = HEAD_DIM ** -0.5

    def block(args):
        qb, fb, i = args
        tpos = i * BLOCK_Q + jnp.arange(BLOCK_Q)
        logits = (jnp.einsum('bhqd,bhkd->bhqk', qb, k).astype(jnp.float32) * scale
                  + fb[..., :, None] - f_cum[:, :, None, :])
        causal = kpos[None, :] <= tpos[:, None]
        logits = jnp.where(causal, logits, -jnp.inf)
        probs = jax.nn.softmax(logits, axis=-1)
        return jnp.einsum('bhqk,bhkd->bhqd', probs.astype(v.dtype), v)

    out = lax.map(block, (to_blocks(q), to_blocks(f_cum), jnp.arange(nb)))
    return from_blocks(out)

def swiglu(h, w_gu, w_d):
    g, u = jnp.split(h @ w_gu, 2, axis=-1)
    return (jax.nn.silu(g) * u) @ w_d

def first_inputs(seed: int = 0) -> dict:
    key = jax.random.key(seed)
    ks = jax.random.split(key, 20)
    f32 = jnp.float32

    def w(k, shape, fan_in, extra=1.0):
        return jax.random.normal(k, shape, f32) * (fan_in ** -0.5) * extra

    def gain(k, shape):
        return 1.0 + 0.05 * jax.random.normal(k, shape, f32)

    res_scale = (2.0 * DEPTH) ** -0.5
    return {
        'x': jax.random.normal(ks[0], (BATCH, SEQ, D_MODEL), f32),
        'p': jax.random.normal(ks[1], (DEPTH, BATCH, SEQ, PLE_DIM), f32),
        'attn_norm_g': gain(ks[2], (DEPTH, D_MODEL)),
        'sb_w_qkv': w(ks[3], (N_A, D_MODEL, 3 * HD), D_MODEL),
        'sb_w_o': w(ks[4], (N_A, HD, D_MODEL), HD, res_scale),
        'shared_norm_g': gain(ks[5], (D_MODEL,)),
        'shared_w_kvf': w(ks[6], (D_MODEL, 2 * HD + N_HEADS), D_MODEL),
        'shared_b_f': 0.1 * jax.random.normal(ks[7], (N_HEADS,), f32),
        'shared_k_norm_g': gain(ks[8], (HEAD_DIM,)),
        'fox_w_q': w(ks[9], (N_B, D_MODEL, HD), D_MODEL),
        'fox_q_norm_g': gain(ks[10], (N_B, HEAD_DIM)),
        'fox_w_o': w(ks[11], (N_B, HD, D_MODEL), HD, res_scale),
        'ffn_norm_g': gain(ks[12], (DEPTH, D_MODEL)),
        'ffn_w_gu': w(ks[13], (DEPTH, D_MODEL, 2 * D_FF), D_MODEL),
        'ffn_w_d': w(ks[14], (DEPTH, D_FF, D_MODEL), D_FF, res_scale),
        'ple_norm_g': gain(ks[15], (DEPTH, D_MODEL)),
        'ple_w_gate': w(ks[16], (DEPTH, D_MODEL, D_MODEL), D_MODEL),
        'ple_w_proj': w(ks[17], (DEPTH, PLE_DIM, D_MODEL), PLE_DIM, res_scale),
    }

def first_block(x, p, attn_norm_g, sb_w_qkv, sb_w_o, shared_norm_g, shared_w_kvf, shared_b_f,
              shared_k_norm_g, fox_w_q, fox_q_norm_g, fox_w_o, ffn_norm_g, ffn_w_gu, ffn_w_d,
              ple_norm_g, ple_w_gate, ple_w_proj):
    h = x
    k_sh = v_sh = f_cum = None
    for i in range(DEPTH):
        hn = rms_norm(h, attn_norm_g[i])
        if i < N_A:
            q, k, v = jnp.split(hn @ sb_w_qkv[i], 3, axis=-1)
            mix = stick_breaking_attention(split_heads(q), split_heads(k), split_heads(v))
            h = h + merge_heads(mix) @ sb_w_o[i]
        else:
            if i == N_A:
                hs = rms_norm(h, shared_norm_g)
                kvf = hs @ shared_w_kvf
                k_sh = rms_norm(split_heads(kvf[..., :HD]), shared_k_norm_g)
                v_sh = split_heads(kvf[..., HD:2 * HD])
                f_logit = kvf[..., 2 * HD:].astype(jnp.float32) + shared_b_f.astype(jnp.float32)
                f_cum = lax.cumsum(jax.nn.log_sigmoid(f_logit), axis=1).transpose(0, 2, 1)
            j = i - N_A
            q = rms_norm(split_heads(hn @ fox_w_q[j]), fox_q_norm_g[j])
            mix = forgetting_attention(q, k_sh, v_sh, f_cum)
            h = h + merge_heads(mix) @ fox_w_o[j]
        h = h + swiglu(rms_norm(h, ffn_norm_g[i]), ffn_w_gu[i], ffn_w_d[i])
        gate = jax.nn.sigmoid(rms_norm(h, ple_norm_g[i]) @ ple_w_gate[i])
        h = h + gate * (p[i] @ ple_w_proj[i])
    return h


DEPTH_2 = 1

N_MEM = 256
HEAD_DIM_2 = 64
A_HEADS = 8
A_WIDTH = A_HEADS * HEAD_DIM_2
IDX_HEADS = 4
IDX_DIM = 64
TOPK_MAX = 256
B_HEADS = 4
B_VDIM = 2 * HEAD_DIM_2
B_WIDTH = B_HEADS * B_VDIM
MIX_WIDTH = A_WIDTH + B_WIDTH
IN_SIZES = (A_WIDTH, HEAD_DIM_2, HEAD_DIM_2, IDX_HEADS * IDX_DIM, IDX_DIM, IDX_HEADS,
            2 * B_HEADS * HEAD_DIM_2, 2 * B_HEADS * HEAD_DIM_2, B_WIDTH)
IN_COLS = sum(IN_SIZES)
X_HEADS = 4
X_HEAD_DIM = D_MODEL // X_HEADS
D_FF_2 = 2816
CONV_W = 3
ROPE_THETA = 10000.0
Q_BLOCK = 128


def rms_normalize(x):
    xf = x.astype(jnp.float32)
    y = xf * lax.rsqrt(jnp.mean(xf * xf, axis=-1, keepdims=True) + EPS)
    return y.astype(x.dtype)

def rmsnorm(x, g):
    xf = x.astype(jnp.float32)
    y = xf * lax.rsqrt(jnp.mean(xf * xf, axis=-1, keepdims=True) + EPS)
    return (y * g.astype(jnp.float32)).astype(x.dtype)

def rope_tables(positions, dim):
    inv_freq = 1.0 / (ROPE_THETA ** (jnp.arange(0, dim, 2, dtype=jnp.float32) / dim))
    ang = positions.astype(jnp.float32)[..., None] * inv_freq
    return jnp.cos(ang), jnp.sin(ang)

def rope(x, cos, sin):
    shape = cos.shape[:2] + (1,) * (x.ndim - 3) + cos.shape[-1:]
    c = cos.reshape(shape).astype(x.dtype)
    s = sin.reshape(shape).astype(x.dtype)
    x1, x2 = jnp.split(x, 2, axis=-1)
    return jnp.concatenate([x1 * c - x2 * s, x2 * c + x1 * s], axis=-1)

def to_blocks_2(t, n_blk):
    return t.reshape((t.shape[0], n_blk, Q_BLOCK) + t.shape[2:]).swapaxes(0, 1)

def from_blocks_2(t):
    t = t.swapaxes(0, 1)
    return t.reshape((t.shape[0], t.shape[1] * t.shape[2]) + t.shape[3:])

def dsa_attention(q, k, v, q_idx, k_idx, w_idx):
    B, S, H, D = q.shape
    n_blk = S // Q_BLOCK
    topk = min(TOPK_MAX, S // 4)
    key_pos = jnp.arange(S)

    def block(args):
        qb, qib, wib, start = args
        qpos = start + jnp.arange(Q_BLOCK)
        causal = key_pos[None, :] <= qpos[:, None]
        logits = jnp.einsum('bqhd,bsd->bqhs', qib, k_idx)
        score = jnp.einsum('bqh,bqhs->bqs', wib, jax.nn.relu(logits)).astype(jnp.float32)
        score = jnp.where(causal[None], score, -jnp.inf)
        _, idx = lax.top_k(score, topk)
        k_sel = jax.vmap(lambda kk, ii: kk[ii])(k, idx)
        v_sel = jax.vmap(lambda vv, ii: vv[ii])(v, idx)
        valid = idx <= qpos[None, :, None]
        s = jnp.einsum('bqhd,bqkd->bqhk', qb, k_sel).astype(jnp.float32) * (D ** -0.5)
        s = jnp.where(valid[:, :, None, :], s, -jnp.inf)
        p = jax.nn.softmax(s, axis=-1).astype(v.dtype)
        return jnp.einsum('bqhk,bqkd->bqhd', p, v_sel)

    starts = jnp.arange(n_blk) * Q_BLOCK
    out = lax.map(block, (to_blocks_2(q, n_blk), to_blocks_2(q_idx, n_blk), to_blocks_2(w_idx, n_blk), starts))
    return from_blocks_2(out)

def diff_attention(q, k, v, lam):
    B, S, H, _, D = q.shape
    n_blk = S // Q_BLOCK
    key_pos = jnp.arange(S)

    def block(args):
        qb, start = args
        qpos = start + jnp.arange(Q_BLOCK)
        causal = key_pos[None, :] <= qpos[:, None]
        s = jnp.einsum('bqhcd,bshcd->bhcqs', qb, k).astype(jnp.float32) * (D ** -0.5)
        s = jnp.where(causal, s, -jnp.inf)
        p = jax.nn.softmax(s, axis=-1)
        a = (p[:, :, 0] - lam * p[:, :, 1]).astype(v.dtype)
        return jnp.einsum('bhqs,bshe->bqhe', a, v)

    starts = jnp.arange(n_blk) * Q_BLOCK
    out = lax.map(block, (to_blocks_2(q, n_blk), starts))
    return from_blocks_2(out)

def token_mixer(hn, cos, sin, w_in, g_qa, g_ka, g_qb, g_kb,
                lam_q1, lam_k1, lam_q2, lam_k2, w_out, lambda_init):
    B, S, _ = hn.shape
    proj = hn @ w_in
    offsets = np.cumsum(IN_SIZES)[:-1].tolist()
    q_a, k_a, v_a, q_i, k_i, w_i, q_b, k_b, v_b = jnp.split(proj, offsets, axis=-1)

    q_a = rope(rmsnorm(q_a.reshape(B, S, A_HEADS, HEAD_DIM_2), g_qa), cos, sin)
    k_a = rope(rmsnorm(k_a, g_ka), cos, sin)
    q_i = rope(q_i.reshape(B, S, IDX_HEADS, IDX_DIM), cos, sin)
    k_i = rope(k_i, cos, sin)
    w_i = w_i * (IDX_HEADS ** -0.5 * IDX_DIM ** -0.5)
    out_a = dsa_attention(q_a, k_a, v_a, q_i, k_i, w_i).reshape(B, S, A_WIDTH)

    q_b = rope(rmsnorm(q_b.reshape(B, S, B_HEADS, 2, HEAD_DIM_2), g_qb), cos, sin)
    k_b = rope(rmsnorm(k_b.reshape(B, S, B_HEADS, 2, HEAD_DIM_2), g_kb), cos, sin)
    v_b = v_b.reshape(B, S, B_HEADS, B_VDIM)
    f32 = jnp.float32
    lam = (jnp.exp(jnp.sum(lam_q1.astype(f32) * lam_k1.astype(f32)))
           - jnp.exp(jnp.sum(lam_q2.astype(f32) * lam_k2.astype(f32))) + lambda_init)
    out_b = diff_attention(q_b, k_b, v_b, lam)
    out_b = (rms_normalize(out_b) * (1.0 - lambda_init)).reshape(B, S, B_WIDTH)

    return jnp.concatenate([out_a, out_b], axis=-1) @ w_out

def cross_attention(hn, memn, w_xq, w_xk, w_xv, w_xo, g_xq, g_xk):
    B, S, _ = hn.shape
    M = memn.shape[1]
    q = rmsnorm((hn @ w_xq).reshape(B, S, X_HEADS, X_HEAD_DIM), g_xq)
    k = rmsnorm((memn @ w_xk).reshape(B, M, X_HEADS, X_HEAD_DIM), g_xk)
    v = (memn @ w_xv).reshape(B, M, X_HEADS, X_HEAD_DIM)
    s = jnp.einsum('bshd,bmhd->bhsm', q, k).astype(jnp.float32) * (X_HEAD_DIM ** -0.5)
    p = jax.nn.softmax(s, axis=-1).astype(v.dtype)
    o = jnp.einsum('bhsm,bmhd->bshd', p, v).reshape(B, S, D_MODEL)
    return o @ w_xo

def conv_glu(hn, w_ffn_in, conv_w, conv_b, w_ffn_out):
    S = hn.shape[1]
    a, gate = jnp.split(hn @ w_ffn_in, 2, axis=-1)
    a_pad = jnp.pad(a, ((0, 0), (CONV_W - 1, 0), (0, 0)))
    conv = conv_b + sum(a_pad[:, j:j + S] * conv_w[j] for j in range(CONV_W))
    return (jax.nn.gelu(conv) * gate) @ w_ffn_out

def second_inputs(seed: int = 0) -> dict:
    key = jax.random.key(seed)
    ks = iter(jax.random.split(key, 48))
    f32 = jnp.float32

    def nrm(shape, fan_in):
        return jax.random.normal(next(ks), shape, f32) * (fan_in ** -0.5)

    def gain(shape):
        return 1.0 + 0.02 * jax.random.normal(next(ks), shape, f32)

    x = jax.random.normal(next(ks), (BATCH, SEQ, D_MODEL), f32)
    mem = jax.random.normal(next(ks), (BATCH, N_MEM, D_MODEL), f32)
    offs = jax.random.randint(next(ks), (BATCH, 1), 0, 1024)
    positions = (offs + jnp.arange(SEQ, dtype=jnp.int32)[None, :]).astype(jnp.int32)
    L = DEPTH_2
    return {
        "x": x,
        "mem": mem,
        "positions": positions,
        "g_mix": gain((L, D_MODEL)),
        "w_in": nrm((L, D_MODEL, IN_COLS), D_MODEL),
        "g_qa": gain((L, HEAD_DIM_2)),
        "g_ka": gain((L, HEAD_DIM_2)),
        "g_qb": gain((L, HEAD_DIM_2)),
        "g_kb": gain((L, HEAD_DIM_2)),
        "lam_q1": 0.1 * jax.random.normal(next(ks), (L, HEAD_DIM_2), f32),
        "lam_k1": 0.1 * jax.random.normal(next(ks), (L, HEAD_DIM_2), f32),
        "lam_q2": 0.1 * jax.random.normal(next(ks), (L, HEAD_DIM_2), f32),
        "lam_k2": 0.1 * jax.random.normal(next(ks), (L, HEAD_DIM_2), f32),
        "w_out": nrm((L, MIX_WIDTH, D_MODEL), MIX_WIDTH),
        "g_xattn": gain((L, D_MODEL)),
        "g_mem": gain((L, D_MODEL)),
        "w_xq": nrm((L, D_MODEL, D_MODEL), D_MODEL),
        "w_xk": nrm((L, D_MODEL, D_MODEL), D_MODEL),
        "w_xv": nrm((L, D_MODEL, D_MODEL), D_MODEL),
        "w_xo": nrm((L, D_MODEL, D_MODEL), D_MODEL),
        "g_xq": gain((L, X_HEAD_DIM)),
        "g_xk": gain((L, X_HEAD_DIM)),
        "g_ffn": gain((L, D_MODEL)),
        "w_ffn_in": nrm((L, D_MODEL, 2 * D_FF_2), D_MODEL),
        "conv_w": nrm((L, CONV_W, D_FF_2), CONV_W),
        "conv_b": 0.02 * jax.random.normal(next(ks), (L, D_FF_2), f32),
        "w_ffn_out": nrm((L, D_FF_2, D_MODEL), D_FF_2),
    }

def second_block(x, mem, positions, g_mix, w_in, g_qa, g_ka, g_qb, g_kb,
              lam_q1, lam_k1, lam_q2, lam_k2, w_out, g_xattn, g_mem,
              w_xq, w_xk, w_xv, w_xo, g_xq, g_xk, g_ffn, w_ffn_in,
              conv_w, conv_b, w_ffn_out):
    cos, sin = rope_tables(positions, HEAD_DIM_2)
    h = x
    for l in range(DEPTH_2):
        lambda_init = 0.8 - 0.6 * math.exp(-0.3 * l)
        h = h + token_mixer(rmsnorm(h, g_mix[l]), cos, sin, w_in[l], g_qa[l], g_ka[l],
                            g_qb[l], g_kb[l], lam_q1[l], lam_k1[l], lam_q2[l], lam_k2[l],
                            w_out[l], lambda_init)
        h = h + cross_attention(rmsnorm(h, g_xattn[l]), rmsnorm(mem, g_mem[l]),
                                w_xq[l], w_xk[l], w_xv[l], w_xo[l], g_xq[l], g_xk[l])
        h = h + conv_glu(rmsnorm(h, g_ffn[l]), w_ffn_in[l], conv_w[l], conv_b[l], w_ffn_out[l])
    return h


def setup_inputs(seed=0):
    out = dict(first_inputs(seed))
    for name, value in second_inputs(seed + 1).items():
        if name != "x":
            out[name + "_2"] = value
    return out


def reference(
    x, p, attn_norm_g, sb_w_qkv, sb_w_o, shared_norm_g, shared_w_kvf, shared_b_f,
    shared_k_norm_g, fox_w_q, fox_q_norm_g, fox_w_o, ffn_norm_g, ffn_w_gu, ffn_w_d, ple_norm_g,
    ple_w_gate, ple_w_proj, mem_2, positions_2, g_mix_2, w_in_2, g_qa_2, g_ka_2, g_qb_2, g_kb_2,
    lam_q1_2, lam_k1_2, lam_q2_2, lam_k2_2, w_out_2, g_xattn_2, g_mem_2, w_xq_2, w_xk_2, w_xv_2,
    w_xo_2, g_xq_2, g_xk_2, g_ffn_2, w_ffn_in_2, conv_w_2, conv_b_2, w_ffn_out_2,
):
    x = first_block(
        x, p, attn_norm_g, sb_w_qkv, sb_w_o, shared_norm_g, shared_w_kvf, shared_b_f,
        shared_k_norm_g, fox_w_q, fox_q_norm_g, fox_w_o, ffn_norm_g, ffn_w_gu, ffn_w_d,
        ple_norm_g, ple_w_gate, ple_w_proj,
    )
    return second_block(
        x, mem_2, positions_2, g_mix_2, w_in_2, g_qa_2, g_ka_2, g_qb_2, g_kb_2, lam_q1_2,
        lam_k1_2, lam_q2_2, lam_k2_2, w_out_2, g_xattn_2, g_mem_2, w_xq_2, w_xk_2, w_xv_2,
        w_xo_2, g_xq_2, g_xk_2, g_ffn_2, w_ffn_in_2, conv_w_2, conv_b_2, w_ffn_out_2,
    )


_drawn_inputs = setup_inputs


def setup_inputs(seed=0):
    import zlib

    import numpy as np

    out = dict(_drawn_inputs(seed))
    spreads = {}
    factors = {'shared_b_f': 4.101,
     'shared_k_norm_g': 5.271,
     'fox_q_norm_g': 4.603,
     'ple_norm_g': 5.512,
     'g_mix_2': 3.166,
     'g_qa_2': 8.0,
     'g_ka_2': 8.0,
     'g_qb_2': 7.504,
     'g_kb_2': 7.589,
     'lam_k1_2': 8.0,
     'g_xattn_2': 8.0,
     'g_mem_2': 8.0,
     'g_xq_2': 8.0,
     'g_xk_2': 8.0,
     'g_ffn_2': 4.751,
     'conv_b_2': 6.436}
    for name, (base, spread) in spreads.items():
        noise = np.random.default_rng([zlib.crc32(name.encode()), seed]).standard_normal(out[name].shape)
        drawn = base * np.exp(spread * noise) if base else spread * noise
        out[name] = __import__('jax').numpy.asarray(drawn.astype(out[name].dtype))
    for name, factor in factors.items():
        out[name] = (out[name] * factor).astype(out[name].dtype)
    return out
```

```python
from contextlib import ExitStack

import numpy as np
import concourse.bass as bass
from concourse import mybir

F32 = mybir.dt.float32
F32R = mybir.dt.float32r
I32 = mybir.dt.int32
ALU = mybir.AluOpType
ACT = mybir.ActivationFunctionType
AX = mybir.AxisListType

P = 128
S = 512
QT = S // P
D = 1024
DT = D // P
HEADS = 16
HD = 64
PAIRS = HEADS // 2
FF = 2816
FT = FF // P
FA, FB = 12, FT - 12
M = 256
MT = M // P
EPS = 1e-6
UNIT = 1024
STAGES = 4
SLOTS = 2
LAMBDA_INIT = 0.8 - 0.6
NEG = -1.0e30

WIDTH = [S - P * j for j in range(QT)]
COL = [0, 512, 1024, 896]
CAUSAL = sum(WIDTH)
GROUPS = [(0, 512, (0,)), (512, 512, (1, 3)), (1024, 256, (2,))]
NG = len(GROUPS)

(G_ATTN0, G_FFN0, G_PLE0, G_ATTN1, G_SHARED, G_FFN1, G_PLE1, G_MIX, G_XATTN, G_FFN2, G_MEM) = range(11)
(H_FOXK, H_FOXQ, H_QA, H_KA, H_QB, H_KB) = range(6)

LAYER_UNITS = 3 * PAIRS + DT + 2 * FA + FA + 2 * FB + FB + 2 + DT
U_QKV0 = 0
U_F1 = LAYER_UNITS
U_KVQ1 = U_F1 + 1
U_IDX = U_F1 + 1 + LAYER_UNITS
U_DIFF = U_IDX + 5
U_QA = U_DIFF + 12
U_OUT2 = U_QA + 4
U_XK = U_OUT2 + DT
U_XV = U_XK + DT
U_XQ = U_XV + DT
U_XO = U_XQ + DT
U_FFN2 = U_XO + DT
UNITS = U_FFN2 + 3 * FT


class Signal:

    def __init__(self, semaphore, base=0):
        self.sem, self.base = semaphore, base

    def at(self, n):
        return self.sem, self.base + n


def at_least(engine, signal, n):
    if not isinstance(n, int) or n > 0:
        engine.wait_ge(*signal.at(n))


def pairs_loop(engine, body):
    body(0, 0, True)
    with engine.Fori(0, (PAIRS - 2) // 2) as i:
        body(2 * i + 1, 1, True)
        body(2 * i + 2, 0, True)
    body(PAIRS - 1, 1, False)


def build_program(nc, W, XT, PT, MEMT, POS, INVF, GAINS, HGAINS, XGAINS, BF, LAM, CONV, OUT):
    with ExitStack() as ctx:
        low = (nc.sbuf_base + 63) // 64 * 64
        place, place_used = [low], {}

        def sb(name, shape, dt):
            size = 4 * int(np.prod(shape[1:]))
            place_used[name] = place[0]
            t = nc.alloc_sbuf_tensor_at(name, shape, dt, offset=place[0])
            place[0] += (size + 63) // 64 * 64
            return t

        def sem(name):
            return Signal(ctx.enter_context(nc.semaphore(name)))

        used = {}

        def again(name, count):
            semaphore, base = used[name] if name in used else (ctx.enter_context(nc.semaphore(name)), 0)
            used[name] = semaphore, base + count
            return Signal(semaphore, base)

        hT = sb("hT", [P, DT, S], F32)
        IN_hi, IN_lo = (sb(f"IN_{x}", [P, DT, S], F32R) for x in ("hi", "lo"))
        MID_hi, MID_lo = (sb(f"MID_{x}", [P, DT, S], F32R) for x in ("hi", "lo"))
        stage = sb("stage", [P, STAGES, UNIT], F32)
        w_hi, w_lo = (sb(f"w_{x}", [P, SLOTS, UNIT], F32R) for x in ("hi", "lo"))
        gains = sb("gains", [P, 11 * DT], F32)
        hgains = sb("hgains", [P, 6], F32)
        xgains = sb("xgains", [P, 4], F32)
        forget_bias = sb("forget_bias", [HEADS, 1], F32)
        conv_s = sb("conv_s", [P, 4 * FT], F32)
        rstd = sb("rstd", [P, S], F32)
        sumsq = sb("sumsq", [P, S], F32)
        square = sb("square", [P, S], F32)
        ident = sb("ident", [P, P], F32)
        ident_r = sb("ident_r", [P, P], F32R)
        ones = sb("ones", [P, P], F32)
        ones_r = sb("ones_r", [P, P], F32R)
        head_ones = sb("head_ones", [P, P], F32)
        neg_upto = sb("neg_upto", [P, P], F32)
        neg_ones = sb("neg_ones", [P, P], F32)
        before = sb("before", [P, P], F32)
        mask_kq_strict = sb("mask_kq_strict", [P, P], F32R)
        mask_kq = sb("mask_kq", [P, P], F32R)
        mask_qk = sb("mask_qk", [P, P], F32R)
        one_c = sb("one_c", [P, 1], F32)
        eps_c = sb("eps_c", [P, 1], F32)
        perm = sb("perm", [P, P], F32)
        tmp_a = sb("tmp_a", [P, 2, S], F32)
        mask_f = tmp_a[:, 0, 0:P]
        tmp_b = sb("tmp_b", [P, 2, S], F32)
        tmp_c = sb("tmp_c", [P, 2, S], F32)
        ple_in = sb("ple_in", [P, 2, S], F32)
        ple_hi, ple_lo = (sb(f"ple_{x}", [P, 2, S], F32R) for x in ("hi", "lo"))
        area0 = place[0]
        areas = [area0]

        def area(name, shape, dt):
            size = 4 * int(np.prod(shape[1:]))
            t = nc.alloc_sbuf_tensor_at(name, shape, dt, offset=areas[0])
            areas[0] += (size + 63) // 64 * 64
            return t

        bank = ctx.enter_context(nc.psum_tensor("bank", [P, 8, S], F32))

        w_loaded = [sem(f"w_loaded{k}") for k in range(STAGES)]
        w_hi_done = sem("w_hi_done")
        w_split = sem("w_split")
        unit_done = sem("unit_done")

        pool_turns, act_turns = sem("pool_turns"), sem("act_turns")

        block = ctx.enter_context(nc.Block())

        small_loaded, x_loaded, p_loaded = sem("small_loaded"), sem("x_loaded"), sem("p_loaded")
        consts_made, masks_filled, consts_cast = sem("consts_made"), sem("masks_filled"), sem("consts_cast")

        @block.sync
        def _(sp):
            sp.dma_start(hT[:], XT).then_inc(x_loaded.sem, 16)
            sp.dma_start(gains[:], GAINS).then_inc(small_loaded.sem, 16)
            sp.dma_start(hgains[:], HGAINS).then_inc(small_loaded.sem, 16)
            sp.dma_start(xgains[:], XGAINS).then_inc(small_loaded.sem, 16)
            sp.dma_start(forget_bias[:], BF).then_inc(small_loaded.sem, 16)
            sp.dma_start(conv_s[:], CONV).then_inc(small_loaded.sem, 16)
            sp.dma_start(ple_in[:], PT[0]).then_inc(p_loaded.sem, 16)
            for u in range(STAGES):
                sp.dma_start(stage[:, u], W[u]).then_inc(w_loaded[u].sem, 16)
            with sp.Fori(1, UNITS // STAGES) as i:
                for k in range(STAGES):
                    sp.wait_ge(*w_split.at(STAGES * (i - 1) + k + 1))
                    sp.dma_start(stage[:, k], W[bass.ds(STAGES * i + k, 1)].rearrange("a p n -> (a p) n")
                                 ).then_inc(w_loaded[k].sem, 16)

        @block.gpsimd
        def _(pool):
            nc.gpsimd.memset(ones[:], 1.0).then_inc(masks_filled.sem, 1)
            nc.gpsimd.memset(neg_ones[:], -1.0).then_inc(masks_filled.sem, 1)
            nc.gpsimd.memset(mask_f, 0.0).then_inc(masks_filled.sem, 1)
            nc.gpsimd.memset(head_ones[:], 0.0).then_inc(masks_filled.sem, 1)
            nc.gpsimd.memset(one_c[:], 1.0).then_inc(masks_filled.sem, 1)
            nc.gpsimd.memset(eps_c[:], EPS).then_inc(masks_filled.sem, 1)
            pool.wait_ge(*masks_filled.at(6))
            nc.gpsimd.affine_select(ident[:], ones[:], [[-1, P]], ALU.is_equal, 0.0, base=0,
                                    channel_multiplier=1).then_inc(consts_made.sem, 1)
            nc.gpsimd.affine_select(neg_upto[:], neg_ones[:], [[-1, P]], ALU.is_ge, 0.0, base=0,
                                    channel_multiplier=1).then_inc(consts_made.sem, 1)
            nc.gpsimd.affine_select(before[:], ones[:], [[1, P]], ALU.is_gt, 0.0, base=0,
                                    channel_multiplier=-1).then_inc(consts_made.sem, 1)
            pool.wait_ge(*consts_made.at(3))
            nc.gpsimd.memset(head_ones[0:HD, 0:HD], 1.0).then_inc(consts_made.sem, 1)
            nc.gpsimd.memset(head_ones[HD:P, HD:P], 1.0).then_inc(consts_made.sem, 1)
            pool.wait_ge(*consts_made.at(5))
            nc.gpsimd.affine_select(square[:, 0:P], mask_f, [[1, P]], ALU.is_ge, NEG, base=0,
                                    channel_multiplier=-1).then_inc(consts_made.sem, 1)
            nc.gpsimd.affine_select(square[:, P:2 * P], mask_f, [[1, P]], ALU.is_gt, NEG, base=0,
                                    channel_multiplier=-1).then_inc(consts_made.sem, 1)
            nc.gpsimd.affine_select(square[:, 2 * P:3 * P], mask_f, [[-1, P]], ALU.is_ge, NEG, base=0,
                                    channel_multiplier=1).then_inc(consts_made.sem, 1)
            for m, (source, shift) in enumerate(((neg_ones, 32), (ones, 0), (neg_ones, 96), (ones, 64))):
                nc.gpsimd.affine_select(perm[:, 32 * m:32 * m + 32], source[:, 0:32], [[-1, 32]], ALU.is_equal,
                                        0.0, base=-shift, channel_multiplier=1).then_inc(consts_made.sem, 1)
            def split(u, k):
                slot = k % SLOTS
                at_least(pool, unit_done, u - SLOTS + 1)
                pool.wait_ge(*w_loaded[k].at(u // STAGES * 16 + 16 if isinstance(u, int) else 4 * u - 4 * k + 16))
                pool.sem_inc(pool_turns.sem, 1)
                nc.gpsimd.tensor_scalar(w_hi[:, slot], stage[:, k], 1.0, 1.0, ALU.mult, ALU.mult
                                        ).then_inc(w_hi_done.sem, 1)
                pool.wait_ge(*w_hi_done.at(u + 1))
                nc.gpsimd.tensor_tensor(w_lo[:, slot], stage[:, k], w_hi[:, slot].bitcast(F32),
                                        ALU.subtract).then_inc(w_split.sem, 1)

            for k in range(STAGES):
                split(k, k)
            with pool.Fori(1, UNITS // STAGES) as i:
                for k in range(STAGES):
                    split(STAGES * i + k, k)

        p_hi_done, p_lo_done = sem("p_hi_done"), sem("p_lo_done")

        @block.scalar
        def _(act):
            act.wait_ge(*consts_made.at(8))
            nc.scalar.copy(ident_r[:], ident[:]).then_inc(consts_cast.sem, 1)
            nc.scalar.copy(ones_r[:], ones[:]).then_inc(consts_cast.sem, 1)
            nc.scalar.copy(mask_kq[:], square[:, 0:P]).then_inc(consts_cast.sem, 1)
            nc.scalar.copy(mask_kq_strict[:], square[:, P:2 * P]).then_inc(consts_cast.sem, 1)
            nc.scalar.copy(mask_qk[:], square[:, 2 * P:3 * P]).then_inc(consts_cast.sem, 1)

        def tile(t, c):
            return t[:, c] if isinstance(c, int) else t[:, bass.ds(c, 1)].rearrange("p a s -> p (a s)")

        def column(t, c):
            return t[:, c:c + 1] if isinstance(c, int) else t[:, bass.ds(c, 1)]

        class Operand:

            def __init__(self, name, targets, previous=None):
                self.targets = targets
                self.previous = previous
                n = DT * len(targets)
                self.h_done = again("h_done", DT)
                self.hi_done = again("operand_hi", n)
                self.lo_done = again("operand_lo", n)
                self.sq_done = again("h_squared", DT)
                self.ss_done = again("squares_added", DT + 1)
                self.ss_ready = again("squares_summed", 1)
                self.ln_done = again("rstd_ln", 1)
                self.rstd_done = again("rstd_ready", 1)

            def on_act(self, act, c):
                act.wait_ge(*self.h_done.at(c + 1))
                act.sem_inc(act_turns.sem, 1)
                for g, hi, lo in self.targets:
                    nc.scalar.activation(tile(hi, c), tile(hT, c), ACT.Copy, scale=column(gains, g * DT + c)
                                         ).then_inc(self.hi_done.sem, 1)
                act.wait_ge(*self.ss_done.at(c + 1))
                act.sem_inc(act_turns.sem, 1)
                nc.scalar.activation(square[:], tile(hT, c), ACT.Square).then_inc(self.sq_done.sem, 1)

            def on_dve_first(self, dve):
                if self.previous is not None:
                    dve.wait_ge(*self.previous.ss_ready.at(1))
                nc.vector.memset(sumsq[:], 0.0).then_inc(self.ss_done.sem, 1)

            def on_dve(self, dve, c):
                n = len(self.targets)
                for k, (g, hi, lo) in enumerate(self.targets):
                    dve.wait_ge(*self.hi_done.at(n * c + k + 1))
                    nc.vector.scalar_tensor_tensor(tile(lo, c), tile(hT, c), column(gains, g * DT + c),
                                                   tile(hi, c).bitcast(F32), ALU.mult, ALU.subtract
                                                   ).then_inc(self.lo_done.sem, 1)
                dve.wait_ge(*self.sq_done.at(c + 1))
                dve.wait_ge(*self.ss_done.at(c + 1))
                nc.vector.tensor_tensor(sumsq[:], sumsq[:], square[:], ALU.add).then_inc(self.ss_done.sem, 1)

            def stats(self, b, before=()):
                @block.tensor
                def _(pe):
                    pe.wait_ge(*self.lo_done.at(DT * len(self.targets)))
                    pe.wait_ge(*self.ss_done.at(DT + 1))
                    for s, n in before:
                        pe.wait_ge(*s.at(n))
                    nc.tensor.matmul(bank[:, b], ones[:], sumsq[:], start=True, stop=True
                                     ).then_inc(self.ss_ready.sem, 1)

                @block.scalar
                def _(act):
                    act.wait_ge(*self.ss_ready.at(1))
                    nc.scalar.activation(rstd[:], bank[:, b], ACT.Ln, bias=eps_c[:], scale=1.0 / D
                                         ).then_inc(self.ln_done.sem, 1)
                    act.wait_ge(*self.ln_done.at(1))
                    nc.scalar.activation(rstd[:], rstd[:], ACT.Exp, scale=-0.5).then_inc(self.rstd_done.sem, 1)

        def unit(pe, u, slot, out, hi, lo, width=S):
            pe.wait_ge(*w_split.at(u + 1))
            n = 0
            for t in range(DT):
                a, b = w_hi[:, slot, t * P:(t + 1) * P], w_lo[:, slot, t * P:(t + 1) * P]
                for w, x in ((a, hi), (a, lo), (b, hi)):
                    last = nc.tensor.matmul(out, w, x[:, t, 0:width], start=(n == 0), stop=(n == 3 * DT - 1))
                    n += 1
            last.then_inc(unit_done.sem, 1)

        x_op = Operand("x", [(G_ATTN0, IN_hi, IN_lo)])

        @block.scalar
        def _(act):
            act.wait_ge(*small_loaded.at(80))
            for c in range(DT):
                x_op.on_act(act, c)
            act.wait_ge(*p_loaded.at(16))
            nc.scalar.copy(ple_hi[:], ple_in[:]).then_inc(p_hi_done.sem, 1)

        @block.vector
        def _(dve):
            dve.wait_ge(*x_loaded.at(16))
            dve.wait_ge(*consts_cast.at(5))
            x_op.on_dve_first(dve)
            dve.wait_ge(*small_loaded.at(80))
            dve.engine_nop().then_inc(x_op.h_done.sem, DT)
            for c in range(DT):
                x_op.on_dve(dve, c)
            dve.wait_ge(*p_hi_done.at(1))
            nc.vector.tensor_tensor(ple_lo[:], ple_in[:], ple_hi[:].bitcast(F32), ALU.subtract
                                    ).then_inc(p_lo_done.sem, 1)

        x_op.stats(6, [(consts_made, 12)])

        areas[0] = area0
        QZ = area("sb_q", [P, 2, 2, S], F32)
        KT_ = area("sb_k", [P, 2, S], F32)
        VN = area("sb_v", [P, 2, QT, P], F32)
        VT = area("sb_vt", [P, S], F32)
        AB = area("sb_ab", [P, 2, CAUSAL], F32)
        sb_zeroed = sem("sb_zeroed")
        sb_taken = sem("sb_taken")
        sb_q_done = sem("sb_q_done")
        sb_vt_ready = sem("sb_vt_ready")
        sb_v_ready = sem("sb_v_ready")
        sb_z = sem("sb_z")
        sb_abs = sem("sb_abs")
        sb_exp = sem("sb_exp")
        sb_ln = sem("sb_ln")
        sb_raw = sem("sb_raw")
        sb_sp = sem("sb_sp")
        sb_sum = sem("sb_sum")
        sb_w = sem("sb_w")
        sb_o = sem("sb_o")
        sb_o_hi = sem("sb_o_hi")
        sb_o_lo = sem("sb_o_lo")
        PER = 2 * NG

        def tile_in_bank(first, j):
            return bank[:, first + (0, 1, 2, 1)[j], (0, 0, 0, WIDTH[1])[j]:][:, 0:WIDTH[j]]

        def z_bank(h, j):
            return tile_in_bank(3 * h, j)

        def rows(h):
            return slice(HD * h, HD * h + HD)

        @block.tensor
        def _(pe):
            def project(p, b, n, u):
                at_least(pe, sb_taken, 3 * p + (0, -1, 1)[n])
                if n == 1:
                    at_least(pe, sb_v_ready, p)
                unit(pe, u, (U_QKV0 + b + n) % SLOTS, bank[:, 6 + n % 2], IN_hi, IN_lo)

            def turn_v(p, b):
                pe.wait_ge(*sb_taken.at(3 * p + 3))
                for t in range(QT):
                    last = nc.tensor.transpose(bank[:, 7, t * P:(t + 1) * P], VT[:, t * P:(t + 1) * P], ident[:])
                last.then_inc(sb_vt_ready.sem, 1)

            def scores(p, b, h):
                at_least(pe, sb_o_lo, 2 * (p - 1) + h + 1)
                pe.wait_ge(*sb_taken.at(3 * p + 2))
                for _, _, tiles in GROUPS:
                    for j in tiles:
                        last = nc.tensor.matmul(z_bank(h, j), KT_[:, b, j * P:(j + 1) * P], QZ[:, b, h, j * P:S],
                                                start=(j != 3), stop=False, skip_group_check=True)
                    last.then_inc(sb_z.sem, 1)

            def sums(p, b, h):
                pe.wait_ge(*sb_sp.at(PER * p + NG * h + NG))
                for _, _, tiles in GROUPS:
                    for j in tiles:
                        for k in range(j, QT):
                            nc.tensor.matmul(z_bank(h, j)[:, (k - j) * P:], (neg_upto if k == j else neg_ones)[:],
                                             AB[:, h, COL[k]:COL[k] + WIDTH[k]], start=False, stop=False,
                                             skip_group_check=True)
                        last = nc.tensor.matmul(z_bank(h, j)[:, 0:P], ident_r[:], mask_kq_strict[:], start=False,
                                                stop=True, skip_group_check=True)
                    last.then_inc(sb_sum.sem, 1)

            def output(p, b, h):
                pe.wait_ge(*sb_v_ready.at(p + 1))
                pe.wait_ge(*sb_w.at(PER * p + NG * h + NG))
                for j in range(QT):
                    last = nc.tensor.matmul(bank[:, 3 * h, j * P:S], VN[:, b, j], AB[:, h, COL[j]:COL[j] + WIDTH[j]],
                                            start=(j == 0), stop=(j == QT - 1))
                last.then_inc(sb_o.sem, 1)

            pe.wait_ge(*consts_cast.at(5))
            pe.wait_ge(*x_op.rstd_done.at(1))
            for n in range(3):
                project(0, 0, n, U_QKV0 + n)
            turn_v(0, 0)

            def pair(p, b, more):
                u = U_QKV0 + 3 * p + 3
                c = (b + 1) % 2
                scores(p, b, 0)
                scores(p, b, 1)
                if more:
                    project(p + 1, c, 0, u)
                sums(p, b, 0)
                if more:
                    project(p + 1, c, 1, u + 1)
                sums(p, b, 1)
                if more:
                    project(p + 1, c, 2, u + 2)
                output(p, b, 0)
                if more:
                    turn_v(p + 1, c)
                output(p, b, 1)

            pairs_loop(pe, pair)

        @block.scalar
        def _(act):
            def copy_v(p, b):
                pe_done = sb_vt_ready
                act.wait_ge(*pe_done.at(p + 1))
                at_least(act, sb_o, 2 * (p - 1))
                nc.scalar.copy(VN[:, b], bank[:, 7].rearrange("p (t c) -> p t c", t=QT)).then_inc(sb_v_ready.sem, 1)

            def soften(p, h):
                at_least(act, sb_o, 2 * (p - 1) + h + 1)
                for n, (c, width, _) in enumerate(GROUPS):
                    k = PER * p + NG * h + n
                    x = AB[:, h, c:c + width]
                    act.wait_ge(*sb_z.at(k + 1))
                    nc.scalar.activation(x, bank[:, 3 * h + n, 0:width], ACT.Abs).then_inc(sb_abs.sem, 1)
                    act.wait_ge(*sb_abs.at(k + 1))
                    nc.scalar.activation(x, x, ACT.Exp, scale=-1.0).then_inc(sb_exp.sem, 1)
                    act.wait_ge(*sb_exp.at(k + 1))
                    nc.scalar.activation(x, x, ACT.Ln, bias=one_c[:]).then_inc(sb_ln.sem, 1)

            def weigh(p, h):
                act.wait_ge(*sb_sum.at(PER * p + NG * h + NG))
                for n, (c, width, _) in enumerate(GROUPS):
                    nc.scalar.activation(AB[:, h, c:c + width], bank[:, 3 * h + n, 0:width], ACT.Exp
                                         ).then_inc(sb_w.sem, 1)

            act.preload_act_table_set("natural_log_exp_and_others")
            copy_v(0, 0)

            def pair(p, b, more):
                soften(p, 0)
                soften(p, 1)
                weigh(p, 0)
                weigh(p, 1)
                if more:
                    copy_v(p + 1, (b + 1) % 2)
                for h in range(2):
                    act.wait_ge(*sb_o.at(2 * p + h + 1))
                    act.sem_inc(act_turns.sem, 1)
                    nc.scalar.copy(tile(MID_hi, p)[rows(h)], bank[rows(h), 3 * h]).then_inc(sb_o_hi.sem, 1)

            pairs_loop(act, pair)

        @block.vector
        def _(dve):
            def take(p, b, n):
                dve.wait_ge(*unit_done.at(U_QKV0 + 3 * p + n + 1))
                if n == 0:
                    at_least(dve, sb_z, PER * (p - 1))
                    for h in range(2):
                        o = nc.vector.scalar_tensor_tensor(QZ[rows(h), b, h], bank[rows(h), 6], HD ** -0.5,
                                                           rstd[rows(h)], ALU.mult, ALU.mult)
                        if h == 0:
                            o.then_inc(sb_q_done.sem, 1)
                    o.then_inc(sb_taken.sem, 1)
                elif n == 1:
                    nc.vector.tensor_tensor(KT_[:, b], bank[:, 7], rstd[:], ALU.mult).then_inc(sb_taken.sem, 1)
                else:
                    at_least(dve, sb_vt_ready, p)
                    nc.vector.tensor_tensor(VT[:], bank[:, 6], rstd[:], ALU.mult).then_inc(sb_taken.sem, 1)

            def softplus(p, h):
                for n, (c, width, tiles) in enumerate(GROUPS):
                    k = PER * p + NG * h + n
                    x = AB[:, h, c:c + width]
                    dve.wait_ge(*sb_ln.at(k + 1))
                    nc.vector.scalar_tensor_tensor(x, bank[:, 3 * h + n, 0:width], 0.0, x, ALU.max, ALU.add
                                                   ).then_inc(sb_raw.sem, 1)
                    dve.wait_ge(*sb_raw.at(k + 1))
                    for j in tiles:
                        x = AB[:, h, COL[j]:COL[j] + P]
                        last = nc.vector.tensor_tensor(x, x, before[:], ALU.mult)
                    last.then_inc(sb_sp.sem, 1)

            dve.wait_ge(*x_op.rstd_done.at(1))
            nc.vector.memset(QZ[:], 0.0).then_inc(sb_zeroed.sem, 1)
            dve.wait_ge(*sb_zeroed.at(1))
            for n in range(3):
                take(0, 0, n)

            def pair(p, b, more):
                c = (b + 1) % 2
                softplus(p, 0)
                softplus(p, 1)
                if more:
                    for n in range(3):
                        take(p + 1, c, n)
                for h in range(2):
                    dve.wait_ge(*sb_o_hi.at(2 * p + h + 1))
                    nc.vector.tensor_tensor(tile(MID_lo, p)[rows(h)], bank[rows(h), 3 * h],
                                            tile(MID_hi, p)[rows(h)].bitcast(F32), ALU.subtract
                                            ).then_inc(sb_o_lo.sem, 1)

            pairs_loop(dve, pair)

        def project_back(name, u0, op, ready):
            @block.tensor
            def _(pe):
                for s, n in ready:
                    pe.wait_ge(*s.at(n))

                def one(c, b):
                    at_least(pe, op.h_done, c - 1)
                    unit(pe, u0 + c, (u0 + b) % 2, bank[:, 6 + b], MID_hi, MID_lo)

                one(0, 0)
                one(1, 1)
                with pe.Fori(1, DT // 2) as i:
                    one(2 * i, 0)
                    one(2 * i + 1, 1)

            @block.scalar
            def _(act):
                with act.Fori(0, DT) as c:
                    op.on_act(act, c)

            @block.vector
            def _(dve):
                op.on_dve_first(dve)

                def one(c, b):
                    dve.wait_ge(*unit_done.at(u0 + c + 1))
                    nc.vector.tensor_tensor(tile(hT, c), tile(hT, c), bank[:, 6 + b], ALU.add
                                            ).then_inc(op.h_done.sem, 1)
                    op.on_dve(dve, c)

                with dve.Fori(0, DT // 2) as i:
                    one(2 * i, 0)
                    one(2 * i + 1, 1)

        def feed_forward(name, u0, op_in, op, conv=False):
            areas[0] = area0
            A_hi = area(name + "_hi", [P, FA, S], F32R)
            A_lo = area(name + "_lo", [P, FA, S], F32R)
            gate_done = again("ff_gate", FT)
            act_done = again("ff_act", FT)
            up_done = again("ff_up", FT)
            prod_done = again("ff_product", FT)
            hi_done = again("ff_hi", FT)
            lo_done = again("ff_lo", FT)
            sums_done = again("ff_sums", 2 * DT)
            added = again("ff_added", DT)
            if conv:
                pad_done, taps = sem("conv_pad"), sem("conv_taps")
                padded = area(name + "_padded", [P, 2, S + 2], F32)
            DOWN_BANKS = (2, 3, 4, 5, 6, 7, 0, 1)

            def gate_up(half, f0, nf, u1):
                @block.tensor
                def _(pe):
                    def one(f, b, first):
                        u = u1 + 2 * (f - f0)
                        if not first:
                            at_least(pe, gate_done, f - 1)
                            at_least(pe, up_done, f - 1)
                        unit(pe, u, u1 % 2, bank[:, (6, 0)[b]], IN_hi, IN_lo)
                        unit(pe, u + 1, (u1 + 1) % 2, bank[:, (7, 1)[b]], IN_hi, IN_lo)

                    if half == 0:
                        pe.wait_ge(*op_in.rstd_done.at(1))
                    else:
                        pe.wait_ge(*added.at(DT))
                    one(f0, 0, True)
                    one(f0 + 1, 1, True)
                    with pe.Fori(1, nf // 2) as i:
                        one(2 * i + f0, 0, False)
                        one(2 * i + f0 + 1, 1, False)

                @block.scalar
                def _(act):
                    def one(f, b):
                        act.wait_ge(*gate_done.at(f + 1))
                        at_least(act, up_done, f - 1)
                        if conv:
                            act.wait_ge(*taps.at(3 * f + 3))
                        nc.scalar.activation(tmp_b[:, b], tmp_a[:, b], ACT.Gelu_apprx_tanh if conv else ACT.Silu
                                             ).then_inc(act_done.sem, 1)
                        act.wait_ge(*prod_done.at(f + 1))
                        act.sem_inc(act_turns.sem, 1)
                        nc.scalar.copy(tile(A_hi, f - f0), tmp_c[:, b]).then_inc(hi_done.sem, 1)

                    if half == 1:
                        act.wait_ge(*sums_done.at(DT))
                    one(f0, 0)
                    one(f0 + 1, 1)
                    with act.Fori(1, nf // 2) as i:
                        one(2 * i + f0, 0)
                        one(2 * i + f0 + 1, 1)

                @block.vector
                def _(dve):
                    def one(f, b):
                        u = u1 + 2 * (f - f0)
                        dve.wait_ge(*unit_done.at(u + 1))
                        at_least(dve, act_done, f - 1)
                        if conv:
                            nc.vector.tensor_tensor(padded[:, b, 2:S + 2], bank[:, (6, 0)[b]], rstd[:], ALU.mult
                                                    ).then_inc(gate_done.sem, 1)
                            dve.wait_ge(*gate_done.at(f + 1))
                            nc.vector.tensor_scalar(tmp_a[:, b], padded[:, b, 0:S], column(conv_s, 4 * f),
                                                    column(conv_s, 4 * f + 3), ALU.mult, ALU.add).then_inc(taps.sem, 1)
                            for k in (1, 2):
                                dve.wait_ge(*taps.at(3 * f + k))
                                nc.vector.scalar_tensor_tensor(tmp_a[:, b], padded[:, b, k:S + k],
                                                               column(conv_s, 4 * f + k), tmp_a[:, b],
                                                               ALU.mult, ALU.add).then_inc(taps.sem, 1)
                        else:
                            nc.vector.tensor_tensor(tmp_a[:, b], bank[:, (6, 0)[b]], rstd[:], ALU.mult
                                                    ).then_inc(gate_done.sem, 1)
                        dve.wait_ge(*unit_done.at(u + 2))
                        dve.wait_ge(*act_done.at(f + 1))
                        at_least(dve, hi_done, f - 1)
                        at_least(dve, lo_done, f - 1)
                        nc.vector.tensor_tensor(tmp_c[:, b], bank[:, (7, 1)[b]], tmp_b[:, b], ALU.mult
                                                ).then_inc(up_done.sem, 1)
                        dve.wait_ge(*up_done.at(f + 1))
                        nc.vector.tensor_tensor(tmp_c[:, b], tmp_c[:, b], rstd[:], ALU.mult).then_inc(prod_done.sem, 1)
                        dve.wait_ge(*hi_done.at(f + 1))
                        nc.vector.tensor_tensor(tile(A_lo, f - f0), tmp_c[:, b], tile(A_hi, f - f0).bitcast(F32),
                                                ALU.subtract).then_inc(lo_done.sem, 1)

                    if conv and half == 0:
                        nc.vector.memset(padded[:, :, 0:2], 0.0).then_inc(pad_done.sem, 1)
                        dve.wait_ge(*pad_done.at(1))
                    one(f0, 0)
                    one(f0 + 1, 1)
                    with dve.Fori(1, nf // 2) as i:
                        one(2 * i + f0, 0)
                        one(2 * i + f0 + 1, 1)

            def down(half, f0, nf, u1):
                @block.tensor
                def _(pe):
                    pe.wait_ge(*up_done.at(f0 + nf))
                    if half == 1:
                        pe.wait_ge(*added.at(DT))
                    for g in range(2):
                        for kp in range(nf // 2):
                            u = u1 + g * (nf // 2) + kp
                            pe.wait_ge(*w_split.at(u + 1))
                            pe.wait_ge(*lo_done.at(f0 + 2 * kp + 2))
                            for n in range(4):
                                b = DOWN_BANKS[4 * g + n]
                                for k in range(2):
                                    x = slice((4 * k + n) * P, (4 * k + n + 1) * P)
                                    wh, wl = w_hi[:, u % SLOTS, x], w_lo[:, u % SLOTS, x]
                                    f = 2 * kp + k
                                    for i, (w, a) in enumerate(((wh, A_hi), (wh, A_lo), (wl, A_hi))):
                                        last = nc.tensor.matmul(bank[:, b], w, a[:, f],
                                                                start=(f == 0 and i == 0), stop=(f == nf - 1 and i == 2),
                                                                skip_group_check=True)
                                if kp == nf // 2 - 1 and n < 3:
                                    last.then_inc(sums_done.sem, 1)
                            if kp == nf // 2 - 1:
                                last.then_inc(sums_done.sem, 1)
                                pe.wait_ge(*sums_done.at(half * DT + 4 * g + 4))
                                pe.nop().then_inc(unit_done.sem, 1)
                            else:
                                last.then_inc(unit_done.sem, 1)

                @block.vector
                def _(dve):
                    if half == 1 and op is not None:
                        op.on_dve_first(dve)
                    for c in range(DT):
                        dve.wait_ge(*sums_done.at(half * DT + c + 1))
                        ins = nc.vector.tensor_tensor(hT[:, c], hT[:, c], bank[:, DOWN_BANKS[c]], ALU.add)
                        if half == 0:
                            ins.then_inc(added.sem, 1)
                        elif op is None:
                            ins.then_inc(h_final.sem, 1)
                        else:
                            ins.then_inc(op.h_done.sem, 1)
                            op.on_dve(dve, c)

                if half == 1 and op is not None:
                    @block.scalar
                    def _(act):
                        for c in range(DT):
                            op.on_act(act, c)

            gate_up(0, 0, FA, u0)
            down(0, 0, FA, u0 + 2 * FA)
            gate_up(1, FA, FB, u0 + 3 * FA)
            down(1, FA, FB, u0 + 3 * FA + 2 * FB)

        def layer_embedding(name, u0, i, op_in, op):
            gate_done = again("ple_gate", DT)
            sig_done = again("ple_sigmoid", DT)
            prod_done = again("ple_product", DT)

            @block.tensor
            def _(pe):
                pe.wait_ge(*op_in.rstd_done.at(1))
                pe.wait_ge(*op_in.h_done.at(DT))
                pe.wait_ge(*p_lo_done.at(i + 1))
                for g in range(2):
                    u = u0 + 5 * g
                    at_least(pe, prod_done, 4 * g)
                    pe.wait_ge(*w_split.at(u + 1))
                    for n in range(4):
                        for k in range(2):
                            x = slice((4 * k + n) * P, (4 * k + n + 1) * P)
                            wh, wl = w_hi[:, u % SLOTS, x], w_lo[:, u % SLOTS, x]
                            for j, (w, a) in enumerate(((wh, ple_hi), (wh, ple_lo), (wl, ple_hi))):
                                last = nc.tensor.matmul(bank[:, 2 + n], w, a[:, k], start=(k == 0 and j == 0),
                                                        stop=(k == 1 and j == 2))
                    last.then_inc(unit_done.sem, 1)
                    for n in range(4):
                        c = 4 * g + n
                        at_least(pe, gate_done, c - 1)
                        unit(pe, u + 1 + n, (u + 1 + n) % 2, bank[:, 6 + n % 2], MID_hi, MID_lo)

            @block.scalar
            def _(act):
                if i == 0:
                    act.wait_ge(*p_lo_done.at(1))
                    act.dma_start(ple_in[:], PT[1]).then_inc(p_loaded.sem, 16)
                for c in range(DT):
                    act.wait_ge(*gate_done.at(c + 1))
                    at_least(act, prod_done, c - 1)
                    nc.scalar.activation(tmp_b[:, c % 2], tmp_a[:, c % 2], ACT.Sigmoid).then_inc(sig_done.sem, 1)
                    op.on_act(act, c)
                if i == 0:
                    act.wait_ge(*p_loaded.at(32))
                    act.wait_ge(*unit_done.at(u0 + 6))
                    nc.scalar.copy(ple_hi[:], ple_in[:]).then_inc(p_hi_done.sem, 1)

            @block.vector
            def _(dve):
                op.on_dve_first(dve)
                for c in range(DT):
                    b, u = c % 2, u0 + 5 * (c // 4)
                    dve.wait_ge(*unit_done.at(u + 2 + c % 4))
                    at_least(dve, sig_done, c - 1)
                    nc.vector.tensor_tensor(tmp_a[:, b], bank[:, 6 + b], rstd[:], ALU.mult).then_inc(gate_done.sem, 1)
                    dve.wait_ge(*sig_done.at(c + 1))
                    at_least(dve, op.h_done, c - 1)
                    nc.vector.tensor_tensor(tmp_c[:, b], bank[:, 2 + c % 4], tmp_b[:, b], ALU.mult
                                            ).then_inc(prod_done.sem, 1)
                    dve.wait_ge(*prod_done.at(c + 1))
                    nc.vector.tensor_tensor(hT[:, c], hT[:, c], tmp_c[:, b], ALU.add).then_inc(op.h_done.sem, 1)
                    op.on_dve(dve, c)
                if i == 0:
                    dve.wait_ge(*p_hi_done.at(2))
                    nc.vector.tensor_tensor(ple_lo[:], ple_in[:], ple_hi[:].bitcast(F32), ALU.subtract
                                            ).then_inc(p_lo_done.sem, 1)

        h_final = sem("h_final")

        def layer_tail(n, u0, previous, ready, ffn_gain, ple_gain, next_targets):
            attn_op = Operand(f"attn{n}", [(ffn_gain, IN_hi, IN_lo)], previous)
            project_back(f"back{n}", u0, attn_op, ready)
            attn_op.stats(2)
            ffn_op = Operand(f"ffn{n}", [(ple_gain, MID_hi, MID_lo)], attn_op)
            feed_forward(f"ffn{n}", u0 + DT, attn_op, ffn_op)
            ffn_op.stats(0)
            next_op = Operand(f"ple{n}", next_targets, ffn_op)
            layer_embedding(f"ple{n}", u0 + DT + 3 * FT, n, ffn_op, next_op)
            next_op.stats(0)
            return next_op

        areas[0] = area0
        SH_hi, SH_lo = area("SH_hi", [P, DT, S], F32R), area("SH_lo", [P, DT, S], F32R)
        layer0 = layer_tail(0, U_QKV0 + 3 * PAIRS, x_op, [(sb_o_lo, HEADS)], G_FFN0, G_PLE0,
                            [(G_ATTN1, IN_hi, IN_lo), (G_SHARED, SH_hi, SH_lo)])

        NOFF = [0, 128, 384, 768]

        def softmax_attention(name, kind, npairs, u0, op_in, ready, src_kv, gain_q, gain_k, shared=None,
                              extra=None):
            fox, diff, dsa = kind == "fox", kind == "diff", kind == "dsa"
            per_pair = {"yq": 1, "sqq": 1, "statq": 1, "lnq": 1, "rnq": 1, "qn": 1, "qs": 1, "nat": 8, "max": 8,
                        "diag": 8, "st": 6, "p": 8, "o": 2, "rc": 2, "od": 2, "hi": 1, "lo": 1}
            if not dsa:
                per_pair |= {"yk": 1, "vt": 1, "sqk": 1, "statk": 1, "lnk": 1, "rnk": 1, "kn": 1, "turned": 1, "v": 1}
            if not fox:
                per_pair |= {"rotq": 1, "ropeq": 1, "qa": 1}
            if diff:
                per_pair |= {"rotk": 1, "ropek": 1, "ka": 1, "ks": 1, "df": 1, "sso": 1, "sto": 1, "lno": 1,
                             "rno": 1, "nrm": 1}
            s = {x: again("soft_" + x, n * npairs) for x, n in per_pair.items()}
            s["zeroed"] = again("soft_zeroed", 2 if fox else 1)
            rope = not fox
            QZ = area(name + "_q", [P, 2, 2, S], F32)
            K = shared["K"] if dsa else area(name + "_k", [P, 2, S], F32)
            VW = P if diff else 3 * HD
            V = shared["V"] if dsa else area(name + "_v", [P, 2, QT, VW], F32)
            DG = nc.alloc_sbuf_tensor_at(name + "_diag", [P, S], F32R, offset=place_used["neg_upto"])
            assert place_used["mask_kq"] == place_used["neg_upto"] + 4 * S
            RC = area(name + "_recip", [P, 2, S], F32) if diff else area(name + "_recip", [P, 1, S], F32)
            P0 = area(name + "_p0", [P, CAUSAL], F32)
            P1 = nc.alloc_sbuf_tensor_at(name + "_p1", [P, CAUSAL], F32, offset=place_used["tmp_b"])
            VT = nc.alloc_sbuf_tensor_at(name + "_vt", [P, S], F32, offset=place_used["tmp_b"] + 4 * CAUSAL)
            PW = (P0, P1)
            YQ, YK = tmp_a[:, 0], tmp_a[:, 1]
            SQ, RN = square, sumsq
            NM = area(name + "_max", [P, 2 * QT], F32)
            assert areas[0] <= nc.sbuf_usable_end, (areas[0], nc.sbuf_usable_end)

            def k_of(b):
                return K[:] if dsa else K[:, b]

            def v_of(b):
                return V if dsa else V[:, b]

            UPP = 1 if dsa else 3

            def loop(engine, body):
                body(0, 0, True)
                if npairs > 4:
                    with engine.Fori(0, (npairs - 2) // 2) as i:
                        body(2 * i + 1, 1, True)
                        body(2 * i + 2, 0, True)
                else:
                    for p in range(1, npairs - 1):
                        body(p, p % 2, True)
                body(npairs - 1, (npairs - 1) % 2, False)

            @block.tensor
            def _(pe):
                def project(p, b, n):
                    u = u0 + UPP * p + n
                    hi, lo = (IN_hi, IN_lo) if n == 0 else src_kv
                    if n == 0:
                        at_least(pe, s["yq"] if dsa else s["v"], p)
                        if dsa:
                            at_least(pe, s["ropeq"], p)
                    elif n == 1:
                        at_least(pe, s["rnk"], p)
                        if rope:
                            at_least(pe, s["ropek"], p)
                    else:
                        pe.wait_ge(*s["ropeq" if rope else "rnq"].at(p + 1))
                    slot = (u0 + UPP * p + n if isinstance(p, int) else u0 + b + n) % SLOTS
                    unit(pe, u, slot, bank[:, 6 + n % 2], hi, lo)

                def stat(p, x, b6):
                    pe.wait_ge(*s["sq" + x].at(p + 1))
                    nc.tensor.matmul(bank[:, b6], head_ones[:], SQ[:], start=True, stop=True
                                     ).then_inc(s["stat" + x].sem, 1)

                def rotate(p, x, b6):
                    pe.wait_ge(*s[x + "n"].at(p + 1))
                    nc.tensor.matmul(bank[:, b6], extra["perm"][:], (YQ if x == "q" else YK), start=True, stop=True
                                     ).then_inc(s["rot" + x].sem, 1)

                def turn_v(p, b):
                    pe.wait_ge(*s["vt"].at(p + 1))
                    for t in range(QT):
                        last = nc.tensor.transpose(bank[:, 6, t * P:(t + 1) * P], VT[:, t * P:(t + 1) * P],
                                                   ident[:])
                    last.then_inc(s["turned"].sem, 1)

                def natural(p, b, h):
                    pe.wait_ge(*s["qs"].at(p + 1))
                    if not dsa:
                        pe.wait_ge(*s["ks" if rope else "kn"].at(p + 1))
                    if diff:
                        at_least(pe, s["nrm"], p)
                    for t in range(QT):
                        at_least(pe, s["max"], 8 * p + 4 * h + t - 1)
                        out = bank[:, t % 2, 0:P * (t + 1)]
                        nc.tensor.matmul(out, QZ[:, b, h, t * P:(t + 1) * P], k_of(b)[:, 0:P * (t + 1)],
                                         start=True, stop=False)
                        if fox:
                            if t == 0:
                                pe.wait_ge(*extra["decay_row"].at(2 * p + h + 1))
                            nc.tensor.matmul(out, ones_r[0:HEADS], extra["row"][:, 0:P * (t + 1)], start=False,
                                             stop=False)
                        if dsa:
                            last = nc.tensor.matmul(out, ident_r[:], extra["mask"][:, NOFF[t]:NOFF[t] + P * (t + 1)],
                                                    start=False, stop=True)
                        else:
                            last = nc.tensor.matmul(out[:, P * t:], ident_r[:], mask_qk[:], start=False, stop=True)
                        last.then_inc(s["nat"].sem, 1)

                def transposed(p, b, h):
                    pe.wait_ge(*s["diag"].at(8 * p + 4 * h + 4))
                    at_least(pe, s["p"], 8 * p + 4 * h)
                    for _, _, tiles in GROUPS:
                        for j in tiles:
                            out = tile_in_bank(2, j)
                            nc.tensor.matmul(out, k_of(b)[:, j * P:(j + 1) * P], QZ[:, b, h, j * P:S],
                                             start=(j != 3), stop=False, skip_group_check=True)
                            nc.tensor.matmul(out, ones_r[:], DG[:, j * P:S], start=False, stop=False,
                                             skip_group_check=True)
                            if dsa:
                                last = nc.tensor.matmul(out, ident_r[:], extra["maskT"][:, COL[j]:COL[j] + WIDTH[j]],
                                                        start=False, stop=True, skip_group_check=True)
                            else:
                                last = nc.tensor.matmul(out[:, 0:P], ident_r[:], mask_kq[:], start=False, stop=True,
                                                        skip_group_check=True)
                        last.then_inc(s["st"].sem, 1)

                def output(p, b, h):
                    if not dsa:
                        pe.wait_ge(*s["v"].at(p + 1))
                    pe.wait_ge(*s["p"].at(8 * p + 4 * h + 4))
                    at_least(pe, s["od"], 2 * p + h)
                    if diff:
                        pe.wait_ge(*s["max"].at(8 * p + 8))
                    x = 0 if diff else HD * h
                    for j in range(QT):
                        w = PW[h][:, COL[j]:COL[j] + WIDTH[j]]
                        last = nc.tensor.matmul(bank[:, 5, j * P:S], v_of(b)[:, j, x:x + P], w, start=(j == 0),
                                                stop=(j == QT - 1))
                    if diff:
                        for j in range(QT):
                            w = PW[h][:, COL[j]:COL[j] + WIDTH[j]]
                            last = nc.tensor.matmul(bank[:, h, j * P:S], ones[:], w, start=(j == 0),
                                                    stop=(j == QT - 1))
                    last.then_inc(s["o"].sem, 1)

                for x, n in ready:
                    pe.wait_ge(*x.at(n))

                def norm_out(p):
                    pe.wait_ge(*s["sso"].at(p + 1))
                    nc.tensor.matmul(bank[:, 0], ones[:], SQ[:], start=True, stop=True).then_inc(s["sto"].sem, 1)

                project(0, 0, 0)
                stat(0, "q", 6)
                if rope:
                    rotate(0, "q", 6)
                if not dsa:
                    project(0, 0, 1)
                    stat(0, "k", 7)
                    if rope:
                        rotate(0, "k", 7)
                    project(0, 0, 2)
                    turn_v(0, 0)

                def pair(p, b, more):
                    c = (b + 1) % 2
                    natural(p, b, 0)
                    if more:
                        project(p + 1, c, 0)
                    transposed(p, b, 0)
                    natural(p, b, 1)
                    if more and not dsa:
                        project(p + 1, c, 1)
                    if more:
                        stat(p + 1, "q", 6)
                    output(p, b, 0)
                    if more and not dsa:
                        stat(p + 1, "k", 7)
                    if more and rope:
                        rotate(p + 1, "q", 6)
                    transposed(p, b, 1)
                    if more and not dsa:
                        if rope:
                            rotate(p + 1, "k", 7)
                        project(p + 1, c, 2)
                    output(p, b, 1)
                    if more and not dsa:
                        turn_v(p + 1, c)
                    if diff:
                        norm_out(p)

                loop(pe, pair)

            @block.scalar
            def _(act):
                def squares(p, x):
                    act.wait_ge(*s["y" + x].at(p + 1))
                    if x == "q":
                        at_least(act, s["statq"] if dsa else s["statk"], p)
                        if diff:
                            at_least(act, s["sto"], p - 1)
                    else:
                        act.wait_ge(*s["statq"].at(p + 1))
                    nc.scalar.activation(SQ[:], YQ if x == "q" else YK, ACT.Square).then_inc(s["sq" + x].sem, 1)

                def norms(p, x, b6):
                    act.wait_ge(*s["stat" + x].at(p + 1))
                    if x == "q":
                        at_least(act, s["qn"] if dsa else s["kn"], p)
                        if diff:
                            at_least(act, s["nrm"], p - 1)
                    else:
                        act.wait_ge(*s["qn" if rope else "qs"].at(p + 1))
                    nc.scalar.activation(RN[:], bank[:, b6], ACT.Ln, bias=eps_c[:], scale=1.0 / HD
                                         ).then_inc(s["ln" + x].sem, 1)
                    act.wait_ge(*s["ln" + x].at(p + 1))
                    nc.scalar.activation(RN[:], RN[:], ACT.Exp, scale=-0.5).then_inc(s["rn" + x].sem, 1)

                def copy_v(p, b):
                    act.wait_ge(*s["turned"].at(p + 1))
                    at_least(act, s["o"], 2 * (p - 1))
                    v = bank[:, 6].rearrange("p (t c) -> p t c", t=QT)
                    if diff:
                        nc.scalar.copy(V[:, b], v).then_inc(s["v"].sem, 1)
                    else:
                        nc.scalar.copy(V[:, b, :, 0:HD], v[:, :, 0:HD])
                        nc.scalar.copy(V[:, b, :, 2 * HD:3 * HD], v[:, :, HD:P]).then_inc(s["v"].sem, 1)

                def weights(p, h):
                    at_least(act, s["o"], 2 * (p - 1) + h + 1)
                    for g, (_, _, tiles) in enumerate(GROUPS):
                        act.wait_ge(*s["st"].at(6 * p + 3 * h + g + 1))
                        if fox:
                            act.sem_inc(act_turns.sem, 1)
                        for j in tiles:
                            bias = column(extra["key_bias"], HEADS * j + 2 * p + h) if fox else 0.0
                            nc.scalar.activation(PW[h][:, COL[j]:COL[j] + WIDTH[j]], tile_in_bank(2, j), ACT.Exp,
                                                 bias=bias).then_inc(s["p"].sem, 1)

                act.preload_act_table_set("natural_log_exp_and_others")
                squares(0, "q")
                norms(0, "q", 6)
                if not dsa:
                    squares(0, "k")
                    norms(0, "k", 7)
                    copy_v(0, 0)

                def pair(p, b, more):
                    weights(p, 0)
                    if more:
                        squares(p + 1, "q")
                        norms(p + 1, "q", 6)
                        if not dsa:
                            squares(p + 1, "k")
                            norms(p + 1, "k", 7)
                    weights(p, 1)
                    if more and not dsa:
                        copy_v(p + 1, (b + 1) % 2)
                    if diff:
                        act.wait_ge(*s["df"].at(p + 1))
                        if more:
                            act.wait_ge(*s["statk"].at(p + 2))
                            act.wait_ge(*s["kn"].at(p + 2))
                        nc.scalar.activation(SQ[:], RC[:, 0], ACT.Square).then_inc(s["sso"].sem, 1)
                        act.wait_ge(*s["sto"].at(p + 1))
                        nc.scalar.activation(RN[:], bank[:, 0], ACT.Ln, bias=eps_c[:], scale=1.0 / P
                                             ).then_inc(s["lno"].sem, 1)
                        act.wait_ge(*s["lno"].at(p + 1))
                        nc.scalar.activation(RN[:], RN[:], ACT.Exp, scale=-0.5).then_inc(s["rno"].sem, 1)
                        act.wait_ge(*s["nrm"].at(p + 1))
                    else:
                        act.wait_ge(*s["od"].at(2 * p + 2))
                    act.sem_inc(act_turns.sem, 1)
                    t = p if not diff else p + 4
                    nc.scalar.copy(tile(MID_hi, t), RC[:, 0]).then_inc(s["hi"].sem, 1)

                loop(act, pair)

            @block.vector
            def _(dve):
                def take(p, b, n):
                    dve.wait_ge(*unit_done.at(u0 + UPP * p + n + 1))
                    if n == 0:
                        if rope:
                            at_least(dve, s["ropeq"], p)
                        at_least(dve, s["qs"], p)
                        nc.vector.tensor_tensor(YQ, bank[:, 6], rstd[:], ALU.mult).then_inc(s["yq"].sem, 1)
                    elif n == 1:
                        nc.vector.tensor_tensor(YK, bank[:, 7], rstd[:], ALU.mult).then_inc(s["yk"].sem, 1)
                    else:
                        at_least(dve, s["turned"], p)
                        nc.vector.tensor_tensor(VT[:], bank[:, 6], rstd[:], ALU.mult).then_inc(s["vt"].sem, 1)

                def finish_q(p, b):
                    dve.wait_ge(*s["rnq"].at(p + 1))
                    if rope:
                        nc.vector.scalar_tensor_tensor(YQ, YQ, extra["gq"], RN[:], ALU.mult, ALU.mult
                                                       ).then_inc(s["qn"].sem, 1)
                        return
                    at_least(dve, s["st"], 6 * (p - 1))
                    for h in range(2):
                        r = rows(h)
                        o = nc.vector.scalar_tensor_tensor(QZ[r, b, h], YQ[r], extra["gq"][r], RN[r],
                                                           ALU.mult, ALU.mult)
                        if h == 0:
                            o.then_inc(s["qn"].sem, 1)
                    o.then_inc(s["qs"].sem, 1)

                def finish_k(p, b):
                    dve.wait_ge(*s["rnk"].at(p + 1))
                    at_least(dve, s["st"], 6 * (p - 1))
                    if rope:
                        nc.vector.scalar_tensor_tensor(YK, YK, hgains[:, gain_k:gain_k + 1], RN[:],
                                                       ALU.mult, ALU.mult).then_inc(s["kn"].sem, 1)
                        return
                    nc.vector.scalar_tensor_tensor(K[:, b], YK, hgains[:, gain_k:gain_k + 1], RN[:],
                                                   ALU.mult, ALU.mult).then_inc(s["kn"].sem, 1)

                def rope_it(p, b, x, b6):
                    y = YQ if x == "q" else YK
                    dve.wait_ge(*s["rot" + x].at(p + 1))
                    at_least(dve, s["st"], 6 * (p - 1))
                    nc.vector.tensor_tensor(SW[:], bank[:, b6], extra["sin"][:], ALU.mult).then_inc(s["rope" + x].sem, 1)
                    nc.vector.tensor_tensor(y, y, extra["cos"][:], ALU.mult).then_inc(s[x + "a"].sem, 1)
                    dve.wait_ge(*s["rope" + x].at(p + 1))
                    dve.wait_ge(*s[x + "a"].at(p + 1))
                    if x == "k":
                        nc.vector.tensor_tensor(K[:, b], y, SW[:], ALU.add).then_inc(s["ks"].sem, 1)
                        dve.wait_ge(*s["ks"].at(p + 1))
                        return
                    for h in range(2):
                        r = rows(h)
                        o = nc.vector.tensor_tensor(QZ[r, b, h], y[r], SW[r], ALU.add)
                    o.then_inc(s["qs"].sem, 1)
                    dve.wait_ge(*s["qs"].at(p + 1))

                def maxima(p, h):
                    if fox:
                        at_least(dve, s["nat"], 8 * p + 4 * h)
                        nc.vector.tensor_scalar(extra["row"][:], extra["F"][:], column(ident, 2 * p + h)[0:HEADS],
                                                -1.0, ALU.mult, ALU.mult).then_inc(extra["decay_row"].sem, 1)
                    at_least(dve, s["st"], 6 * p + 3 * h)
                    for t in range(QT):
                        k = 8 * p + 4 * h + t
                        dve.wait_ge(*s["nat"].at(k + 1))
                        m = NM[:, 4 * h + t:4 * h + t + 1]
                        nc.vector.tensor_reduce(m, bank[:, t % 2, 0:P * (t + 1)], AX.X, ALU.max, negate=True
                                                ).then_inc(s["max"].sem, 1)
                        dve.wait_ge(*s["max"].at(k + 1))
                        nc.vector.tensor_scalar(DG[:, t * P:(t + 1) * P], ident[:], m, None, ALU.mult
                                                ).then_inc(s["diag"].sem, 1)

                def outputs(p, h):
                    if h == 0:
                        at_least(dve, s["lo"], p)
                    dve.wait_ge(*s["o"].at(2 * p + h + 1))
                    if diff:
                        nc.vector.reciprocal(RC[:, h], bank[:, h]).then_inc(s["rc"].sem, 1)
                        dve.wait_ge(*s["rc"].at(2 * p + h + 1))
                        nc.vector.tensor_tensor(RC[:, h], RC[:, h], bank[:, 5], ALU.mult).then_inc(s["od"].sem, 1)
                        if h == 1:
                            dve.wait_ge(*s["od"].at(2 * p + 2))
                            nc.vector.scalar_tensor_tensor(RC[:, 0], RC[:, 1], extra["neg_lam"], RC[:, 0],
                                                           ALU.mult, ALU.add).then_inc(s["df"].sem, 1)
                            dve.wait_ge(*s["rno"].at(p + 1))
                            nc.vector.scalar_tensor_tensor(RC[:, 0], RC[:, 0], 1.0 - LAMBDA_INIT, RN[:],
                                                           ALU.mult, ALU.mult).then_inc(s["nrm"].sem, 1)
                        return
                    r = rows(h)
                    nc.vector.reciprocal(RC[r, 0], bank[rows(1 - h), 5]).then_inc(s["rc"].sem, 1)
                    dve.wait_ge(*s["rc"].at(2 * p + h + 1))
                    nc.vector.tensor_tensor(RC[r, 0], RC[r, 0], bank[r, 5], ALU.mult).then_inc(s["od"].sem, 1)

                def low(p):
                    dve.wait_ge(*s["hi"].at(p + 1))
                    t = p if not diff else p + 4
                    nc.vector.tensor_tensor(tile(MID_lo, t), RC[:, 0], tile(MID_hi, t).bitcast(F32), ALU.subtract
                                            ).then_inc(s["lo"].sem, 1)

                SW = extra.get("swap")
                nc.vector.memset(QZ[:], 0.0).then_inc(s["zeroed"].sem, 1)
                if fox:
                    nc.vector.memset(V[:, :, :, HD:2 * HD], 1.0).then_inc(s["zeroed"].sem, 1)
                dve.wait_ge(*s["zeroed"].at(2 if fox else 1))
                take(0, 0, 0)
                finish_q(0, 0)
                if rope:
                    rope_it(0, 0, "q", 6)
                if not dsa:
                    take(0, 0, 1)
                    finish_k(0, 0)
                    if rope:
                        rope_it(0, 0, "k", 7)
                    take(0, 0, 2)

                meanwhile = extra.get("meanwhile", lambda p, part: None)

                def pair(p, b, more):
                    c = (b + 1) % 2
                    maxima(p, 0)
                    if more:
                        take(p + 1, c, 0)
                    meanwhile(p, 0)
                    maxima(p, 1)
                    meanwhile(p, 1)
                    if more:
                        if not dsa:
                            take(p + 1, c, 1)
                        finish_q(p + 1, c)
                    outputs(p, 0)
                    meanwhile(p, 2)
                    if more:
                        if not dsa:
                            finish_k(p + 1, c)
                        if rope:
                            rope_it(p + 1, c, "q", 6)
                            if not dsa:
                                rope_it(p + 1, c, "k", 7)
                        if not dsa:
                            take(p + 1, c, 2)
                    meanwhile(p, 3)
                    outputs(p, 1)
                    low(p)

                loop(dve, pair)
            return s

        areas[0] = area0 + 2 * 4 * DT * S
        LF = nc.alloc_sbuf_tensor_at("LF", [HEADS, S], F32, offset=place_used["ple_in"])
        decay_row = nc.alloc_sbuf_tensor_at("decay_row", [HEADS, S], F32R, offset=place_used["ple_in"] + 4 * S)
        key_bias = nc.alloc_sbuf_tensor_at("key_bias", [P, QT * HEADS], F32,
                                           offset=place_used["tmp_b"] + 4 * (CAUSAL + S))
        gq_fox = area("gq_fox", [P, 1], F32)
        f_x, f_abs, f_exp, f_ln, f_min, f_log, f_cum, f_turned, f_bias = (
            sem("f_" + x) for x in "x abs exp ln min log cum turned bias".split())
        f_row = sem("f_row")

        @block.tensor
        def _(pe):
            pe.wait_ge(*layer0.rstd_done.at(1))
            unit(pe, U_F1, U_F1 % SLOTS, bank[:, 6], SH_hi, SH_lo)
            pe.wait_ge(*f_cum.at(1))
            for t in range(QT):
                last = nc.tensor.transpose(bank[:, 7, t * HEADS:(t + 1) * HEADS], LF[:, t * P:(t + 1) * P],
                                           ident[0:HEADS, 0:HEADS])
            last.then_inc(f_turned.sem, 1)

        @block.vector
        def _(dve):
            x, a = tmp_a[0:HEADS, 0], tmp_a[0:HEADS, 1]
            dve.wait_ge(*unit_done.at(U_F1 + 1))
            dve.wait_ge(*small_loaded.at(80))
            nc.vector.tensor_tensor(x, bank[0:HEADS, 6], rstd[0:HEADS], ALU.mult).then_inc(f_x.sem, 1)
            dve.wait_ge(*f_x.at(1))
            nc.vector.tensor_scalar(x, x, forget_bias[:], None, ALU.add).then_inc(f_x.sem, 1)
            dve.wait_ge(*f_abs.at(1))
            nc.vector.tensor_scalar(x, x, 0.0, None, ALU.min).then_inc(f_min.sem, 1)
            dve.wait_ge(*f_min.at(1))
            dve.wait_ge(*f_ln.at(1))
            nc.vector.tensor_tensor(x, x, a, ALU.subtract).then_inc(f_log.sem, 1)
            nc.vector.memset(tmp_b[0:HEADS, 0], 1.0).then_inc(f_log.sem, 1)
            nc.vector.tensor_scalar(gq_fox[:], hgains[:, H_FOXQ:H_FOXQ + 1], HD ** -0.5, None, ALU.mult
                                    ).then_inc(f_log.sem, 1)
            dve.wait_ge(*f_log.at(3))
            nc.vector.tensor_tensor_scan(LF[:], tmp_b[0:HEADS, 0], x, 0.0, ALU.mult, ALU.add).then_inc(f_cum.sem, 1)
            dve.wait_ge(*f_turned.at(1))
            nc.vector.tensor_scalar(key_bias[:], bank[:, 7, 0:QT * HEADS], -1.0, None, ALU.mult).then_inc(f_bias.sem, 1)
            dve.wait_ge(*f_bias.at(1))

        @block.scalar
        def _(act):
            x, a = tmp_a[0:HEADS, 0], tmp_a[0:HEADS, 1]
            act.wait_ge(*f_x.at(2))
            nc.scalar.activation(a, x, ACT.Abs).then_inc(f_abs.sem, 1)
            act.wait_ge(*f_abs.at(1))
            nc.scalar.activation(a, a, ACT.Exp, scale=-1.0).then_inc(f_exp.sem, 1)
            act.wait_ge(*f_exp.at(1))
            nc.scalar.activation(a, a, ACT.Ln, bias=one_c[0:HEADS]).then_inc(f_ln.sem, 1)
            act.wait_ge(*f_bias.at(1))

        fox = softmax_attention("fox", "fox", PAIRS, U_KVQ1, layer0, [(f_bias, 1)], (SH_hi, SH_lo), H_FOXQ, H_FOXK,
                                extra={"row": decay_row, "F": LF, "decay_row": f_row, "key_bias": key_bias,
                                       "gq": gq_fox})
        layer1 = layer_tail(1, U_KVQ1 + 3 * PAIRS, layer0, [(fox["lo"], PAIRS)], G_FFN1, G_PLE1,
                            [(G_MIX, IN_hi, IN_lo)])

        mem_in = nc.alloc_sbuf_tensor_at("mem_in", [P, DT, M], F32, offset=place_used["ple_in"])
        areas[0] = area0 + 2 * 4 * FA * S
        sin_t, cos_t = area("sin_t", [P, S], F32), area("cos_t", [P, S], F32)
        swap = area("swap", [P, S], F32)
        small = area("small", [P, 24], F32)
        inv_freq, lam_in, lam_products, lam_exp = small[:, 0:1], small[0:HD, 1:5], small[0:HD, 5:7], small[:, 7:9]
        neg_lam, gq_a, gq_b = small[:, 9:10], small[:, 10:11], small[:, 11:12]
        gq_x, top8 = small[:, 12:14], small[:, 16:24]
        pos_i = nc.alloc_sbuf_tensor_at("pos_i", [P, S], I32, offset=place_used["tmp_b"])
        angle, turns = tmp_a[:, 0], tmp_a[:, 1]
        areas[0] = area0
        dsa_k = area("dsa_k", [P, S], F32)
        dsa_v = area("dsa_v", [P, QT, 3 * HD], F32)
        chosen = area("chosen", [P, CAUSAL], F32R)
        chosen_t = area("chosen_t", [P, CAUSAL], F32R)
        TOP_OFF = {1: 0, 2: 256, 3: 640}
        index_scores = area("index_scores", [P, 1152], F32)
        after_index = areas[0]
        idx_q = area("idx_q", [P, 2, 2, S], F32)
        idx_k = area("idx_k", [P, S], F32)
        idx_w = area("idx_w", [P, QT, 4], F32)
        relu = area("relu", [P, 2, S], F32)
        idx_tmp = area("idx_tmp", [P, 5, S], F32)
        i_loaded, m_loaded = sem("index_loaded"), sem("memory_loaded")
        t_step, t_sin, t_lam, t_exp = (sem("table_" + x) for x in ("step", "sin", "lam", "exp"))
        i_taken, i_rot, i_sw, i_cos, i_done = (sem("index_" + x) for x in "taken rotated swapped cosine done".split())
        i_sq, i_stat, i_ln, i_rn, i_kn = (again("soft_" + x, 1) for x in "sqk statk lnk rnk kn".split())
        i_turned, i_v = again("soft_turned", 1), again("soft_v", 3)
        i_z, i_relu, i_sum = (sem("index_" + x) for x in "z relu sum".split())
        i_max, i_out, i_mask, i_maskt, i_copied = (sem("top_" + x) for x in "max out mask turned copied".split())
        i_zeroed = sem("index_zeroed")
        TOPK = S // 4
        K_I, V_W, Q_I, Q_J, K_A = range(5)
        UNIT_BANK, ROT_BANK = (1, 2, 3, 4, 5), {K_I: 6, Q_I: 7, Q_J: 1, K_A: 3}
        ROTATED = (K_I, Q_I, Q_J, K_A)

        @block.scalar
        def _(act):
            act.dma_start(inv_freq, INVF).then_inc(i_loaded.sem, 16)
            act.dma_start(lam_in, LAM).then_inc(i_loaded.sem, 16)
            act.dma_start(pos_i[:], POS[0].partition_broadcast(P)).then_inc(i_loaded.sem, 16)
            act.wait_ge(*layer1.h_done.at(DT))
            act.dma_start(mem_in[:], MEMT).then_inc(m_loaded.sem, 16)
            act.wait_ge(*t_step.at(9))
            nc.scalar.activation(sin_t[:], turns, ACT.Sin).then_inc(t_sin.sem, 1)
            nc.scalar.activation(cos_t[:], turns, ACT.Sin, scale=0.5).then_inc(t_sin.sem, 1)
            act.preload_act_table_set("natural_log_exp_and_others")
            act.wait_ge(*t_lam.at(2))
            nc.scalar.activation(lam_exp, bank[:, 6, 0:2], ACT.Exp).then_inc(t_exp.sem, 1)

        @block.vector
        def _(dve):
            def step(n):
                dve.wait_ge(*t_step.at(n))

            dve.wait_ge(*layer1.rstd_done.at(1))
            dve.wait_ge(*i_loaded.at(48))
            nc.vector.tensor_copy(angle, pos_i[:]).then_inc(t_step.sem, 1)
            step(1)
            nc.vector.tensor_scalar(angle, angle, inv_freq, None, ALU.mult).then_inc(t_step.sem, 1)
            step(2)
            ROUND = 1.5 * 2.0 ** 23
            nc.vector.tensor_scalar(turns, angle, 1.0 / (2 * np.pi), ROUND, ALU.mult, ALU.add).then_inc(t_step.sem, 1)
            step(3)
            nc.vector.tensor_scalar(turns, turns, ROUND, None, ALU.subtract).then_inc(t_step.sem, 1)
            step(4)
            c1 = 6.28125
            c2 = float(np.round((2 * np.pi - c1) * 2.0 ** 20) / 2.0 ** 20)
            for n, c in enumerate((c1, c2, 2 * np.pi - c1 - c2)):
                nc.vector.scalar_tensor_tensor(angle, turns, -c, angle, ALU.mult, ALU.add).then_inc(t_step.sem, 1)
                step(5 + n)
            nc.vector.tensor_scalar(turns, angle, 3.1415925, -3.1415925, ALU.min, ALU.max).then_inc(t_step.sem, 1)
            nc.vector.tensor_tensor(lam_products, small[0:HD, 1:5:2], small[0:HD, 2:5:2], ALU.mult
                                    ).then_inc(t_step.sem, 1)
            dve.wait_ge(*t_sin.at(2))
            nc.vector.tensor_tensor(cos_t[:], cos_t[:], cos_t[:], ALU.mult).then_inc(t_step.sem, 1)
            step(10)
            nc.vector.tensor_scalar(cos_t[:], cos_t[:], -2.0, 1.0, ALU.mult, ALU.add).then_inc(t_step.sem, 1)
            dve.wait_ge(*t_exp.at(1))
            nc.vector.tensor_tensor(neg_lam, lam_exp[:, 1:2], lam_exp[:, 0:1], ALU.subtract).then_inc(t_step.sem, 1)
            step(12)
            nc.vector.tensor_scalar(neg_lam, neg_lam, LAMBDA_INIT, None, ALU.subtract).then_inc(t_step.sem, 1)
            nc.vector.tensor_scalar(gq_a, hgains[:, H_QA:H_QA + 1], HD ** -0.5, None, ALU.mult).then_inc(t_step.sem, 1)
            nc.vector.tensor_scalar(gq_b, hgains[:, H_QB:H_QB + 1], HD ** -0.5, None, ALU.mult).then_inc(t_step.sem, 1)
            nc.vector.tensor_scalar(gq_x, xgains[:, 0:2], 1.0 / 16, None, ALU.mult).then_inc(t_step.sem, 1)
            nc.vector.memset(idx_q[:], 0.0).then_inc(i_zeroed.sem, 1)
            nc.vector.memset(dsa_v[:, :, HD:2 * HD], 1.0).then_inc(i_zeroed.sem, 1)
            dve.wait_ge(*i_zeroed.at(2))
            step(16)

            def take(n):
                dve.wait_ge(*unit_done.at(U_IDX + n + 1))
                nc.vector.tensor_tensor(idx_tmp[:, n], bank[:, UNIT_BANK[n]], rstd[:], ALU.mult).then_inc(i_taken.sem, 1)

            def rotary(n, k):
                dve.wait_ge(*i_rot.at(k + 1))
                at_least(dve, i_done, k)
                nc.vector.tensor_tensor(swap[:], bank[:, ROT_BANK[n]], sin_t[:], ALU.mult).then_inc(i_sw.sem, 1)
                nc.vector.tensor_tensor(idx_tmp[:, n], idx_tmp[:, n], cos_t[:], ALU.mult).then_inc(i_cos.sem, 1)
                dve.wait_ge(*i_sw.at(k + 1))
                dve.wait_ge(*i_cos.at(k + 1))
                if n in (Q_I, Q_J):
                    for h in range(2):
                        last = nc.vector.tensor_tensor(idx_q[rows(h), n - Q_I, h], idx_tmp[rows(h), n], swap[rows(h)],
                                                       ALU.add)
                else:
                    last = nc.vector.tensor_tensor((idx_k if n == K_I else dsa_k)[:], idx_tmp[:, n], swap[:], ALU.add)
                last.then_inc(i_done.sem, 1)

            take(K_I)
            take(V_W)
            rotary(K_I, 0)
            take(Q_I)
            take(Q_J)
            rotary(Q_I, 1)
            rotary(Q_J, 2)
            take(K_A)
            dve.wait_ge(*i_rn.at(1))
            dve.wait_ge(*i_taken.at(5))
            nc.vector.scalar_tensor_tensor(idx_tmp[:, K_A], idx_tmp[:, K_A], hgains[:, H_KA:H_KA + 1], sumsq[:],
                                           ALU.mult, ALU.mult).then_inc(i_kn.sem, 1)
            for t in range(1, QT):
                acc = index_scores[:, TOP_OFF[t]:TOP_OFF[t] + P * (t + 1)]
                for h in range(4):
                    k = 4 * (t - 1) + h
                    dve.wait_ge(*i_relu.at(k + 1))
                    if h == 0:
                        dve.wait_ge(*i_v.at(3))
                        nc.vector.tensor_scalar(acc, relu[:, k % 2, 0:P * (t + 1)], idx_w[:, t, h:h + 1], None, ALU.mult
                                                ).then_inc(i_sum.sem, 1)
                    else:
                        dve.wait_ge(*i_sum.at(k))
                        nc.vector.scalar_tensor_tensor(acc, relu[:, k % 2, 0:P * (t + 1)], idx_w[:, t, h:h + 1], acc,
                                                       ALU.mult, ALU.add).then_inc(i_sum.sem, 1)
            dve.wait_ge(*i_sum.at(12))
            for t in range(1, QT):
                x = index_scores[:, TOP_OFF[t] + P * t:TOP_OFF[t] + P * (t + 1)]
                nc.vector.tensor_tensor(x, x, mask_qk[:].bitcast(F32), ALU.add).then_inc(i_sum.sem, 1)
            rotary(K_A, 3)
            nc.vector.tensor_copy(chosen[:, 0:P], mask_qk[:].bitcast(F32)).then_inc(i_mask.sem, 1)
            dve.wait_ge(*i_sum.at(15))
            dve.wait_ge(*i_done.at(4))

        FOUND = -3.0e38

        def choose(part):
            for t in range(1, QT):
                k = 3 * part + t - 1
                x = index_scores[:, TOP_OFF[t]:TOP_OFF[t] + P * (t + 1)]
                nc.vector.wait_ge(*i_out.at(k)) if k else None
                nc.vector.max(top8, x).then_inc(i_max.sem, 1)
                nc.vector.wait_ge(*i_max.at(k + 1))
                nc.vector.match_replace(x, top8, x, FOUND).then_inc(i_out.sem, 1)
            if part == TOPK // 8 - 1:
                nc.vector.wait_ge(*i_out.at(3 * TOPK // 8))
                nc.vector.tensor_scalar(chosen[:, P:], index_scores[:], FOUND / 1.5, NEG, ALU.is_gt, ALU.mult
                                        ).then_inc(i_mask.sem, 1)

        @block.tensor
        def _(pe):
            pe.wait_ge(*t_step.at(9))
            nc.tensor.matmul(bank[:, 6, 0:2], ones[0:HD], lam_products, start=True, stop=True).then_inc(t_lam.sem, 2)

            def rotate(n, k):
                nc.tensor.matmul(bank[:, ROT_BANK[n]], perm[:], idx_tmp[:, n], start=True, stop=True
                                 ).then_inc(i_rot.sem, 1)

            def project(n):
                unit(pe, U_IDX + n, (U_IDX + n) % SLOTS, bank[:, UNIT_BANK[n]], IN_hi, IN_lo)

            project(K_I)
            project(V_W)
            pe.wait_ge(*t_exp.at(1))
            pe.wait_ge(*i_taken.at(1))
            rotate(K_I, 0)
            project(Q_I)
            project(Q_J)
            pe.wait_ge(*i_taken.at(3))
            rotate(Q_I, 1)
            pe.wait_ge(*i_taken.at(4))
            rotate(Q_J, 2)
            for t in range(QT):
                last = nc.tensor.transpose(bank[:, 2, t * P:(t + 1) * P], idx_tmp[:, V_W, t * P:(t + 1) * P], ident[:])
            last.then_inc(i_turned.sem, 1)
            project(K_A)
            pe.wait_ge(*i_sq.at(1))
            nc.tensor.matmul(bank[:, 4], head_ones[:], square[:], start=True, stop=True).then_inc(i_stat.sem, 1)
            pe.wait_ge(*i_done.at(3))
            for t in range(1, QT):
                for h in range(4):
                    k = 4 * (t - 1) + h
                    at_least(pe, i_relu, k - 1)
                    nc.tensor.matmul(bank[:, 6 + k % 2, 0:P * (t + 1)], idx_q[:, h // 2, h % 2, t * P:(t + 1) * P],
                                     idx_k[:, 0:P * (t + 1)], start=True, stop=True).then_inc(i_z.sem, 1)
            pe.wait_ge(*i_kn.at(1))
            rotate(K_A, 3)

        @block.scalar
        def _(act):
            v = bank[:, 2].rearrange("p (t c) -> p t c", t=QT)
            act.wait_ge(*i_turned.at(1))
            act.wait_ge(*i_zeroed.at(2))
            nc.scalar.copy(dsa_v[:, :, 0:HD], v[:, :, 0:HD]).then_inc(i_v.sem, 1)
            nc.scalar.copy(dsa_v[:, :, 2 * HD:], v[:, :, 0:HD]).then_inc(i_v.sem, 1)
            nc.scalar.activation(idx_w[:], v[:, :, HD:HD + 4], ACT.Copy, scale=1.0 / 16).then_inc(i_v.sem, 1)
            act.wait_ge(*i_taken.at(5))
            nc.scalar.activation(square[:], idx_tmp[:, K_A], ACT.Square).then_inc(i_sq.sem, 1)
            act.wait_ge(*i_stat.at(1))
            nc.scalar.activation(sumsq[:], bank[:, 4], ACT.Ln, bias=eps_c[:], scale=1.0 / HD).then_inc(i_ln.sem, 1)
            act.wait_ge(*i_ln.at(1))
            nc.scalar.activation(sumsq[:], sumsq[:], ACT.Exp, scale=-0.5).then_inc(i_rn.sem, 1)
            for t in range(1, QT):
                for h in range(4):
                    k = 4 * (t - 1) + h
                    act.wait_ge(*i_z.at(k + 1))
                    at_least(act, i_sum, k - 1)
                    nc.scalar.activation(relu[:, k % 2, 0:P * (t + 1)], bank[:, 6 + k % 2, 0:P * (t + 1)], ACT.Relu
                                         ).then_inc(i_relu.sem, 1)

        rotary_extra = {"perm": perm, "sin": sin_t, "cos": cos_t, "swap": swap}
        areas[0] = after_index
        diff = softmax_attention("diff", "diff", 4, U_DIFF, layer1, [(i_done, 4)], (IN_hi, IN_lo), H_QB, H_KB,
                                 extra=rotary_extra | {"gq": gq_b, "neg_lam": neg_lam,
                                                       "meanwhile": lambda p, part: choose(4 * p + part)})

        @block.tensor
        def _(pe):
            pe.wait_ge(*i_mask.at(2))
            pe.wait_ge(*diff["nrm"].at(4))
            for j in (0, 1, 3, 2):
                for t in range(j, QT):
                    last = nc.tensor.transpose(tile_in_bank(2, j)[:, (t - j) * P:(t - j + 1) * P],
                                               chosen[:, NOFF[t] + j * P:NOFF[t] + (j + 1) * P].bitcast(F32), ident[:])
            last.then_inc(i_maskt.sem, 1)

        @block.scalar
        def _(act):
            act.wait_ge(*i_maskt.at(1))
            for n, (c, width, _) in enumerate(GROUPS):
                nc.scalar.copy(chosen_t[:, c:c + width], bank[:, 2 + n, 0:width]).then_inc(i_copied.sem, 1)

        areas[0] = after_index
        dsa = softmax_attention("dsa", "dsa", 4, U_QA, layer1, [(i_copied, NG)], None, H_QA, None,
                                shared={"K": dsa_k, "V": dsa_v},
                                extra=rotary_extra | {"gq": gq_a, "mask": chosen, "maskT": chosen_t})

        XHEADS = 4
        areas[0] = area0
        mem_hi, mem_lo = (area(f"mem_{x}", [P, DT, M], F32R) for x in ("hi", "lo"))
        cross_k = area("cross_k", [P, DT, M], F32)
        cross_v = area("cross_v", [P, MT, D], F32)
        cross_q = area("cross_q", [P, 2, 2, S], F32)
        cross_w = area("cross_w", [P, MT, S], F32)
        cross_sq = area("cross_sq", [P, DT, M], F32)
        mem_squares = tmp_c[:, 0, 0:M]
        mem_rstd = area("mem_rstd", [P, M + MT], F32)
        cross_diag = nc.alloc_sbuf_tensor_at("cross_diag", [P, S], F32R, offset=place_used["tmp_a"])
        cross_max = area("cross_max", [P, QT], F32)
        assert areas[0] <= area0 + 2 * 4 * FA * S + 8 * S + 3000
        c_hi, c_lo, c_sq, c_sum, c_stat, c_ln, c_rstd = (
            sem("mem_" + x) for x in "hi lo sq sum stat ln rstd".split())
        k_out, k_sq, k_stat, k_ln, k_rn, k_done, v_out = (
            again("soft_" + x, n) for x, n in (("yk", DT), ("sqk", 1), ("statk", 1), ("lnk", 2), ("rnk", 1),
                                               ("kn", DT), ("v", MT * DT)))
        q_out, q_sq, q_stat, q_ln, q_rn, q_done = (
            again("soft_" + x, n * XHEADS) for x, n in (("yq", 2), ("sqq", 1), ("statq", 1), ("lnq", 1), ("rnq", 1),
                                                        ("qn", 2)))
        x_nat, x_max, x_diag, x_st, x_p, x_o, x_rc, x_od, x_hi, x_lo = (
            again("soft_" + x, n * XHEADS) for x, n in (("nat", 2), ("max", QT), ("diag", QT), ("st", MT), ("p", MT),
                                                        ("o", 3), ("rc", 1), ("od", 2), ("hi", 2), ("lo", 2)))

        @block.scalar
        def _(act):
            act.wait_ge(*m_loaded.at(16))
            act.wait_ge(*dsa["lo"].at(4))
            for c in range(DT):
                nc.scalar.activation(mem_hi[:, c], mem_in[:, c], ACT.Copy, scale=column(gains, G_MEM * DT + c)
                                     ).then_inc(c_hi.sem, 1)
            nc.scalar.activation(cross_sq[:], mem_in[:], ACT.Square).then_inc(c_sq.sem, 1)

        @block.vector
        def _(dve):
            for c in range(DT):
                dve.wait_ge(*c_hi.at(c + 1))
                nc.vector.scalar_tensor_tensor(mem_lo[:, c], mem_in[:, c], column(gains, G_MEM * DT + c),
                                               mem_hi[:, c].bitcast(F32), ALU.mult, ALU.subtract).then_inc(c_lo.sem, 1)
            dve.wait_ge(*c_sq.at(1))
            nc.vector.tensor_reduce(mem_squares, cross_sq[:].rearrange("p c m -> p m c"), AX.X, ALU.add
                                    ).then_inc(c_sum.sem, 1)

        mix_op = Operand("mix", [(G_XATTN, IN_hi, IN_lo)], None)
        project_back("mix", U_OUT2, mix_op, [(dsa["lo"], 4), (diff["lo"], 4)])

        @block.tensor
        def _(pe):
            pe.wait_ge(*c_sum.at(1))
            pe.wait_ge(*c_lo.at(DT))
            nc.tensor.matmul(bank[:, 0, 0:M], ones[:], mem_squares, start=True, stop=True)
            for m in range(MT):
                last = nc.tensor.matmul(bank[:, 0, M + m:M + m + 1], mem_squares[:, m * P:(m + 1) * P], ones[:, 0:1],
                                        start=True, stop=True)
            last.then_inc(c_stat.sem, 1)
            for c in range(DT):
                if c < 2:
                    pe.wait_ge(*mix_op.h_done.at(DT + c - 1))
                else:
                    pe.wait_ge(*k_out.at(c - 1))
                unit(pe, U_XK + c, (U_XK + c) % SLOTS, bank[:, 6 + c % 2, 0:M], mem_hi, mem_lo, width=M)

        @block.scalar
        def _(act):
            act.wait_ge(*c_stat.at(1))
            nc.scalar.activation(mem_rstd[:], bank[:, 0, 0:M + MT], ACT.Ln, bias=eps_c[:], scale=1.0 / D
                                 ).then_inc(c_ln.sem, 1)
            act.wait_ge(*c_ln.at(1))
            nc.scalar.activation(mem_rstd[:], mem_rstd[:], ACT.Exp, scale=-0.5).then_inc(c_rstd.sem, 1)

        @block.vector
        def _(dve):
            dve.wait_ge(*c_rstd.at(1))
            for c in range(DT):
                dve.wait_ge(*unit_done.at(U_XK + c + 1))
                nc.vector.tensor_tensor(cross_k[:, c], bank[:, 6 + c % 2, 0:M], mem_rstd[:, 0:M], ALU.mult
                                        ).then_inc(k_out.sem, 1)

        mix_op.stats(1)

        @block.tensor
        def _(pe):
            for c in range(DT):
                u = U_XV + c
                pe.wait_ge(*w_split.at(u + 1))
                at_least(pe, v_out, 2 * (c - 1))
                for m in range(MT):
                    out = bank[:, 2 + c % 2, m * P:(m + 1) * P]
                    n = 0
                    for t in range(DT):
                        x = slice(m * P, (m + 1) * P)
                        for a, w in ((mem_hi, w_hi), (mem_hi, w_lo), (mem_lo, w_hi)):
                            last = nc.tensor.matmul(out, a[:, t, x], w[:, u % SLOTS, t * P:(t + 1) * P], start=(n == 0),
                                                    stop=(n == 3 * DT - 1))
                            n += 1
                last.then_inc(unit_done.sem, 1)
            pe.wait_ge(*k_sq.at(1))
            for h in range(XHEADS):
                out = bank[:, 4 + h // 2, (h % 2) * M:(h % 2 + 1) * M]
                for k in range(2):
                    last = nc.tensor.matmul(out, ones[:], cross_sq[:, 2 * h + k], start=(k == 0), stop=(k == 1))
            last.then_inc(k_stat.sem, 1)

        @block.scalar
        def _(act):
            act.wait_ge(*k_out.at(DT))
            nc.scalar.activation(cross_sq[:], cross_k[:], ACT.Square).then_inc(k_sq.sem, 1)
            for c in range(DT):
                act.wait_ge(*unit_done.at(U_XV + c + 1))
                for m in range(MT):
                    nc.scalar.activation(cross_v[:, m, c * P:(c + 1) * P], bank[:, 2 + c % 2, m * P:(m + 1) * P],
                                         ACT.Copy, scale=mem_rstd[:, M + m:M + m + 1]).then_inc(v_out.sem, 1)
            act.wait_ge(*k_stat.at(1))
            for g in range(2):
                nc.scalar.activation(tmp_b[:, g], bank[:, 4 + g], ACT.Ln, bias=eps_c[:], scale=1.0 / M
                                     ).then_inc(k_ln.sem, 1)
            act.wait_ge(*k_ln.at(2))
            nc.scalar.activation(tmp_b[:], tmp_b[:], ACT.Exp, scale=-0.5).then_inc(k_rn.sem, 1)

        @block.vector
        def _(dve):
            dve.wait_ge(*k_rn.at(1))
            for c in range(DT):
                h = c // 2
                nc.vector.scalar_tensor_tensor(cross_k[:, c], cross_k[:, c], xgains[:, 2 + c % 2:3 + c % 2],
                                               tmp_b[:, h // 2, (h % 2) * M:(h % 2 + 1) * M], ALU.mult, ALU.mult
                                               ).then_inc(k_done.sem, 1)

        cross_sq_q = nc.alloc_sbuf_tensor_at("cross_sq_q", [P, 2, S], F32, offset=place_used["tmp_b"])
        cross_rn, cross_rc = tmp_a[:, 1], square[:]
        cross_out = nc.alloc_sbuf_tensor_at("cross_out", [P, 2, S], F32, offset=place_used["tmp_c"])

        @block.tensor
        def _(pe):
            def project(h, k):
                at_least(pe, q_out, 2 * (h - 1) + k + 1)
                u = U_XQ + 2 * h + k
                unit(pe, u, u % SLOTS, bank[:, 6 + k], IN_hi, IN_lo)

            def stat(h):
                pe.wait_ge(*q_sq.at(h + 1))
                at_least(pe, x_max, 4 * h)
                for k in range(2):
                    last = nc.tensor.matmul(bank[:, 1], ones[:], cross_sq_q[:, k], start=(k == 0), stop=(k == 1))
                last.then_inc(q_stat.sem, 1)

            def natural(h):
                pe.wait_ge(*q_done.at(2 * h + 2))
                at_least(pe, x_rc, h)
                for t in range(QT):
                    out = bank[:, t // 2, (t % 2) * M:(t % 2 + 1) * M]
                    for k in range(2):
                        last = nc.tensor.matmul(out, cross_q[:, h % 2, k, t * P:(t + 1) * P], cross_k[:, 2 * h + k],
                                                start=(k == 0), stop=(k == 1))
                    if t % 2 == 1:
                        last.then_inc(x_nat.sem, 1)

            def transposed(h):
                pe.wait_ge(*x_diag.at(4 * h + 4))
                at_least(pe, x_p, 2 * h)
                for m in range(MT):
                    out = bank[:, 2 + m]
                    for k in range(2):
                        nc.tensor.matmul(out, cross_k[:, 2 * h + k, m * P:(m + 1) * P], cross_q[:, h % 2, k],
                                         start=(k == 0), stop=False)
                    nc.tensor.matmul(out, ones_r[:], cross_diag[:], start=False, stop=True).then_inc(x_st.sem, 1)

            def output(h):
                pe.wait_ge(*x_p.at(2 * h + 2))
                at_least(pe, x_od, 2 * h)
                for m in range(MT):
                    last = nc.tensor.matmul(bank[:, 0], ones[:], cross_w[:, m], start=(m == 0), stop=(m == MT - 1))
                last.then_inc(x_o.sem, 1)
                for k in range(2):
                    for m in range(MT):
                        c = 2 * h + k
                        last = nc.tensor.matmul(bank[:, 4 + k], cross_v[:, m, c * P:(c + 1) * P], cross_w[:, m],
                                                start=(m == 0), stop=(m == MT - 1))
                    last.then_inc(x_o.sem, 1)

            pe.wait_ge(*mix_op.rstd_done.at(1))
            project(0, 0)
            project(0, 1)
            stat(0)
            pe.wait_ge(*k_done.at(DT))
            pe.wait_ge(*v_out.at(2 * DT))
            for h in range(XHEADS):
                natural(h)
                if h + 1 < XHEADS:
                    project(h + 1, 0)
                transposed(h)
                if h + 1 < XHEADS:
                    project(h + 1, 1)
                    stat(h + 1)
                output(h)

        @block.scalar
        def _(act):
            def squares(h):
                act.wait_ge(*q_out.at(2 * h + 2))
                if h == 0:
                    act.wait_ge(*k_done.at(DT))
                at_least(act, q_stat, h)
                nc.scalar.activation(cross_sq_q[:], cross_q[:, h % 2], ACT.Square).then_inc(q_sq.sem, 1)

            def norms(h):
                act.wait_ge(*q_stat.at(h + 1))
                at_least(act, q_done, 2 * h)
                nc.scalar.activation(cross_rn, bank[:, 1], ACT.Ln, bias=eps_c[:], scale=1.0 / M).then_inc(q_ln.sem, 1)
                act.wait_ge(*q_ln.at(h + 1))
                nc.scalar.activation(cross_rn, cross_rn, ACT.Exp, scale=-0.5).then_inc(q_rn.sem, 1)

            squares(0)
            norms(0)
            for h in range(XHEADS):
                at_least(act, x_o, 3 * h)
                for m in range(MT):
                    act.wait_ge(*x_st.at(2 * h + m + 1))
                    nc.scalar.activation(cross_w[:, m], bank[:, 2 + m], ACT.Exp).then_inc(x_p.sem, 1)
                if h + 1 < XHEADS:
                    squares(h + 1)
                    norms(h + 1)
                for k in range(2):
                    act.wait_ge(*x_od.at(2 * h + k + 1))
                    nc.scalar.copy(MID_hi[:, 2 * h + k], cross_out[:, k]).then_inc(x_hi.sem, 1)

        @block.vector
        def _(dve):
            def take(h, k):
                dve.wait_ge(*unit_done.at(U_XQ + 2 * h + k + 1))
                at_least(dve, x_st, 2 * (h - 1))
                nc.vector.tensor_tensor(cross_q[:, h % 2, k], bank[:, 6 + k], rstd[:], ALU.mult).then_inc(q_out.sem, 1)

            def finish(h):
                dve.wait_ge(*q_rn.at(h + 1))
                dve.wait_ge(*q_out.at(2 * h + 2))
                for k in range(2):
                    nc.vector.scalar_tensor_tensor(cross_q[:, h % 2, k], cross_q[:, h % 2, k], gq_x[:, k:k + 1], cross_rn,
                                                   ALU.mult, ALU.mult).then_inc(q_done.sem, 1)

            take(0, 0)
            take(0, 1)
            finish(0)
            for h in range(XHEADS):
                at_least(dve, x_st, 2 * h)
                for t in range(QT):
                    dve.wait_ge(*x_nat.at(2 * h + t // 2 + 1))
                    nc.vector.tensor_reduce(cross_max[:, t:t + 1], bank[:, t // 2, (t % 2) * M:(t % 2 + 1) * M], AX.X,
                                            ALU.max, negate=True).then_inc(x_max.sem, 1)
                    dve.wait_ge(*x_max.at(4 * h + t + 1))
                    nc.vector.tensor_scalar(cross_diag[:, t * P:(t + 1) * P], ident[:], cross_max[:, t:t + 1], None,
                                            ALU.mult).then_inc(x_diag.sem, 1)
                if h + 1 < XHEADS:
                    take(h + 1, 0)
                    take(h + 1, 1)
                    finish(h + 1)
                dve.wait_ge(*x_o.at(3 * h + 1))
                at_least(dve, x_od, 2 * h)
                nc.vector.reciprocal(cross_rc, bank[:, 0]).then_inc(x_rc.sem, 1)
                dve.wait_ge(*x_rc.at(h + 1))
                at_least(dve, x_lo, 2 * h)
                for k in range(2):
                    dve.wait_ge(*x_o.at(3 * h + k + 2))
                    nc.vector.tensor_tensor(cross_out[:, k], bank[:, 4 + k], cross_rc, ALU.mult).then_inc(x_od.sem, 1)
                for k in range(2):
                    dve.wait_ge(*x_hi.at(2 * h + k + 1))
                    nc.vector.tensor_tensor(MID_lo[:, 2 * h + k], cross_out[:, k], MID_hi[:, 2 * h + k].bitcast(F32),
                                            ALU.subtract).then_inc(x_lo.sem, 1)

        cross_op = Operand("cross", [(G_FFN2, IN_hi, IN_lo)], mix_op)
        project_back("cross", U_XO, cross_op, [(x_lo, 2 * XHEADS)])
        cross_op.stats(2)
        feed_forward("conv", U_FFN2, cross_op, None, conv=True)

        stored = sem("stored")

        @block.sync
        def _(sp):
            sp.wait_ge(*h_final.at(DT))
            sp.dma_start(OUT, hT[:]).then_inc(stored.sem, 16)
            sp.wait_ge(*stored.at(16))


def feature_tiles(a):
    a = a.reshape(a.shape[:-2] + (a.shape[-2] // P, P, a.shape[-1]))
    return np.ascontiguousarray(np.swapaxes(a, -3, -2))


def column_units(w):
    return w.reshape(DT, P, -1, P).transpose(2, 1, 0, 3).reshape(-1, P, UNIT)


def row_units(w):
    return w.reshape(-1, 2, P, 2, 4, P).transpose(3, 0, 2, 1, 4, 5).reshape(-1, P, UNIT)


def ffn_units(w_gu, w_d):
    gate_up = column_units(w_gu).reshape(2, FT, P, UNIT).transpose(1, 0, 2, 3)
    out = []
    for a, b in ((0, FA), (FA, FT)):
        out += [gate_up[a:b].reshape(-1, P, UNIT), row_units(w_d[a * P:b * P])]
    return out


def ple_units(w_gate, w_proj):
    g, p = column_units(w_gate), row_units(w_proj)
    return [p[0:1], g[0:4], p[1:2], g[4:8]]


def interleaved(*ws):
    return np.stack([column_units(w) for w in ws], 1).reshape(-1, P, UNIT)


def padded(w):
    return np.pad(w, ((0, 0), (0, P - w.shape[1])))


def weight_stream(i):
    qkv = i["sb_w_qkv"][0]
    kvf = i["shared_w_kvf"]
    w_in = i["w_in_2"][0]
    qa, ka, va, qi, ki, wi, qb, kb, vb = np.split(w_in, np.cumsum([512, 64, 64, 256, 64, 4, 512, 512])
                                                  .tolist(), axis=1)
    twice = lambda w: np.concatenate([w, w], axis=1)
    units = [interleaved(qkv[:, 0:D], qkv[:, D:2 * D], qkv[:, 2 * D:]), column_units(i["sb_w_o"][0]),
             *ffn_units(i["ffn_w_gu"][0], i["ffn_w_d"][0]), *ple_units(i["ple_w_gate"][0], i["ple_w_proj"][0]),
             column_units(padded(kvf[:, 2 * D:])),
             interleaved(i["fox_w_q"][0], kvf[:, 0:D], kvf[:, D:2 * D]), column_units(i["fox_w_o"][0]),
             *ffn_units(i["ffn_w_gu"][1], i["ffn_w_d"][1]), *ple_units(i["ple_w_gate"][1], i["ple_w_proj"][1]),
             column_units(twice(ki)), column_units(padded(np.concatenate([va, wi], axis=1))), column_units(qi),
             column_units(twice(ka)), interleaved(qb, kb, vb), column_units(qa), column_units(i["w_out_2"][0]),
             column_units(i["w_xk_2"][0]), column_units(i["w_xv_2"][0]), column_units(i["w_xq_2"][0]),
             column_units(i["w_xo_2"][0]), *ffn_units(i["w_ffn_in_2"][0], i["w_ffn_out_2"][0])]
    return np.concatenate(units)


def kernel(**inputs):
    import concourse.bacc as bacc
    from concourse.bass_utils import run_bass_kernel_spmd

    i = {k: np.asarray(v) for k, v in inputs.items()}
    per_tile = lambda g: g.reshape(-1, P).T
    gains = [i["attn_norm_g"][0], i["ffn_norm_g"][0], i["ple_norm_g"][0], i["attn_norm_g"][1], i["shared_norm_g"],
             i["ffn_norm_g"][1], i["ple_norm_g"][1], i["g_mix_2"][0], i["g_xattn_2"][0], i["g_ffn_2"][0],
             i["g_mem_2"][0]]
    heads = [i["shared_k_norm_g"], i["fox_q_norm_g"][0], i["g_qa_2"][0], i["g_ka_2"][0], i["g_qb_2"][0],
             i["g_kb_2"][0]]
    half = HD // 2
    inv_freq = (1.0 / 10000.0 ** (np.arange(half, dtype=np.float32) / np.float32(half))).astype(np.float32)
    arrays = {
        "W": weight_stream(i),
        "XT": feature_tiles(i["x"][0].T),
        "PT": feature_tiles(np.swapaxes(i["p"][:, 0], 1, 2)),
        "MEMT": feature_tiles(i["mem_2"][0].T),
        "POS": i["positions_2"].astype(np.int32),
        "INVF": np.tile(inv_freq, 4).reshape(P, 1),
        "GAINS": np.concatenate([per_tile(g) for g in gains], axis=1),
        "HGAINS": np.stack([np.tile(g, 2) for g in heads], axis=1),
        "XGAINS": np.concatenate([per_tile(i["g_xq_2"][0]), per_tile(i["g_xk_2"][0])], axis=1),
        "BF": i["shared_b_f"].reshape(HEADS, 1),
        "LAM": np.concatenate([i["lam_q1_2"], i["lam_k1_2"], i["lam_q2_2"], i["lam_k2_2"]]).T,
        "CONV": np.stack([*i["conv_w_2"][0], i["conv_b_2"][0]]).reshape(4, FT, P).transpose(2, 1, 0)
                .reshape(P, 4 * FT),
    }
    arrays = {k: np.ascontiguousarray(a) for k, a in arrays.items()}
    nc = bacc.Bacc("TRN2", target_bir_lowering=False, num_devices=1)
    args = [nc.dram_tensor(k, a.shape, mybir.dt.from_np(a.dtype), kind="ExternalInput").ap()
            for k, a in arrays.items()]
    out = nc.dram_tensor("OUT", [P, DT, S], F32, kind="ExternalOutput").ap()
    build_program(nc, *args, out)
    r = run_bass_kernel_spmd(nc, [arrays], core_ids=[0])
    got = r.results[0]["OUT"]
    return np.ascontiguousarray(got.transpose(1, 0, 2).reshape(D, S).T)[None]
```

```python
from contextlib import ExitStack

import numpy as np
import concourse.bass as bass
from concourse import mybir

F32 = mybir.dt.float32
F32R = mybir.dt.float32r
I32 = mybir.dt.int32
ALU = mybir.AluOpType
ACT = mybir.ActivationFunctionType
AX = mybir.AxisListType

P = 128
S = 512
QT = S // P
D = 1024
DT = D // P
HEADS = 16
HD = 64
PAIRS = HEADS // 2
FF = 2816
FT = FF // P
FA, FB = FT - DT, DT
M = 256
MT = M // P
EPS = 1e-6
UNIT = 1024
STAGES = 4
SLOTS = 2
LAMBDA_INIT = 0.8 - 0.6
NEG = -1.0e30

WIDTH = [S - P * j for j in range(QT)]
COL = [0, 512, 1024, 896]
CAUSAL = sum(WIDTH)
GROUPS = [(0, 512, (0,)), (512, 512, (1, 3)), (1024, 256, (2,))]
NG = len(GROUPS)

(G_ATTN0, G_FFN0, G_PLE0, G_ATTN1, G_SHARED, G_FFN1, G_PLE1, G_MIX, G_XATTN, G_FFN2, G_MEM) = range(11)
(H_FOXK, H_FOXQ, H_QA, H_KA, H_QB, H_KB) = range(6)

LAYER_UNITS = 3 * PAIRS + DT + 2 * FA + FA + 2 * FB + FB + 2 + DT
U_QKV0 = 0
U_F1 = LAYER_UNITS
U_KVQ1 = U_F1 + 1
U_IDX = U_F1 + 1 + LAYER_UNITS
U_DIFF = U_IDX + 5
U_QA = U_DIFF + 12
U_OUT2 = U_QA + 4
U_XK = U_OUT2 + DT
U_XQ0 = U_XK + DT
U_XV = U_XQ0 + 2
U_XQ = U_XV + DT
U_XO = U_XQ + DT - 2
U_FFN2 = U_XO + DT
UNITS = U_FFN2 + 3 * FT


class Signal:

    def __init__(self, semaphore, base=0):
        self.sem, self.base = semaphore, base

    def at(self, n):
        return self.sem, self.base + n


def at_least(engine, signal, n):
    if not isinstance(n, int) or n > 0:
        engine.wait_ge(*signal.at(n))


def pairs_loop(engine, body):
    body(0, 0, True)
    with engine.Fori(0, (PAIRS - 2) // 2) as i:
        body(2 * i + 1, 1, True)
        body(2 * i + 2, 0, True)
    body(PAIRS - 1, 1, False)


def build_program(nc, W, XT, PT, MEMT, POS, INVF, GAINS, HGAINS, XGAINS, BF, LAM, CONV, OUT):
    with ExitStack() as ctx:
        low = (nc.sbuf_base + 63) // 64 * 64
        place, place_used = [low], {}

        def sb(name, shape, dt):
            size = 4 * int(np.prod(shape[1:]))
            place_used[name] = place[0]
            t = nc.alloc_sbuf_tensor_at(name, shape, dt, offset=place[0])
            place[0] += (size + 63) // 64 * 64
            return t

        def sem(name):
            return Signal(ctx.enter_context(nc.semaphore(name)))

        used = {}

        def again(name, count):
            semaphore, base = used[name] if name in used else (ctx.enter_context(nc.semaphore(name)), 0)
            used[name] = semaphore, base + count
            return Signal(semaphore, base)

        hT = sb("hT", [P, DT, S], F32)
        IN_hi, IN_lo = (sb(f"IN_{x}", [P, DT, S], F32R) for x in ("hi", "lo"))
        MID_hi, MID_lo = (sb(f"MID_{x}", [P, DT, S], F32R) for x in ("hi", "lo"))
        stage = sb("stage", [P, STAGES, UNIT], F32)
        w_hi, w_lo = (sb(f"w_{x}", [P, SLOTS, UNIT], F32R) for x in ("hi", "lo"))
        gains = sb("gains", [P, 11 * DT], F32)
        hgains = sb("hgains", [P, 6], F32)
        xgains = sb("xgains", [P, 4], F32)
        forget_bias = sb("forget_bias", [HEADS, 1], F32)
        conv_s = sb("conv_s", [P, 4 * FT], F32)
        rstd = sb("rstd", [P, S], F32)
        sumsq = sb("sumsq", [P, S], F32)
        square = sb("square", [P, S], F32)
        ident = sb("ident", [P, P], F32)
        ident_r = sb("ident_r", [P, P], F32R)
        ones = sb("ones", [P, P], F32)
        ones_r = sb("ones_r", [P, P], F32R)
        head_ones = sb("head_ones", [P, P], F32)
        neg_upto = sb("neg_upto", [P, P], F32R)
        neg_ones = sb("neg_ones", [P, P], F32R)
        before = sb("before", [P, P], F32)
        mask_kq_strict = sb("mask_kq_strict", [P, P], F32R)
        mask_kq = sb("mask_kq", [P, P], F32R)
        mask_qk = sb("mask_qk", [P, P], F32R)
        one_c = sb("one_c", [P, 1], F32)
        eps_c = sb("eps_c", [P, 1], F32)
        small = sb("small", [P, 24], F32)
        perm = sb("perm", [P, P], F32)
        tmp_a = sb("tmp_a", [P, 2, S], F32)
        mask_f, neg_ones_f = tmp_a[:, 0, 0:P], tmp_a[:, 1, 0:P]
        tmp_b = sb("tmp_b", [P, 2, S], F32)
        tmp_c = sb("tmp_c", [P, 2, S], F32)
        ple_in = sb("ple_in", [P, 2, S], F32)
        ple_hi, ple_lo = (sb(f"ple_{x}", [P, 2, S], F32R) for x in ("hi", "lo"))
        area0 = place[0]
        areas = [area0]

        def area(name, shape, dt):
            size = 4 * int(np.prod(shape[1:]))
            t = nc.alloc_sbuf_tensor_at(name, shape, dt, offset=areas[0])
            areas[0] += (size + 63) // 64 * 64
            return t

        bank = ctx.enter_context(nc.psum_tensor("bank", [P, 8, S], F32))

        w_loaded = [sem(f"w_loaded{k}") for k in range(STAGES)]
        w_hi_done = sem("w_hi_done")
        w_split = sem("w_split")
        unit_done = sem("unit_done")

        pool_turns, act_turns = sem("pool_turns"), sem("act_turns")

        block = ctx.enter_context(nc.Block())

        small_loaded, gains_loaded, p_loaded = sem("small_loaded"), sem("gains_loaded"), sem("p_loaded")
        x_loaded = [sem("x_loaded0"), sem("x_loaded1")]
        consts_made, masks_filled, consts_cast = sem("consts_made"), sem("masks_filled"), sem("consts_cast")

        @block.sync
        def _(sp):
            sp.dma_start(gains[:], GAINS).then_inc(gains_loaded.sem, 16)
            for g in range(2):
                x = slice(g * DT // 2, (g + 1) * DT // 2)
                sp.dma_start(hT[:, x], XT[:, x]).then_inc(x_loaded[g].sem, 16)
                for u in range(2 * g, 2 * g + 2):
                    sp.dma_start(stage[:, u], W[u]).then_inc(w_loaded[u].sem, 16)
            sp.dma_start(hgains[:], HGAINS).then_inc(small_loaded.sem, 16)
            sp.dma_start(xgains[:], XGAINS).then_inc(small_loaded.sem, 16)
            sp.dma_start(forget_bias[:], BF).then_inc(small_loaded.sem, 16)
            sp.dma_start(conv_s[:], CONV).then_inc(small_loaded.sem, 16)
            with sp.Fori(1, UNITS // STAGES) as i:
                for k in range(STAGES):
                    sp.wait_ge(*w_split.at(STAGES * (i - 1) + k + 1))
                    sp.dma_start(stage[:, k], W[bass.ds(STAGES * i + k, 1)].rearrange("a p n -> (a p) n")
                                 ).then_inc(w_loaded[k].sem, 16)

        @block.gpsimd
        def _(pool):
            nc.gpsimd.memset(ones[:], 1.0).then_inc(masks_filled.sem, 1)
            nc.gpsimd.memset(neg_ones_f, -1.0).then_inc(masks_filled.sem, 1)
            nc.gpsimd.memset(mask_f, 0.0).then_inc(masks_filled.sem, 1)
            nc.gpsimd.memset(head_ones[:], 0.0).then_inc(masks_filled.sem, 1)
            nc.gpsimd.memset(one_c[:], 1.0).then_inc(masks_filled.sem, 1)
            nc.gpsimd.memset(eps_c[:], EPS).then_inc(masks_filled.sem, 1)
            pool.wait_ge(*masks_filled.at(6))
            nc.gpsimd.affine_select(ident[:], ones[:], [[-1, P]], ALU.is_equal, 0.0, base=0,
                                    channel_multiplier=1).then_inc(consts_made.sem, 1)
            nc.gpsimd.affine_select(square[:, 3 * P:], neg_ones_f, [[-1, P]], ALU.is_ge, 0.0, base=0,
                                    channel_multiplier=1).then_inc(consts_made.sem, 1)
            nc.gpsimd.affine_select(before[:], ones[:], [[1, P]], ALU.is_gt, 0.0, base=0,
                                    channel_multiplier=-1).then_inc(consts_made.sem, 1)
            pool.wait_ge(*consts_made.at(3))
            nc.gpsimd.memset(head_ones[0:HD, 0:HD], 1.0).then_inc(consts_made.sem, 1)
            nc.gpsimd.memset(head_ones[HD:P, HD:P], 1.0).then_inc(consts_made.sem, 1)
            pool.wait_ge(*consts_made.at(5))
            nc.gpsimd.affine_select(square[:, 0:P], mask_f, [[1, P]], ALU.is_ge, NEG, base=0,
                                    channel_multiplier=-1).then_inc(consts_made.sem, 1)
            nc.gpsimd.affine_select(square[:, P:2 * P], mask_f, [[1, P]], ALU.is_gt, NEG, base=0,
                                    channel_multiplier=-1).then_inc(consts_made.sem, 1)
            nc.gpsimd.affine_select(square[:, 2 * P:3 * P], mask_f, [[-1, P]], ALU.is_ge, NEG, base=0,
                                    channel_multiplier=1).then_inc(consts_made.sem, 1)
            for m, (source, shift) in enumerate(((neg_ones_f, 32), (ones, 0), (neg_ones_f, 96), (ones, 64))):
                nc.gpsimd.affine_select(perm[:, 32 * m:32 * m + 32], source[:, 0:32], [[-1, 32]], ALU.is_equal,
                                        0.0, base=-shift, channel_multiplier=1).then_inc(consts_made.sem, 1)
            def split(u, k):
                slot = k % SLOTS
                at_least(pool, unit_done, u - SLOTS + 1)
                pool.wait_ge(*w_loaded[k].at(u // STAGES * 16 + 16 if isinstance(u, int) else 4 * u - 4 * k + 16))
                pool.sem_inc(pool_turns.sem, 1)
                nc.gpsimd.tensor_scalar(w_hi[:, slot], stage[:, k], 1.0, 1.0, ALU.mult, ALU.mult
                                        ).then_inc(w_hi_done.sem, 1)
                pool.wait_ge(*w_hi_done.at(u + 1))
                nc.gpsimd.tensor_tensor(w_lo[:, slot], stage[:, k], w_hi[:, slot].bitcast(F32),
                                        ALU.subtract).then_inc(w_split.sem, 1)

            for k in range(STAGES):
                split(k, k)
            with pool.Fori(1, UNITS // STAGES) as i:
                for k in range(STAGES):
                    split(STAGES * i + k, k)

        p_hi_done, p_lo_done = sem("p_hi_done"), sem("p_lo_done")

        @block.scalar
        def _(act):
            act.wait_ge(*consts_made.at(8))
            nc.scalar.copy(ident_r[:], ident[:]).then_inc(consts_cast.sem, 1)
            nc.scalar.copy(ones_r[:], ones[:]).then_inc(consts_cast.sem, 1)
            nc.scalar.copy(mask_kq[:], square[:, 0:P]).then_inc(consts_cast.sem, 1)
            nc.scalar.copy(mask_kq_strict[:], square[:, P:2 * P]).then_inc(consts_cast.sem, 1)
            nc.scalar.copy(mask_qk[:], square[:, 2 * P:3 * P]).then_inc(consts_cast.sem, 1)
            nc.scalar.copy(neg_upto[:], square[:, 3 * P:]).then_inc(consts_cast.sem, 1)
            nc.scalar.copy(neg_ones[:], neg_ones_f).then_inc(consts_cast.sem, 1)

        def tile(t, c):
            return t[:, c] if isinstance(c, int) else t[:, bass.ds(c, 1)].rearrange("p a s -> p (a s)")

        def column(t, c):
            return t[:, c:c + 1] if isinstance(c, int) else t[:, bass.ds(c, 1)]

        class Operand:

            def __init__(self, name, targets, previous=None):
                self.targets = targets
                self.previous = previous
                n = DT * len(targets)
                self.h_done = again("h_done", DT)
                self.hi_done = again("operand_hi", n)
                self.lo_done = again("operand_lo", n)
                self.sq_done = again("h_squared", DT)
                self.ss_done = again("squares_added", DT + 1)
                self.ss_ready = again("squares_summed", 1)
                self.ln_done = again("rstd_ln", 1)
                self.rstd_done = again("rstd_ready", 1)

            def on_act(self, act, c):
                act.wait_ge(*self.h_done.at(c + 1))
                act.sem_inc(act_turns.sem, 1)
                for g, hi, lo in self.targets:
                    nc.scalar.activation(tile(hi, c), tile(hT, c), ACT.Copy, scale=column(gains, g * DT + c)
                                         ).then_inc(self.hi_done.sem, 1)
                act.wait_ge(*self.ss_done.at(c + 1))
                act.sem_inc(act_turns.sem, 1)
                nc.scalar.activation(square[:], tile(hT, c), ACT.Square).then_inc(self.sq_done.sem, 1)

            def on_dve_first(self, dve):
                if self.previous is not None:
                    dve.wait_ge(*self.previous.ss_ready.at(1))
                nc.vector.memset(sumsq[:], 0.0).then_inc(self.ss_done.sem, 1)

            def on_dve(self, dve, c):
                n = len(self.targets)
                for k, (g, hi, lo) in enumerate(self.targets):
                    dve.wait_ge(*self.hi_done.at(n * c + k + 1))
                    nc.vector.scalar_tensor_tensor(tile(lo, c), tile(hT, c), column(gains, g * DT + c),
                                                   tile(hi, c).bitcast(F32), ALU.mult, ALU.subtract
                                                   ).then_inc(self.lo_done.sem, 1)
                dve.wait_ge(*self.sq_done.at(c + 1))
                dve.wait_ge(*self.ss_done.at(c + 1))
                nc.vector.tensor_tensor(sumsq[:], sumsq[:], square[:], ALU.add).then_inc(self.ss_done.sem, 1)

            def tile_ready(self, pe, t):
                pe.wait_ge(*self.lo_done.at(len(self.targets) * (t + 1)))

            def add_up(self, pe):
                pe.wait_ge(*self.ss_done.at(DT + 1))
                nc.tensor.matmul(bank[:, self.bank], ones[:], sumsq[:], start=True, stop=True
                                 ).then_inc(self.ss_ready.sem, 1)

            def stats(self, b):
                self.bank = b

                @block.scalar
                def _(act):
                    act.wait_ge(*self.ss_ready.at(1))
                    nc.scalar.activation(rstd[:], bank[:, b], ACT.Ln, bias=eps_c[:], scale=1.0 / D
                                         ).then_inc(self.ln_done.sem, 1)
                    act.wait_ge(*self.ln_done.at(1))
                    nc.scalar.activation(rstd[:], rstd[:], ACT.Exp, scale=-0.5).then_inc(self.rstd_done.sem, 1)

        def unit(pe, u, slot, out, hi, lo, width=S, ready=None, order=range(DT)):
            pe.wait_ge(*w_split.at(u + 1))
            n = 0
            for t in order:
                if ready is not None:
                    ready(pe, t)
                a, b = w_hi[:, slot, t * P:(t + 1) * P], w_lo[:, slot, t * P:(t + 1) * P]
                for w, x in ((a, hi), (a, lo), (b, hi)):
                    last = nc.tensor.matmul(out, w, x[:, t, 0:width], start=(n == 0), stop=(n == 3 * DT - 1))
                    n += 1
            last.then_inc(unit_done.sem, 1)

        x_op = Operand("x", [(G_ATTN0, IN_hi, IN_lo)])

        @block.scalar
        def _(act):
            act.wait_ge(*gains_loaded.at(16))
            for c in range(DT):
                x_op.on_act(act, c)

        @block.vector
        def _(dve):
            dve.wait_ge(*consts_cast.at(7))
            x_op.on_dve_first(dve)
            dve.wait_ge(*gains_loaded.at(16))
            for g in range(2):
                dve.wait_ge(*x_loaded[g].at(16))
                dve.engine_nop().then_inc(x_op.h_done.sem, DT // 2)
                for c in range(g * DT // 2, (g + 1) * DT // 2):
                    x_op.on_dve(dve, c)

        x_op.stats(0)


        def rows(h):
            return slice(HD * h, HD * h + HD)

        def high_q(act, y, QA, signal, n):
            for h in (0, 1, 2, 3):
                src, dst = rows(h % 2), rows(h % 2 if h < 2 else 1 - h % 2)
                nc.scalar.copy(QA[dst, h % 2], y[src]).then_inc(signal.sem, 1)

        def low_q(dve, y, QA, QB, high, n, signal):
            for h in range(2):
                dve.wait_ge(*high.at(n + h + 1))
                for dst in (rows(h), rows(1 - h)):
                    nc.vector.tensor_tensor(QB[dst, h], y[rows(h)], QA[rows(h), h].bitcast(F32), ALU.subtract
                                            ).then_inc(signal.sem, 1)

        def high_k(act, y, KS, signal):
            for h in range(2):
                nc.scalar.copy(KS[rows(h), h], y[rows(h)]).then_inc(signal.sem, 1)

        def low_k(dve, y, KS, high, n, signal):
            for h in range(2):
                dve.wait_ge(*high.at(n + h + 1))
                nc.vector.tensor_tensor(KS[rows(1 - h), h], y[rows(h)], KS[rows(h), h].bitcast(F32), ALU.subtract
                                        ).then_inc(signal.sem, 1)

        areas[0] = area0
        QA, QB, KS = (area(f"sb_{x}", [P, 2, S], F32R) for x in ("q_high", "q_low", "k"))
        YQ, YK = tmp_a[:, 0], tmp_a[:, 1]
        VN_hi, VN_lo = (area(f"sb_v_{x}", [P, 2, QT, P], F32R) for x in ("hi", "lo"))
        VT = area("sb_vt", [P, S], F32)
        AB = area("sb_ab", [P, 2, CAUSAL], F32)
        SP_hi, SP_lo = (area(f"softplus_{x}", [P, 2, CAUSAL], F32R) for x in ("hi", "lo"))
        sb_w_hi, sb_w_lo = sem("sb_w_hi"), sem("sb_w_lo")
        sb_sp_hi = sem("sb_sp_hi")
        sb_taken = sem("sb_taken")
        sb_high, sb_low = sem("sb_high"), sem("sb_low")
        sb_vt_ready = sem("sb_vt_ready")
        sb_v_hi, sb_v_ready = sem("sb_v_hi"), sem("sb_v_ready")
        sb_z = sem("sb_z")
        sb_abs = sem("sb_abs")
        sb_exp = sem("sb_exp")
        sb_ln = sem("sb_ln")
        sb_raw = sem("sb_raw")
        sb_sp = sem("sb_sp")
        sb_sum = sem("sb_sum")
        sb_w = sem("sb_w")
        sb_o = sem("sb_o")
        sb_o_hi = sem("sb_o_hi")
        sb_o_lo = sem("sb_o_lo")
        PER = 2 * NG

        def tile_in_bank(first, j):
            return bank[:, first + (0, 1, 2, 1)[j], (0, 0, 0, WIDTH[1])[j]:][:, 0:WIDTH[j]]

        def z_bank(h, j):
            return tile_in_bank(3 * h, j)

        @block.tensor
        def _(pe):
            def project(p, b, n, u, ready=None):
                at_least(pe, sb_taken, 3 * p + (0, -1, 1)[n])
                if n == 1:
                    at_least(pe, sb_v_ready, p)
                unit(pe, u, (U_QKV0 + b + n) % SLOTS, bank[:, 6 + n % 2], IN_hi, IN_lo,
                     ready=ready)

            def turn_v(p, b):
                pe.wait_ge(*sb_taken.at(3 * p + 3))
                for t in range(QT):
                    last = nc.tensor.transpose(bank[:, 7, t * P:(t + 1) * P], VT[:, t * P:(t + 1) * P], ident[:])
                last.then_inc(sb_vt_ready.sem, 1)

            def scores(p, b, h):
                at_least(pe, sb_o_lo, 2 * (p - 1) + h + 1)
                pe.wait_ge(*sb_high.at(6 * p + 6))
                pe.wait_ge(*sb_low.at(6 * p + 6))
                for _, _, tiles in GROUPS:
                    for j in tiles:
                        for q in (QA, QB):
                            last = nc.tensor.matmul(z_bank(h, j), KS[:, h, j * P:(j + 1) * P], q[:, h, j * P:S],
                                                    start=(j != 3 and q is QA), stop=False, skip_group_check=True)
                    last.then_inc(sb_z.sem, 1)

            def sums(p, b, h):
                pe.wait_ge(*sb_sp.at(PER * p + NG * h + NG))
                for _, _, tiles in GROUPS:
                    for j in tiles:
                        for k in range(j, QT):
                            for sp in (SP_hi, SP_lo):
                                nc.tensor.matmul(z_bank(h, j)[:, (k - j) * P:], (neg_upto if k == j else neg_ones)[:],
                                                 sp[:, h, COL[k]:COL[k] + WIDTH[k]], start=False, stop=False,
                                                 skip_group_check=True)
                        last = nc.tensor.matmul(z_bank(h, j)[:, 0:P], ident_r[:], mask_kq_strict[:], start=False,
                                                stop=True, skip_group_check=True)
                    last.then_inc(sb_sum.sem, 1)

            def output(p, b, h):
                pe.wait_ge(*sb_v_ready.at(p + 1))
                pe.wait_ge(*sb_w_lo.at(PER * p + NG * h + NG))
                for j in range(QT):
                    x = slice(COL[j], COL[j] + WIDTH[j])
                    for n, (v, w) in enumerate(((VN_hi, SP_hi), (VN_lo, SP_hi), (VN_hi, SP_lo))):
                        last = nc.tensor.matmul(bank[:, 3 * h, j * P:S], v[:, b, j], w[:, h, x],
                                                start=(j == 0 and n == 0), stop=(j == QT - 1 and n == 2))
                last.then_inc(sb_o.sem, 1)

            pe.wait_ge(*consts_cast.at(7))
            project(0, 0, 0, U_QKV0, x_op.tile_ready)
            pe.wait_ge(*consts_made.at(12))
            x_op.add_up(pe)
            project(0, 0, 1, U_QKV0 + 1)
            project(0, 0, 2, U_QKV0 + 2)
            turn_v(0, 0)

            def pair(p, b, more):
                u = U_QKV0 + 3 * p + 3
                c = (b + 1) % 2
                scores(p, b, 0)
                scores(p, b, 1)
                if more:
                    project(p + 1, c, 0, u)
                sums(p, b, 0)
                if more:
                    project(p + 1, c, 1, u + 1)
                sums(p, b, 1)
                if more:
                    project(p + 1, c, 2, u + 2)
                output(p, b, 0)
                if more:
                    turn_v(p + 1, c)
                output(p, b, 1)

            pairs_loop(pe, pair)

        @block.scalar
        def _(act):
            def copy_v(p, b):
                pe_done = sb_vt_ready
                act.wait_ge(*pe_done.at(p + 1))
                at_least(act, sb_o, 2 * (p - 1))
                nc.scalar.copy(VN_hi[:, b], bank[:, 7].rearrange("p (t c) -> p t c", t=QT)).then_inc(sb_v_hi.sem, 1)

            def soften(p, h):
                at_least(act, sb_o, 2 * (p - 1) + h + 1)
                for n, (c, width, _) in enumerate(GROUPS):
                    k = PER * p + NG * h + n
                    x = AB[:, h, c:c + width]
                    act.wait_ge(*sb_z.at(k + 1))
                    nc.scalar.activation(x, bank[:, 3 * h + n, 0:width], ACT.Abs).then_inc(sb_abs.sem, 1)
                    act.wait_ge(*sb_abs.at(k + 1))
                    nc.scalar.activation(x, x, ACT.Exp, scale=-1.0).then_inc(sb_exp.sem, 1)
                    act.wait_ge(*sb_exp.at(k + 1))
                    nc.scalar.activation(x, x, ACT.Ln, bias=one_c[:]).then_inc(sb_ln.sem, 1)

            def round_softplus(p, h):
                at_least(act, sb_o, 2 * (p - 1) + h + 1)
                for n, (c, width, _) in enumerate(GROUPS):
                    act.wait_ge(*sb_raw.at(2 * (PER * p + NG * h + n) + 2))
                    nc.scalar.copy(SP_hi[:, h, c:c + width], AB[:, h, c:c + width]).then_inc(sb_sp_hi.sem, 1)

            def weigh(p, h):
                act.wait_ge(*sb_sum.at(PER * p + NG * h + NG))
                for n, (c, width, _) in enumerate(GROUPS):
                    nc.scalar.activation(AB[:, h, c:c + width], bank[:, 3 * h + n, 0:width], ACT.Exp
                                         ).then_inc(sb_w.sem, 1)
                for n, (c, width, _) in enumerate(GROUPS):
                    act.wait_ge(*sb_w.at(PER * p + NG * h + n + 1))
                    nc.scalar.copy(SP_hi[:, h, c:c + width], AB[:, h, c:c + width]).then_inc(sb_w_hi.sem, 1)

            act.preload_act_table_set("natural_log_exp_and_others")
            act.wait_ge(*sb_taken.at(1))
            high_q(act, YQ, QA, sb_high, 0)
            act.wait_ge(*sb_taken.at(2))
            high_k(act, YK, KS, sb_high)
            copy_v(0, 0)

            def pair(p, b, more):
                soften(p, 0)
                round_softplus(p, 0)
                soften(p, 1)
                round_softplus(p, 1)
                if more:
                    act.wait_ge(*sb_taken.at(3 * p + 4))
                    high_q(act, YQ, QA, sb_high, 6 * p + 6)
                weigh(p, 0)
                if more:
                    act.wait_ge(*sb_taken.at(3 * p + 5))
                    high_k(act, YK, KS, sb_high)
                weigh(p, 1)
                if more:
                    copy_v(p + 1, (b + 1) % 2)
                for h in range(2):
                    act.wait_ge(*sb_o.at(2 * p + h + 1))
                    act.sem_inc(act_turns.sem, 1)
                    nc.scalar.copy(tile(MID_hi, p)[rows(h)], bank[rows(h), 3 * h]).then_inc(sb_o_hi.sem, 1)

            pairs_loop(act, pair)

        @block.vector
        def _(dve):
            def take(p, b, n):
                dve.wait_ge(*unit_done.at(U_QKV0 + 3 * p + n + 1))
                if n == 0:
                    at_least(dve, sb_low, 6 * p)
                    nc.vector.scalar_tensor_tensor(YQ, bank[:, 6], HD ** -0.5, rstd[:], ALU.mult, ALU.mult
                                                   ).then_inc(sb_taken.sem, 1)
                    low_q(dve, YQ, QA, QB, sb_high, 6 * p, sb_low)
                elif n == 1:
                    nc.vector.tensor_tensor(YK, bank[:, 7], rstd[:], ALU.mult).then_inc(sb_taken.sem, 1)
                    low_k(dve, YK, KS, sb_high, 6 * p + 4, sb_low)
                else:
                    at_least(dve, sb_vt_ready, p)
                    nc.vector.tensor_tensor(VT[:], bank[:, 6], rstd[:], ALU.mult).then_inc(sb_taken.sem, 1)

            def softplus(p, h):
                for n, (c, width, tiles) in enumerate(GROUPS):
                    k = PER * p + NG * h + n
                    x = AB[:, h, c:c + width]
                    dve.wait_ge(*sb_ln.at(k + 1))
                    nc.vector.scalar_tensor_tensor(x, bank[:, 3 * h + n, 0:width], 0.0, x, ALU.max, ALU.add
                                                   ).then_inc(sb_raw.sem, 1)
                    dve.wait_ge(*sb_raw.at(2 * k + 1))
                    for j in tiles:
                        x = AB[:, h, COL[j]:COL[j] + P]
                        last = nc.vector.tensor_tensor(x, x, before[:], ALU.mult)
                    last.then_inc(sb_raw.sem, 1)
                for n, (c, width, _) in enumerate(GROUPS):
                    x = slice(c, c + width)
                    dve.wait_ge(*sb_sp_hi.at(PER * p + NG * h + n + 1))
                    nc.vector.tensor_tensor(SP_lo[:, h, x], AB[:, h, x], SP_hi[:, h, x].bitcast(F32), ALU.subtract
                                            ).then_inc(sb_sp.sem, 1)

            def split_weights(p, h):
                for n, (c, width, _) in enumerate(GROUPS):
                    x = slice(c, c + width)
                    dve.wait_ge(*sb_w_hi.at(PER * p + NG * h + n + 1))
                    nc.vector.tensor_tensor(SP_lo[:, h, x], AB[:, h, x], SP_hi[:, h, x].bitcast(F32), ALU.subtract
                                            ).then_inc(sb_w_lo.sem, 1)

            def split_v(p, b):
                dve.wait_ge(*sb_v_hi.at(p + 1))
                nc.vector.tensor_tensor(VN_lo[:, b].rearrange("p t c -> p (t c)"), bank[:, 7],
                                        VN_hi[:, b].rearrange("p t c -> p (t c)").bitcast(F32), ALU.subtract
                                        ).then_inc(sb_v_ready.sem, 1)

            dve.wait_ge(*x_op.rstd_done.at(1))
            for n in range(3):
                take(0, 0, n)
            split_v(0, 0)

            def pair(p, b, more):
                c = (b + 1) % 2
                softplus(p, 0)
                softplus(p, 1)
                if more:
                    take(p + 1, c, 0)
                split_weights(p, 0)
                if more:
                    take(p + 1, c, 1)
                split_weights(p, 1)
                if more:
                    take(p + 1, c, 2)
                    split_v(p + 1, c)
                for h in range(2):
                    dve.wait_ge(*sb_o_hi.at(2 * p + h + 1))
                    nc.vector.tensor_tensor(tile(MID_lo, p)[rows(h)], bank[rows(h), 3 * h],
                                            tile(MID_hi, p)[rows(h)].bitcast(F32), ALU.subtract
                                            ).then_inc(sb_o_lo.sem, 1)

            pairs_loop(dve, pair)

        def tile_by_tile(name, u0, hi, lo, ready, op, banks=(6, 7), before=(),
                         order=range(DT)):
            done = h_final if op is None else op.h_done

            @block.tensor
            def _(pe):
                for s, n in before:
                    pe.wait_ge(*s.at(n))

                def one(c, b, first=None):
                    at_least(pe, done, c - 1)
                    unit(pe, u0 + c, (u0 + b) % 2, bank[:, banks[b]], hi, lo, ready=first,
                         order=order)

                one(0, 0, ready)
                one(1, 1)
                with pe.Fori(1, DT // 2) as i:
                    one(2 * i, 0)
                    one(2 * i + 1, 1)

            if op is not None:
                @block.scalar
                def _(act):
                    with act.Fori(0, DT) as c:
                        op.on_act(act, c)

            @block.vector
            def _(dve):
                if op is not None:
                    op.on_dve_first(dve)

                def one(c, b):
                    dve.wait_ge(*unit_done.at(u0 + c + 1))
                    nc.vector.tensor_tensor(tile(hT, c), tile(hT, c), bank[:, banks[b]], ALU.add
                                            ).then_inc(done.sem, 1)
                    if op is not None:
                        op.on_dve(dve, c)

                with dve.Fori(0, DT // 2) as i:
                    one(2 * i, 0)
                    one(2 * i + 1, 1)

        def feed_forward(name, u0, op_in, op, conv=False, meanwhile=None):
            areas[0] = area0
            A_hi = area(name + "_hi", [P, FA, S], F32R)
            A_lo = area(name + "_lo", [P, FA, S], F32R)
            gate_done = again("ff_gate", FT)
            act_done = again("ff_act", FT)
            up_done = again("ff_up", FT)
            prod_done = again("ff_product", FT)
            hi_done = again("ff_hi", FT)
            lo_done = again("ff_lo", FT)
            sums_done = again("ff_sums", DT)
            added = again("ff_added", DT)
            if conv:
                pad_done, taps = sem("conv_pad"), sem("conv_taps")
                padded = nc.alloc_sbuf_tensor_at(name + "_padded", [P, 2, S + 2], F32, offset=place_used["ple_in"])
            BANKS = ((2, 3, 4, 5), (6, 7, 0, 1))
            DOWN_BANKS = (6, 7, 0, 1, 2, 3, 4, 5)

            def gate_up(half, f0, nf, u1):
                gate_bank, up_bank = BANKS[half][0::2], BANKS[half][1::2]

                @block.tensor
                def _(pe):
                    def one(f, b, first):
                        u = u1 + 2 * (f - f0)
                        if not first:
                            at_least(pe, gate_done, f - 1)
                            at_least(pe, up_done, f - 1)
                        start = first and b == 0 and half == 0
                        unit(pe, u, u1 % 2, bank[:, gate_bank[b]], IN_hi, IN_lo,
                             ready=op_in.tile_ready if start else None)
                        if start:
                            op_in.add_up(pe)
                        unit(pe, u + 1, (u1 + 1) % 2, bank[:, up_bank[b]], IN_hi, IN_lo)

                    if half == 1:
                        pe.wait_ge(*added.at(4))
                    one(f0, 0, True)
                    one(f0 + 1, 1, True)
                    with pe.Fori(1, nf // 2) as i:
                        one(2 * i + f0, 0, False)
                        one(2 * i + f0 + 1, 1, False)

                @block.scalar
                def _(act):
                    def one(f, b):
                        act.wait_ge(*gate_done.at(f + 1))
                        at_least(act, up_done, f - 1)
                        if conv:
                            act.wait_ge(*taps.at(3 * f + 3))
                        nc.scalar.activation(tmp_b[:, b], tmp_a[:, b], ACT.Gelu_apprx_tanh if conv else ACT.Silu
                                             ).then_inc(act_done.sem, 1)
                        act.wait_ge(*prod_done.at(f + 1))
                        act.sem_inc(act_turns.sem, 1)
                        nc.scalar.copy(tile(A_hi, f - f0), tmp_c[:, b]).then_inc(hi_done.sem, 1)

                    if half == 1:
                        act.wait_ge(*sums_done.at(DT))
                    one(f0, 0)
                    one(f0 + 1, 1)
                    with act.Fori(1, nf // 2) as i:
                        one(2 * i + f0, 0)
                        one(2 * i + f0 + 1, 1)

                @block.vector
                def _(dve):
                    def one(f, b):
                        u = u1 + 2 * (f - f0)
                        dve.wait_ge(*unit_done.at(u + 1))
                        at_least(dve, act_done, f - 1)
                        if conv:
                            nc.vector.tensor_tensor(padded[:, b, 2:S + 2], bank[:, gate_bank[b]], rstd[:], ALU.mult
                                                    ).then_inc(gate_done.sem, 1)
                            dve.wait_ge(*gate_done.at(f + 1))
                            nc.vector.tensor_scalar(tmp_a[:, b], padded[:, b, 0:S], column(conv_s, 4 * f),
                                                    column(conv_s, 4 * f + 3), ALU.mult, ALU.add).then_inc(taps.sem, 1)
                            for k in (1, 2):
                                dve.wait_ge(*taps.at(3 * f + k))
                                nc.vector.scalar_tensor_tensor(tmp_a[:, b], padded[:, b, k:S + k],
                                                               column(conv_s, 4 * f + k), tmp_a[:, b],
                                                               ALU.mult, ALU.add).then_inc(taps.sem, 1)
                        else:
                            nc.vector.tensor_tensor(tmp_a[:, b], bank[:, gate_bank[b]], rstd[:], ALU.mult
                                                    ).then_inc(gate_done.sem, 1)
                        dve.wait_ge(*unit_done.at(u + 2))
                        dve.wait_ge(*act_done.at(f + 1))
                        at_least(dve, hi_done, f - 1)
                        at_least(dve, lo_done, f - 1)
                        nc.vector.tensor_tensor(tmp_c[:, b], bank[:, up_bank[b]], tmp_b[:, b], ALU.mult
                                                ).then_inc(up_done.sem, 1)
                        dve.wait_ge(*up_done.at(f + 1))
                        nc.vector.tensor_tensor(tmp_c[:, b], tmp_c[:, b], rstd[:], ALU.mult).then_inc(prod_done.sem, 1)
                        dve.wait_ge(*hi_done.at(f + 1))
                        nc.vector.tensor_tensor(tile(A_lo, f - f0), tmp_c[:, b], tile(A_hi, f - f0).bitcast(F32),
                                                ALU.subtract).then_inc(lo_done.sem, 1)

                    if half == 0:
                        dve.wait_ge(*op_in.rstd_done.at(1))
                    if conv and half == 0:
                        nc.vector.memset(padded[:, :, 0:2], 0.0).then_inc(pad_done.sem, 1)
                        dve.wait_ge(*pad_done.at(1))
                    one(f0, 0)
                    one(f0 + 1, 1)
                    with dve.Fori(1, nf // 2) as i:
                        one(2 * i + f0, 0)
                        one(2 * i + f0 + 1, 1)

            def down():
                u1, nf = u0 + 2 * FA, FA

                @block.tensor
                def _(pe):
                    for g in range(2):
                        if g == 1:
                            pe.wait_ge(*up_done.at(FA))
                        for kp in range(nf // 2):
                            u = u1 + g * (nf // 2) + kp
                            pe.wait_ge(*w_split.at(u + 1))
                            pe.wait_ge(*lo_done.at(2 * kp + 2))
                            for n in range(4):
                                b = DOWN_BANKS[4 * g + n]
                                for k in range(2):
                                    x = slice((4 * k + n) * P, (4 * k + n + 1) * P)
                                    wh, wl = w_hi[:, u % SLOTS, x], w_lo[:, u % SLOTS, x]
                                    f = 2 * kp + k
                                    for i, (w, a) in enumerate(((wh, A_hi), (wh, A_lo), (wl, A_hi))):
                                        last = nc.tensor.matmul(bank[:, b], w, a[:, f],
                                                                start=(f == 0 and i == 0), stop=(f == nf - 1 and i == 2),
                                                                skip_group_check=True)
                                if kp == nf // 2 - 1 and n < 3:
                                    last.then_inc(sums_done.sem, 1)
                            if kp == nf // 2 - 1:
                                last.then_inc(sums_done.sem, 1)
                                pe.wait_ge(*sums_done.at(4 * g + 4))
                                pe.nop().then_inc(unit_done.sem, 1)
                            else:
                                last.then_inc(unit_done.sem, 1)

                @block.vector
                def _(dve):
                    for c in range(DT):
                        dve.wait_ge(*sums_done.at(c + 1))
                        nc.vector.tensor_tensor(hT[:, c], hT[:, c], bank[:, DOWN_BANKS[c]], ALU.add
                                                ).then_inc(added.sem, 1)

            gate_up(0, 0, FA, u0)
            if meanwhile is not None:
                meanwhile([(hi_done, FA), (lo_done, FA)])
            down()
            gate_up(1, FA, FB, u0 + 3 * FA)
            tile_by_tile(name, u0 + 3 * FA + 2 * FB, A_hi, A_lo, lambda pe, t: pe.wait_ge(*lo_done.at(FA + t + 1)), op,
                         banks=(2, 3), before=[(added, DT)])

        def layer_embedding(name, u0, i, op_in, op):
            gate_done = again("ple_gate", DT)
            sig_done = again("ple_sigmoid", DT)
            prod_done = again("ple_product", DT)
            P_BANKS = (4, 5, 0, 1, 2, 3, 4, 5)

            @block.tensor
            def _(pe):
                pe.wait_ge(*p_lo_done.at(i + 1))
                for g in range(2):
                    u = u0 + 5 * g
                    at_least(pe, prod_done, 2 * g)
                    pe.wait_ge(*w_split.at(u + 1))
                    for n in range(4):
                        for k in range(2):
                            x = slice((4 * k + n) * P, (4 * k + n + 1) * P)
                            wh, wl = w_hi[:, u % SLOTS, x], w_lo[:, u % SLOTS, x]
                            for j, (w, a) in enumerate(((wh, ple_hi), (wh, ple_lo), (wl, ple_hi))):
                                last = nc.tensor.matmul(bank[:, P_BANKS[4 * g + n]], w, a[:, k], start=(k == 0 and j == 0),
                                                        stop=(k == 1 and j == 2))
                    last.then_inc(unit_done.sem, 1)
                    for n in range(4):
                        c = 4 * g + n
                        at_least(pe, gate_done, c - 1)
                        unit(pe, u + 1 + n, (u + 1 + n) % 2, bank[:, 6 + n % 2], MID_hi, MID_lo,
                             ready=op_in.tile_ready if c == 0 else None)
                        if c == 0:
                            op_in.add_up(pe)

            @block.scalar
            def _(act):
                for c in range(DT):
                    act.wait_ge(*gate_done.at(c + 1))
                    at_least(act, prod_done, c - 1)
                    nc.scalar.activation(tmp_b[:, c % 2], tmp_a[:, c % 2], ACT.Sigmoid).then_inc(sig_done.sem, 1)
                    op.on_act(act, c)

            @block.vector
            def _(dve):
                dve.wait_ge(*op_in.rstd_done.at(1))
                op.on_dve_first(dve)
                for c in range(DT):
                    b, u = c % 2, u0 + 5 * (c // 4)
                    dve.wait_ge(*unit_done.at(u + 2 + c % 4))
                    at_least(dve, sig_done, c - 1)
                    nc.vector.tensor_tensor(tmp_a[:, b], bank[:, 6 + b], rstd[:], ALU.mult).then_inc(gate_done.sem, 1)
                    dve.wait_ge(*sig_done.at(c + 1))
                    at_least(dve, op.h_done, c - 1)
                    nc.vector.tensor_tensor(tmp_c[:, b], bank[:, P_BANKS[c]], tmp_b[:, b], ALU.mult
                                            ).then_inc(prod_done.sem, 1)
                    dve.wait_ge(*prod_done.at(c + 1))
                    nc.vector.tensor_tensor(hT[:, c], hT[:, c], tmp_c[:, b], ALU.add).then_inc(op.h_done.sem, 1)
                    op.on_dve(dve, c)

        h_final = sem("h_final")

        def layer_tail(n, u0, previous, ready, ffn_gain, ple_gain, next_targets, meanwhile=None):
            attn_op = Operand(f"attn{n}", [(ffn_gain, IN_hi, IN_lo)], previous)

            @block.scalar
            def _(act):
                act.dma_start(ple_in[:], PT[n]).then_inc(p_loaded.sem, 16)

            tile_by_tile(f"back{n}", u0, MID_hi, MID_lo, ready, attn_op)
            attn_op.stats(0)

            @block.scalar
            def _(act):
                act.wait_ge(*p_loaded.at(16 * n + 16))
                nc.scalar.copy(ple_hi[:], ple_in[:]).then_inc(p_hi_done.sem, 1)

            @block.vector
            def _(dve):
                dve.wait_ge(*p_hi_done.at(n + 1))
                nc.vector.tensor_tensor(ple_lo[:], ple_in[:], ple_hi[:].bitcast(F32), ALU.subtract
                                        ).then_inc(p_lo_done.sem, 1)

            ffn_op = Operand(f"ffn{n}", [(ple_gain, MID_hi, MID_lo)], attn_op)
            feed_forward(f"ffn{n}", u0 + DT, attn_op, ffn_op, meanwhile=meanwhile)
            ffn_op.stats(2)
            next_op = Operand(f"ple{n}", next_targets, ffn_op)
            layer_embedding(f"ple{n}", u0 + DT + 3 * FT, n, ffn_op, next_op)
            return next_op

        areas[0] = area0
        SH_hi, SH_lo = area("SH_hi", [P, DT, S], F32R), area("SH_lo", [P, DT, S], F32R)
        layer0 = layer_tail(0, U_QKV0 + 3 * PAIRS, x_op, lambda pe, t: pe.wait_ge(*sb_o_lo.at(2 * t + 2)), G_FFN0, G_PLE0,
                            [(G_ATTN1, IN_hi, IN_lo), (G_SHARED, SH_hi, SH_lo)])
        layer0.stats(1)

        NOFF = [0, 128, 384, 768]
        tables_at = area0 + 52 * 1024
        NATURAL = ((3,), (2,), (1, 0))

        def softmax_attention(name, kind, npairs, u0, op_in, src_kv, gain_k, shared=None, extra=None):
            fox, diff, dsa = kind == "fox", kind == "diff", kind == "dsa"
            HI = 4 if dsa else 6
            per_pair = {"yq": 1, "sqq": 1, "statq": 1, "lnq": 1, "rnq": 1, "qn": 1, "qh": HI, "ql": HI, "nat": 6,
                        "max": 8, "diag": 2, "st": 6, "p": 8, "o": 2, "lns": 2, "rc": 2, "od": 2, "hi": 1, "lo": 1}
            if not dsa:
                per_pair |= {"yk": 1, "vt": 1, "sqk": 1, "statk": 1, "lnk": 1, "rnk": 1, "kn": 1, "turned": 1, "v": 1}
            if not fox:
                per_pair |= {"rotq": 1, "ropeq": 1, "qa": 1, "qs": 1}
            if diff:
                per_pair |= {"rotk": 1, "ropek": 1, "ka": 1, "ks": 1, "df": 1, "sso": 1, "sto": 1, "lno": 1,
                             "rno": 1, "nrm": 1}
            s = {x: again("soft_" + x, n * npairs + (x in ("qh", "ql") and dsa)) for x, n in per_pair.items()}
            KH0 = 1 if dsa else 0
            if fox:
                s["zeroed"] = again("soft_zeroed", 1)
            rope = not fox
            QA, QB = (area(name + "_q_" + x, [P, 2, S], F32R) for x in ("high", "low"))
            KS = area(name + "_k", [P, 1 if dsa else 2, S], F32R)
            VW = P if diff else 3 * HD
            V = shared["V"] if dsa else area(name + "_v", [P, 2, QT, VW], F32)
            DG = nc.alloc_sbuf_tensor_at(name + "_diag", [P, S], F32R, offset=place_used["neg_upto"])
            assert place_used["mask_kq"] == place_used["neg_upto"] + 4 * S
            RC = area(name + "_recip", [P, 2, S], F32) if diff else area(name + "_recip", [P, 1, S], F32)
            P0 = area(name + "_p0", [P, CAUSAL], F32)
            P1 = nc.alloc_sbuf_tensor_at(name + "_p1", [P, CAUSAL], F32, offset=place_used["tmp_b"])
            VT = nc.alloc_sbuf_tensor_at(name + "_vt", [P, S], F32, offset=place_used["tmp_b"] + 4 * CAUSAL)
            PW = (P0, P1)
            YQ, YK = tmp_a[:, 0], tmp_a[:, 1]
            SQ, RN = square, sumsq
            NM = area(name + "_max", [P, 2 * QT], F32)
            assert areas[0] <= (nc.sbuf_usable_end if fox else tables_at), (areas[0], nc.sbuf_usable_end)
            third_bank = (4, 5)
            out_bank = (5, 4 if diff else 7 if dsa else 1)

            def k_of(h):
                return KS[:, 0 if dsa else h]

            def v_of(b):
                return V if dsa else V[:, b]

            def natural_bank(h, t):
                b = (third_bank[h], third_bank[h], *((0, 7) if dsa and h == 1 else (1, 0)))[t]
                return bank[:, b, (0, P, 0, 0)[t]:][:, 0:P * (t + 1)]

            UPP = 1 if dsa else 3
            Q_BANK, K_BANK, V_BANK = 6, 7, 2

            def loop(engine, body):
                body(0, 0, True)
                if npairs > 4:
                    with engine.Fori(0, (npairs - 2) // 2) as i:
                        body(2 * i + 1, 1, True)
                        body(2 * i + 2, 0, True)
                else:
                    for p in range(1, npairs - 1):
                        body(p, p % 2, True)
                body(npairs - 1, (npairs - 1) % 2, False)

            @block.tensor
            def _(pe):
                def project(p, b, n):
                    u = u0 + UPP * p + n
                    hi, lo = (IN_hi, IN_lo) if n == 0 else src_kv
                    if n == 0:
                        at_least(pe, s["ropeq" if rope else "lnq"], p)
                    elif n == 1:
                        at_least(pe, s["ropek" if rope else "lnk"], p)
                    else:
                        at_least(pe, s["p"], 8 * p)
                        at_least(pe, s["v"], p)
                    slot = (u0 + UPP * p + n if isinstance(p, int) else u0 + b + n) % SLOTS
                    unit(pe, u, slot, bank[:, (Q_BANK, K_BANK, V_BANK)[n]], hi, lo)

                def stat(p, x):
                    pe.wait_ge(*s["sq" + x].at(p + 1))
                    nc.tensor.matmul(bank[:, Q_BANK if x == "q" else K_BANK], head_ones[:], SQ[:], start=True,
                                     stop=True).then_inc(s["stat" + x].sem, 1)

                def rotate(p, x):
                    pe.wait_ge(*s[x + "n"].at(p + 1))
                    nc.tensor.matmul(bank[:, Q_BANK if x == "q" else K_BANK], extra["perm"][:],
                                     (YQ if x == "q" else YK), start=True, stop=True).then_inc(s["rot" + x].sem, 1)

                def turn_v(p, b):
                    pe.wait_ge(*s["vt"].at(p + 1))
                    for t in range(QT):
                        last = nc.tensor.transpose(bank[:, V_BANK, t * P:(t + 1) * P], VT[:, t * P:(t + 1) * P],
                                                   ident[:])
                    last.then_inc(s["turned"].sem, 1)

                def natural(p, h):
                    if h == 0:
                        pe.wait_ge(*s["qh"].at(KH0 + HI * (p + 1)))
                        pe.wait_ge(*s["ql"].at(KH0 + HI * (p + 1)))
                    at_least(pe, s["max"], 8 * p + (1 if dsa and h == 1 else 4 * h))
                    if h == 1 or not dsa:
                        at_least(pe, s["od"], 2 * p)
                    if h == 0:
                        at_least(pe, s["p"], 8 * p)
                    if diff and h == 1:
                        at_least(pe, s["nrm"], p)
                    if fox:
                        pe.wait_ge(*extra["decay_row"].at(2 * p + h + 1))
                    for tiles in NATURAL:
                        for t in tiles:
                            out = natural_bank(h, t)
                            nc.tensor.matmul(out, QA[:, h, t * P:(t + 1) * P], k_of(h)[:, 0:P * (t + 1)],
                                             start=True, stop=False)
                            if fox:
                                nc.tensor.matmul(out, ones_r[0:HEADS], extra["rows"][:, h, 0:P * (t + 1)], start=False,
                                                 stop=False)
                            if dsa:
                                last = nc.tensor.matmul(out, ident_r[:],
                                                        extra["mask"][:, NOFF[t]:NOFF[t] + P * (t + 1)],
                                                        start=False, stop=True)
                            else:
                                last = nc.tensor.matmul(out[:, P * t:], ident_r[:], mask_qk[:], start=False, stop=True)
                        last.then_inc(s["nat"].sem, 1)

                def transposed(p, b, h):
                    pe.wait_ge(*s["diag"].at(2 * p + h + 1))
                    at_least(pe, s["p"], 8 * p + 4 * h)
                    if h == 0 and not dsa:
                        pe.wait_ge(*s["v"].at(p + 1))
                    for _, _, tiles in GROUPS:
                        for j in tiles:
                            out = tile_in_bank(2, j)
                            for q in (QA, QB):
                                nc.tensor.matmul(out, k_of(h)[:, j * P:(j + 1) * P], q[:, h, j * P:S],
                                                 start=(j != 3 and q is QA), stop=False, skip_group_check=True)
                            nc.tensor.matmul(out, ones_r[:], DG[:, j * P:S], start=False, stop=False,
                                             skip_group_check=True)
                            if dsa:
                                last = nc.tensor.matmul(out, ident_r[:], extra["maskT"][:, COL[j]:COL[j] + WIDTH[j]],
                                                        start=False, stop=True, skip_group_check=True)
                            else:
                                last = nc.tensor.matmul(out[:, 0:P], ident_r[:], mask_kq[:], start=False, stop=True,
                                                        skip_group_check=True)
                        last.then_inc(s["st"].sem, 1)

                def output(p, b, h):
                    pe.wait_ge(*s["p"].at(8 * p + 4 * h + 4))
                    pe.wait_ge(*s["max"].at(8 * p + 8))
                    if diff and h == 1:
                        pe.wait_ge(*s["p"].at(8 * p + 8))
                    x = 0 if diff else HD * h
                    for j in range(QT):
                        w = PW[h][:, COL[j]:COL[j] + WIDTH[j]]
                        last = nc.tensor.matmul(bank[:, out_bank[h], j * P:S], v_of(b)[:, j, x:x + P], w,
                                                start=(j == 0), stop=(j == QT - 1))
                    if diff:
                        for j in range(QT):
                            w = PW[h][:, COL[j]:COL[j] + WIDTH[j]]
                            last = nc.tensor.matmul(bank[:, h, j * P:S], ones[:], w, start=(j == 0),
                                                    stop=(j == QT - 1))
                    last.then_inc(s["o"].sem, 1)

                def norm_out(p):
                    pe.wait_ge(*s["sso"].at(p + 1))
                    nc.tensor.matmul(bank[:, 5], ones[:], SQ[:], start=True, stop=True).then_inc(s["sto"].sem, 1)

                last_pair = extra.get("last_pair", lambda pe, part: None)
                if "before" in extra:
                    pe.wait_ge(*extra["before"].at(extra["before_count"]))
                project(0, 0, 0)
                if not dsa:
                    project(0, 0, 1)
                if fox:
                    extra["turn_decay"](pe)
                stat(0, "q")
                if not dsa:
                    stat(0, "k")
                if rope:
                    rotate(0, "q")
                    if not dsa:
                        rotate(0, "k")
                if not dsa:
                    project(0, 0, 2)
                if not dsa:
                    turn_v(0, 0)

                def pair(p, b, more):
                    c = (b + 1) % 2
                    if more and dsa:
                        project(p + 1, c, 0)
                    natural(p, 0)
                    if more and not dsa:
                        project(p + 1, c, 0)
                    if not more:
                        last_pair(pe, 0)
                    natural(p, 1)
                    transposed(p, b, 0)
                    if more and dsa:
                        stat(p + 1, "q")
                    if more and not dsa:
                        project(p + 1, c, 1)
                    if not more:
                        last_pair(pe, 1)
                    transposed(p, b, 1)
                    if more and not dsa:
                        stat(p + 1, "q")
                    if more and dsa:
                        rotate(p + 1, "q")
                    if not more:
                        last_pair(pe, 2)
                    output(p, b, 0)
                    if more and not dsa:
                        stat(p + 1, "k")
                        if rope:
                            rotate(p + 1, "q")
                    output(p, b, 1)
                    if more and not dsa:
                        if rope:
                            rotate(p + 1, "k")
                        project(p + 1, c, 2)
                    if diff:
                        norm_out(p)
                    if more and not dsa:
                        turn_v(p + 1, c)

                loop(pe, pair)

            @block.scalar
            def _(act):
                def squares(p, x):
                    act.wait_ge(*s["y" + x].at(p + 1))
                    if x == "q":
                        at_least(act, s["statq"] if dsa else s["statk"], p)
                        if diff:
                            at_least(act, s["sto"], p - 1)
                    else:
                        act.wait_ge(*s["statq"].at(p + 1))
                    nc.scalar.activation(SQ[:], YQ if x == "q" else YK, ACT.Square).then_inc(s["sq" + x].sem, 1)

                def norms(p, x):
                    act.wait_ge(*s["stat" + x].at(p + 1))
                    if x == "q":
                        at_least(act, s["qn"] if dsa else s["kn"], p)
                        if diff:
                            at_least(act, s["nrm"], p - 1)
                    else:
                        act.wait_ge(*s["qn"].at(p + 1))
                    nc.scalar.activation(RN[:], bank[:, Q_BANK if x == "q" else K_BANK], ACT.Ln, bias=eps_c[:],
                                         scale=1.0 / HD).then_inc(s["ln" + x].sem, 1)
                    act.wait_ge(*s["ln" + x].at(p + 1))
                    nc.scalar.activation(RN[:], RN[:], ACT.Exp, scale=-0.5).then_inc(s["rn" + x].sem, 1)

                def split_q(p):
                    act.wait_ge(*s["qs" if rope else "qn"].at(p + 1))
                    at_least(act, s["st"], 6 * p)
                    high_q(act, YQ, QA, s["qh"], 0)

                def split_k(p):
                    act.wait_ge(*s["ks" if rope else "kn"].at(p + 1))
                    high_k(act, YK, KS, s["qh"])

                def copy_v(p, b):
                    act.wait_ge(*s["turned"].at(p + 1))
                    at_least(act, s["o"], 2 * (p - 1))
                    v = bank[:, V_BANK].rearrange("p (t c) -> p t c", t=QT)
                    if diff:
                        nc.scalar.copy(V[:, b], v).then_inc(s["v"].sem, 1)
                    else:
                        nc.scalar.copy(V[:, b, :, 0:HD], v[:, :, 0:HD])
                        nc.scalar.copy(V[:, b, :, 2 * HD:3 * HD], v[:, :, HD:P]).then_inc(s["v"].sem, 1)

                def weights(p, h):
                    at_least(act, s["o"], 2 * (p - 1) + h + 1)
                    for g, (_, _, tiles) in enumerate(GROUPS):
                        act.wait_ge(*s["st"].at(6 * p + 3 * h + g + 1))
                        if fox:
                            act.sem_inc(act_turns.sem, 1)
                        for j in tiles:
                            bias = column(extra["key_bias"], HEADS * j + 2 * p + h) if fox else 0.0
                            nc.scalar.activation(PW[h][:, COL[j]:COL[j] + WIDTH[j]], tile_in_bank(2, j), ACT.Exp,
                                                 bias=bias).then_inc(s["p"].sem, 1)

                def decay_row(p, h):
                    at_least(act, s["nat"], 6 * (p - 1) + 3 * h + 3)
                    act.sem_inc(act_turns.sem, 1)
                    nc.scalar.activation(extra["rows"][:, h], extra["minus_f"][:], ACT.Copy,
                                         scale=column(ident, 2 * p + h)[0:HEADS]).then_inc(extra["decay_row"].sem, 1)

                def reciprocals(p, h):
                    if h == 0:
                        at_least(act, s["lo"], p)
                    act.wait_ge(*s["o"].at(2 * p + h + 1))
                    x = RC[:, h] if diff else RC[rows(h), 0]
                    nc.scalar.activation(x, bank[:, h] if diff else bank[rows(1 - h), out_bank[h]], ACT.Ln
                                         ).then_inc(s["lns"].sem, 1)
                    act.wait_ge(*s["lns"].at(2 * p + h + 1))
                    nc.scalar.activation(x, x, ACT.Exp, scale=-1.0).then_inc(s["rc"].sem, 1)

                act.preload_act_table_set("natural_log_exp_and_others")
                if dsa:
                    nc.scalar.copy(KS[:, 0], shared["K"][:]).then_inc(s["qh"].sem, 1)
                squares(0, "q")
                norms(0, "q")
                if not dsa:
                    squares(0, "k")
                    norms(0, "k")
                split_q(0)
                if not dsa:
                    split_k(0)
                if fox:
                    act.wait_ge(*f_turned.at(1))
                    nc.scalar.copy(key_bias[:], bank[:, 3, 0:QT * HEADS]).then_inc(f_bias.sem, 1)
                    act.wait_ge(*f_bias.at(1))
                    decay_row(0, 0)
                    decay_row(0, 1)
                if not dsa:
                    copy_v(0, 0)

                def pair(p, b, more):
                    c = (b + 1) % 2
                    if more and dsa:
                        squares(p + 1, "q")
                    if not more and "last_pair_act" in extra:
                        extra["last_pair_act"](act, 0)
                    weights(p, 0)
                    if not more and "last_pair_act" in extra:
                        extra["last_pair_act"](act, 1)
                    if more:
                        if not dsa:
                            squares(p + 1, "q")
                        if fox:
                            decay_row(p + 1, 0)
                            decay_row(p + 1, 1)
                        if dsa:
                            norms(p + 1, "q")
                    weights(p, 1)
                    if not more and "last_pair_act" in extra:
                        extra["last_pair_act"](act, 2)
                    if more and not dsa:
                        norms(p + 1, "q")
                        squares(p + 1, "k")
                    reciprocals(p, 0)
                    if more and not dsa:
                        norms(p + 1, "k")
                    if more:
                        split_q(p + 1)
                    reciprocals(p, 1)
                    if diff:
                        act.wait_ge(*s["df"].at(p + 1))
                        if more:
                            act.wait_ge(*s["statk"].at(p + 2))
                            act.wait_ge(*s["kn"].at(p + 2))
                        nc.scalar.activation(SQ[:], RC[:, 0], ACT.Square).then_inc(s["sso"].sem, 1)
                    if more and not dsa:
                        split_k(p + 1)
                    if diff:
                        act.wait_ge(*s["sto"].at(p + 1))
                        nc.scalar.activation(RN[:], bank[:, 5], ACT.Ln, bias=eps_c[:], scale=1.0 / P
                                             ).then_inc(s["lno"].sem, 1)
                        act.wait_ge(*s["lno"].at(p + 1))
                        nc.scalar.activation(RN[:], RN[:], ACT.Exp, scale=-0.5).then_inc(s["rno"].sem, 1)
                        if more:
                            copy_v(p + 1, c)
                        act.wait_ge(*s["nrm"].at(p + 1))
                    else:
                        act.wait_ge(*s["od"].at(2 * p + 2))
                    act.sem_inc(act_turns.sem, 1)
                    t = p if not diff else p + 4
                    nc.scalar.copy(tile(MID_hi, t), RC[:, 0]).then_inc(s["hi"].sem, 1)
                    if more and fox:
                        copy_v(p + 1, c)

                loop(act, pair)

            @block.vector
            def _(dve):
                def take(p, n):
                    dve.wait_ge(*unit_done.at(u0 + UPP * p + n + 1))
                    if n == 0:
                        if rope:
                            at_least(dve, s["ropeq"], p)
                        at_least(dve, s["ql"], KH0 + HI * p)
                        at_least(dve, s["qh"], KH0 + HI * p)
                        nc.vector.tensor_tensor(YQ, bank[:, Q_BANK], rstd[:], ALU.mult).then_inc(s["yq"].sem, 1)
                    elif n == 1:
                        nc.vector.tensor_tensor(YK, bank[:, K_BANK], rstd[:], ALU.mult).then_inc(s["yk"].sem, 1)
                    else:
                        at_least(dve, s["turned"], p)
                        nc.vector.tensor_tensor(VT[:], bank[:, V_BANK], rstd[:], ALU.mult).then_inc(s["vt"].sem, 1)

                def finish_q(p, b):
                    dve.wait_ge(*s["rnq"].at(p + 1))
                    nc.vector.scalar_tensor_tensor(YQ, YQ, extra["gq"] if rope else extra["gq"][:], RN[:],
                                                   ALU.mult, ALU.mult).then_inc(s["qn"].sem, 1)

                def finish_k(p, b):
                    dve.wait_ge(*s["rnk"].at(p + 1))
                    nc.vector.scalar_tensor_tensor(YK, YK, hgains[:, gain_k:gain_k + 1], RN[:],
                                                   ALU.mult, ALU.mult).then_inc(s["kn"].sem, 1)

                def rope_it(p, b, x):
                    y = YQ if x == "q" else YK
                    dve.wait_ge(*s["rot" + x].at(p + 1))
                    nc.vector.tensor_tensor(SW[:], bank[:, Q_BANK if x == "q" else K_BANK], extra["sin"][:], ALU.mult
                                            ).then_inc(s["rope" + x].sem, 1)
                    nc.vector.tensor_tensor(y, y, extra["cos"][:], ALU.mult).then_inc(s[x + "a"].sem, 1)
                    dve.wait_ge(*s["rope" + x].at(p + 1))
                    dve.wait_ge(*s[x + "a"].at(p + 1))
                    nc.vector.tensor_tensor(y, y, SW[:], ALU.add).then_inc(s[x + "s"].sem, 1)
                    dve.wait_ge(*s[x + "s"].at(p + 1))

                def maxima(p, h):
                    at_least(dve, s["diag"], 2 * p - 1 + h)
                    for k, t in enumerate((3, 2, 1, 0)):
                        dve.wait_ge(*s["nat"].at(6 * p + 3 * h + min(k, 2) + 1))
                        nc.vector.tensor_reduce(NM[:, 4 * h + t:4 * h + t + 1], natural_bank(h, t), AX.X, ALU.max,
                                                negate=True).then_inc(s["max"].sem, 1)

                def diagonal(p, h):
                    dve.wait_ge(*s["max"].at(8 * p + 4 * h + 4))
                    at_least(dve, s["st"], 6 * p + 3 * h)
                    nc.vector.tensor_tensor(DG[:].rearrange("p (t c) -> p t c", t=QT),
                                            ident[:].unsqueeze(1).to_broadcast([P, QT, P]),
                                            NM[:, 4 * h:4 * h + 4].unsqueeze(2).to_broadcast([P, QT, P]), ALU.mult
                                            ).then_inc(s["diag"].sem, 1)

                def outputs(p, h):
                    dve.wait_ge(*s["rc"].at(2 * p + h + 1))
                    x, r = (RC[:, h], slice(0, P)) if diff else (RC[rows(h), 0], rows(h))
                    nc.vector.tensor_tensor(x, x, bank[r, out_bank[h]], ALU.mult).then_inc(s["od"].sem, 1)
                    if diff and h == 1:
                        dve.wait_ge(*s["od"].at(2 * p + 2))
                        nc.vector.scalar_tensor_tensor(RC[:, 0], RC[:, 1], extra["neg_lam"], RC[:, 0],
                                                       ALU.mult, ALU.add).then_inc(s["df"].sem, 1)

                def norm_out(p):
                    dve.wait_ge(*s["rno"].at(p + 1))
                    nc.vector.scalar_tensor_tensor(RC[:, 0], RC[:, 0], 1.0 - LAMBDA_INIT, RN[:],
                                                   ALU.mult, ALU.mult).then_inc(s["nrm"].sem, 1)

                def low(p):
                    dve.wait_ge(*s["hi"].at(p + 1))
                    t = p if not diff else p + 4
                    nc.vector.tensor_tensor(tile(MID_lo, t), RC[:, 0], tile(MID_hi, t).bitcast(F32), ALU.subtract
                                            ).then_inc(s["lo"].sem, 1)

                def prepare(p, b, part):
                    if part == 0:
                        take(p, 0)
                    elif part == 1:
                        if not dsa:
                            take(p, 1)
                    elif part == 2:
                        finish_q(p, b)
                    elif part == 3:
                        if not dsa:
                            finish_k(p, b)
                    elif part == 4:
                        if rope:
                            rope_it(p, b, "q")
                    else:
                        if diff:
                            rope_it(p, b, "k")

                def split(p):
                    low_q(dve, YQ, QA, QB, s["qh"], KH0 + HI * p, s["ql"])
                    if not dsa:
                        low_k(dve, YK, KS, s["qh"], HI * p + 4, s["ql"])

                SW = extra.get("swap")
                meanwhile = extra.get("meanwhile", lambda p, part: None)
                if fox:
                    nc.vector.memset(V[:, :, :, HD:2 * HD], 1.0).then_inc(s["zeroed"].sem, 1)
                    dve.wait_ge(*s["zeroed"].at(1))
                if dsa:
                    dve.wait_ge(*s["qh"].at(1))
                    nc.vector.tensor_tensor(KS[HD:P, 0], shared["K"][HD:P], KS[HD:P, 0].bitcast(F32), ALU.subtract
                                            ).then_inc(s["ql"].sem, 1)
                for part in range(4):
                    prepare(0, 0, part)
                if fox:
                    split(0)
                prepare(0, 0, 4)
                prepare(0, 0, 5)
                if not fox:
                    split(0)
                if not dsa:
                    take(0, 2)

                def pair(p, b, more):
                    c = (b + 1) % 2
                    if more and dsa:
                        prepare(p + 1, c, 0)
                    maxima(p, 0)
                    diagonal(p, 0)
                    meanwhile(p, 0)
                    maxima(p, 1)
                    if more and not dsa:
                        prepare(p + 1, c, 0)
                    diagonal(p, 1)
                    meanwhile(p, 1)
                    if more:
                        prepare(p + 1, c, 1)
                    meanwhile(p, 2)
                    if more:
                        prepare(p + 1, c, 2)
                    meanwhile(p, 3)
                    if more and dsa:
                        prepare(p + 1, c, 4)
                    outputs(p, 0)
                    if more:
                        if diff:
                            prepare(p + 1, c, 4)
                        prepare(p + 1, c, 3)
                        low_q(dve, YQ, QA, QB, s["qh"], KH0 + HI * (p + 1), s["ql"])
                    outputs(p, 1)
                    if more and not dsa:
                        if diff:
                            prepare(p + 1, c, 5)
                            take(p + 1, 2)
                        low_k(dve, YK, KS, s["qh"], HI * (p + 1) + 4, s["ql"])
                        if fox:
                            take(p + 1, 2)
                    if diff:
                        norm_out(p)
                    low(p)

                loop(dve, pair)
            return s

        areas[0] = area0 + 2 * 4 * DT * S
        LF = nc.alloc_sbuf_tensor_at("LF", [HEADS, S], F32, offset=place_used["ple_in"])
        decay_rows = nc.alloc_sbuf_tensor_at("decay_rows", [HEADS, 2, S], F32R, offset=place_used["ple_in"] + 4 * S)
        key_bias = nc.alloc_sbuf_tensor_at("key_bias", [P, QT * HEADS], F32,
                                           offset=place_used["tmp_b"] + 4 * (CAUSAL + S))
        gq_fox = area("gq_fox", [P, 1], F32)
        f_x, f_abs, f_exp, f_ln, f_min, f_log, f_cum, f_turned, f_bias = (
            sem("f_" + x) for x in "x abs exp ln min log cum turned bias".split())
        f_row = sem("f_row")

        @block.tensor
        def _(pe):
            unit(pe, U_F1, U_F1 % SLOTS, bank[:, 0], SH_hi, SH_lo, ready=layer0.tile_ready)
            layer0.add_up(pe)

        def turn_decay(pe):
            pe.wait_ge(*f_cum.at(1))
            for t in range(QT):
                last = nc.tensor.transpose(bank[:, 3, t * HEADS:(t + 1) * HEADS], LF[:, t * P:(t + 1) * P],
                                           ident[0:HEADS, 0:HEADS])
            last.then_inc(f_turned.sem, 1)

        @block.vector
        def _(dve):
            x, a = tmp_a[0:HEADS, 0], tmp_a[0:HEADS, 1]
            dve.wait_ge(*layer0.rstd_done.at(1))
            dve.wait_ge(*unit_done.at(U_F1 + 1))
            dve.wait_ge(*small_loaded.at(64))
            nc.vector.tensor_tensor(x, bank[0:HEADS, 0], rstd[0:HEADS], ALU.mult).then_inc(f_x.sem, 1)
            dve.wait_ge(*f_x.at(1))
            nc.vector.tensor_scalar(x, x, forget_bias[:], None, ALU.add).then_inc(f_x.sem, 1)
            dve.wait_ge(*f_abs.at(1))
            nc.vector.tensor_scalar(x, x, 0.0, None, ALU.min).then_inc(f_min.sem, 1)
            dve.wait_ge(*f_min.at(1))
            dve.wait_ge(*f_ln.at(1))
            nc.vector.tensor_tensor(x, a, x, ALU.subtract).then_inc(f_log.sem, 1)
            nc.vector.memset(tmp_b[0:HEADS, 0], 1.0).then_inc(f_log.sem, 1)
            nc.vector.tensor_scalar(gq_fox[:], hgains[:, H_FOXQ:H_FOXQ + 1], HD ** -0.5, None, ALU.mult
                                    ).then_inc(f_log.sem, 1)
            dve.wait_ge(*f_log.at(3))
            nc.vector.tensor_tensor_scan(LF[:], tmp_b[0:HEADS, 0], x, 0.0, ALU.mult, ALU.add).then_inc(f_cum.sem, 1)

        @block.scalar
        def _(act):
            x, a = tmp_a[0:HEADS, 0], tmp_a[0:HEADS, 1]
            act.wait_ge(*f_x.at(2))
            nc.scalar.activation(a, x, ACT.Abs).then_inc(f_abs.sem, 1)
            act.wait_ge(*f_abs.at(1))
            nc.scalar.activation(a, a, ACT.Exp, scale=-1.0).then_inc(f_exp.sem, 1)
            act.wait_ge(*f_exp.at(1))
            nc.scalar.activation(a, a, ACT.Ln, bias=one_c[0:HEADS]).then_inc(f_ln.sem, 1)

        fox = softmax_attention("fox", "fox", PAIRS, U_KVQ1, layer0, (SH_hi, SH_lo), H_FOXK,
                                extra={"rows": decay_rows, "minus_f": LF, "decay_row": f_row, "key_bias": key_bias,
                                       "gq": gq_fox, "turn_decay": turn_decay})
        sin_t = nc.alloc_sbuf_tensor_at("sin_t", [P, S], F32, offset=place_used["ple_in"])
        cos_t = nc.alloc_sbuf_tensor_at("cos_t", [P, S], F32, offset=place_used["ple_in"] + 4 * S)
        inv_freq, lam_in, lam_products, lam_exp = small[:, 0:1], small[0:HD, 1:5], small[0:HD, 5:7], small[:, 7:9]
        neg_lam, gq_a, gq_b = small[:, 9:10], small[:, 10:11], small[:, 11:12]
        gq_x, top8 = small[:, 12:14], small[:, 16:24]
        pos_i = nc.alloc_sbuf_tensor_at("pos_i", [P, S], I32, offset=place_used["tmp_b"])
        angle, turns = tmp_a[:, 0], tmp_a[:, 1]
        i_loaded, m_loaded = sem("index_loaded"), sem("memory_loaded")
        t_step, t_sin, t_lam, t_exp = (sem("table_" + x) for x in ("step", "sin", "lam", "exp"))

        def make_tables(before):

            @block.scalar
            def _(act):
                for s, n in before:
                    act.wait_ge(*s.at(n))
                act.dma_start(inv_freq, INVF).then_inc(i_loaded.sem, 16)
                act.dma_start(lam_in, LAM).then_inc(i_loaded.sem, 16)
                act.dma_start(pos_i[:], POS[0].partition_broadcast(P)).then_inc(i_loaded.sem, 16)
                act.wait_ge(*t_step.at(8))
                nc.scalar.activation(sin_t[:], turns, ACT.Sin).then_inc(t_sin.sem, 1)
                nc.scalar.activation(cos_t[:], turns, ACT.Sin, scale=0.5).then_inc(t_sin.sem, 1)

            @block.vector
            def _(dve):
                def step(n):
                    dve.wait_ge(*t_step.at(n))

                dve.wait_ge(*i_loaded.at(48))
                nc.vector.tensor_copy(angle, pos_i[:]).then_inc(t_step.sem, 1)
                step(1)
                nc.vector.tensor_scalar(angle, angle, inv_freq, None, ALU.mult).then_inc(t_step.sem, 1)
                step(2)
                ROUND = 1.5 * 2.0 ** 23
                nc.vector.tensor_scalar(turns, angle, 1.0 / (2 * np.pi), ROUND, ALU.mult, ALU.add).then_inc(t_step.sem, 1)
                step(3)
                nc.vector.tensor_scalar(turns, turns, ROUND, None, ALU.subtract).then_inc(t_step.sem, 1)
                step(4)
                c1 = 6.28125
                c2 = float(np.round((2 * np.pi - c1) * 2.0 ** 20) / 2.0 ** 20)
                for n, c in enumerate((c1, c2, 2 * np.pi - c1 - c2)):
                    nc.vector.scalar_tensor_tensor(angle, turns, -c, angle, ALU.mult, ALU.add).then_inc(t_step.sem, 1)
                    step(5 + n)
                nc.vector.tensor_scalar(turns, angle, 3.1415925, -3.1415925, ALU.min, ALU.max).then_inc(t_step.sem, 1)
                nc.vector.tensor_tensor(lam_products, small[0:HD, 1:5:2], small[0:HD, 2:5:2], ALU.mult
                                        ).then_inc(t_step.sem, 1)
                dve.wait_ge(*t_sin.at(2))
                nc.vector.tensor_tensor(cos_t[:], cos_t[:], cos_t[:], ALU.mult).then_inc(t_step.sem, 1)
                step(10)
                nc.vector.tensor_scalar(cos_t[:], cos_t[:], -2.0, 1.0, ALU.mult, ALU.add).then_inc(t_step.sem, 1)
                nc.vector.tensor_scalar(gq_a, hgains[:, H_QA:H_QA + 1], HD ** -0.5, None, ALU.mult).then_inc(t_step.sem, 1)
                nc.vector.tensor_scalar(gq_b, hgains[:, H_QB:H_QB + 1], HD ** -0.5, None, ALU.mult).then_inc(t_step.sem, 1)
                nc.vector.tensor_scalar(gq_x, xgains[:, 0:2], 1.0 / 16, None, ALU.mult).then_inc(t_step.sem, 1)
                step(14)

        layer1 = layer_tail(1, U_KVQ1 + 3 * PAIRS, layer0, lambda pe, t: pe.wait_ge(*fox["lo"].at(t + 1)), G_FFN1, G_PLE1,
                            [(G_MIX, IN_hi, IN_lo)], meanwhile=make_tables)
        layer1.stats(0)

        mem_in = nc.alloc_sbuf_tensor_at("mem_in", [P, DT, M], F32, offset=place_used["ple_hi"])
        areas[0] = tables_at
        swap = area("swap", [P, S], F32)
        areas[0] = area0
        dsa_k = area("dsa_k", [P, S], F32)
        dsa_v = area("dsa_v", [P, QT, 3 * HD], F32)
        chosen = area("chosen", [P, CAUSAL], F32R)
        chosen_t = area("chosen_t", [P, CAUSAL], F32R)
        TOP_OFF = {1: 0, 2: 256, 3: 640}
        index_scores = area("index_scores", [P, 1152], F32)
        after_index = areas[0]
        idx_q = area("idx_q", [P, 2, 2, S], F32)
        idx_k = area("idx_k", [P, S], F32)
        idx_w = area("idx_w", [P, QT, 4], F32)
        relu = area("relu", [P, 2, S], F32)
        idx_tmp = area("idx_tmp", [P, 5, S], F32)
        i_taken, i_rot, i_sw, i_cos, i_done = (sem("index_" + x) for x in "taken rotated swapped cosine done".split())
        i_sq, i_stat, i_ln, i_rn, i_kn = (again("soft_" + x, 1) for x in "sqk statk lnk rnk kn".split())
        i_turned, i_v = again("soft_turned", 1), again("soft_v", 3)
        i_z, i_relu, i_sum = (sem("index_" + x) for x in "z relu sum".split())
        i_max, i_out, i_mask, i_maskt, i_copied = (sem("top_" + x) for x in "max out mask turned copied".split())
        i_zeroed = sem("index_zeroed")
        TOPK = S // 4
        K_I, V_W, Q_I, Q_J, K_A = range(5)
        UNIT_BANK, ROT_BANK = (1, 2, 3, 4, 5), {K_I: 6, Q_I: 7, Q_J: 1, K_A: 3}
        ROTATED = (K_I, Q_I, Q_J, K_A)

        FOUND = -3.0e38

        CHOICE_STEPS = (0, 6, 12, 13, 15)
        CHOICES = 3 * TOPK // 8

        def choose(first, last):
            for k in range(first, min(last, CHOICES)):
                t = k % 3 + 1
                x = index_scores[:, TOP_OFF[t]:TOP_OFF[t] + P * (t + 1)]
                at_least(nc.vector, i_out, k)
                nc.vector.max(top8, x).then_inc(i_max.sem, 1)
                nc.vector.wait_ge(*i_max.at(k + 1))
                nc.vector.match_replace(x, top8, x, FOUND).then_inc(i_out.sem, 1)
                if k == CHOICES - 1:
                    nc.vector.wait_ge(*i_out.at(CHOICES))
                    nc.vector.tensor_scalar(chosen[:, P:], index_scores[:], FOUND / 1.5, NEG, ALU.is_gt, ALU.mult
                                            ).then_inc(i_mask.sem, 1)

        @block.scalar
        def _(act):
            act.wait_ge(*layer1.h_done.at(DT))
            act.dma_start(mem_in[:], MEMT).then_inc(m_loaded.sem, 16)
            act.preload_act_table_set("natural_log_exp_and_others")
            act.wait_ge(*t_lam.at(1))
            nc.scalar.activation(lam_exp, bank[:, 6, 0:2], ACT.Exp).then_inc(t_exp.sem, 1)

        @block.vector
        def _(dve):
            def step(n):
                dve.wait_ge(*t_step.at(n))

            nc.vector.memset(idx_q[:], 0.0).then_inc(i_zeroed.sem, 1)
            nc.vector.memset(dsa_v[:, :, HD:2 * HD], 1.0).then_inc(i_zeroed.sem, 1)
            dve.wait_ge(*layer1.rstd_done.at(1))
            dve.wait_ge(*i_zeroed.at(2))

            def take(n):
                dve.wait_ge(*unit_done.at(U_IDX + n + 1))
                nc.vector.tensor_tensor(idx_tmp[:, n], bank[:, UNIT_BANK[n]], rstd[:], ALU.mult).then_inc(i_taken.sem, 1)

            def rotary(n, k):
                dve.wait_ge(*i_rot.at(k + 1))
                at_least(dve, i_done, k)
                nc.vector.tensor_tensor(swap[:], bank[:, ROT_BANK[n]], sin_t[:], ALU.mult).then_inc(i_sw.sem, 1)
                nc.vector.tensor_tensor(idx_tmp[:, n], idx_tmp[:, n], cos_t[:], ALU.mult).then_inc(i_cos.sem, 1)
                dve.wait_ge(*i_sw.at(k + 1))
                dve.wait_ge(*i_cos.at(k + 1))
                if n in (Q_I, Q_J):
                    for h in range(2):
                        last = nc.vector.tensor_tensor(idx_q[rows(h), n - Q_I, h], idx_tmp[rows(h), n], swap[rows(h)],
                                                       ALU.add)
                else:
                    last = nc.vector.tensor_tensor((idx_k if n == K_I else dsa_k)[:], idx_tmp[:, n], swap[:], ALU.add)
                last.then_inc(i_done.sem, 1)

            take(K_I)
            take(V_W)
            rotary(K_I, 0)
            take(Q_I)
            take(Q_J)
            rotary(Q_I, 1)
            rotary(Q_J, 2)
            take(K_A)
            dve.wait_ge(*i_rn.at(1))
            dve.wait_ge(*i_taken.at(5))
            nc.vector.scalar_tensor_tensor(idx_tmp[:, K_A], idx_tmp[:, K_A], hgains[:, H_KA:H_KA + 1], sumsq[:],
                                           ALU.mult, ALU.mult).then_inc(i_kn.sem, 1)
            for t in range(1, QT):
                acc = index_scores[:, TOP_OFF[t]:TOP_OFF[t] + P * (t + 1)]
                for h in range(4):
                    k = 4 * (t - 1) + h
                    dve.wait_ge(*i_relu.at(k + 1))
                    if h == 0:
                        dve.wait_ge(*i_v.at(3))
                        nc.vector.tensor_scalar(acc, relu[:, k % 2, 0:P * (t + 1)], idx_w[:, t, h:h + 1], None, ALU.mult
                                                ).then_inc(i_sum.sem, 1)
                    else:
                        dve.wait_ge(*i_sum.at(k))
                        nc.vector.scalar_tensor_tensor(acc, relu[:, k % 2, 0:P * (t + 1)], idx_w[:, t, h:h + 1], acc,
                                                       ALU.mult, ALU.add).then_inc(i_sum.sem, 1)
            dve.wait_ge(*i_sum.at(12))
            for t in range(1, QT):
                x = index_scores[:, TOP_OFF[t] + P * t:TOP_OFF[t] + P * (t + 1)]
                nc.vector.tensor_tensor(x, x, mask_qk[:].bitcast(F32), ALU.add).then_inc(i_sum.sem, 1)
            dve.wait_ge(*t_exp.at(1))
            nc.vector.tensor_tensor(neg_lam, lam_exp[:, 1:2], lam_exp[:, 0:1], ALU.subtract).then_inc(t_step.sem, 1)
            step(15)
            nc.vector.tensor_scalar(neg_lam, neg_lam, LAMBDA_INIT, None, ALU.subtract).then_inc(t_step.sem, 1)
            rotary(K_A, 3)
            nc.vector.tensor_copy(chosen[:, 0:P], mask_qk[:].bitcast(F32)).then_inc(i_mask.sem, 1)
            dve.wait_ge(*i_sum.at(15))
            dve.wait_ge(*i_done.at(4))
            choose(0, 4)

        @block.tensor
        def _(pe):
            def rotate(n, k):
                nc.tensor.matmul(bank[:, ROT_BANK[n]], perm[:], idx_tmp[:, n], start=True, stop=True
                                 ).then_inc(i_rot.sem, 1)

            def project(n, ready=None):
                unit(pe, U_IDX + n, (U_IDX + n) % SLOTS, bank[:, UNIT_BANK[n]], IN_hi, IN_lo, ready=ready)

            project(K_I, layer1.tile_ready)
            layer1.add_up(pe)
            project(V_W)
            nc.tensor.matmul(bank[:, 6, 0:2], ones[0:HD], lam_products, start=True, stop=True).then_inc(t_lam.sem, 1)
            pe.wait_ge(*t_exp.at(1))
            pe.wait_ge(*i_taken.at(1))
            rotate(K_I, 0)
            project(Q_I)
            project(Q_J)
            pe.wait_ge(*i_taken.at(3))
            rotate(Q_I, 1)
            pe.wait_ge(*i_taken.at(4))
            rotate(Q_J, 2)
            for t in range(QT):
                last = nc.tensor.transpose(bank[:, 2, t * P:(t + 1) * P], idx_tmp[:, V_W, t * P:(t + 1) * P], ident[:])
            last.then_inc(i_turned.sem, 1)
            project(K_A)
            pe.wait_ge(*i_sq.at(1))
            nc.tensor.matmul(bank[:, 4], head_ones[:], square[:], start=True, stop=True).then_inc(i_stat.sem, 1)
            pe.wait_ge(*i_done.at(3))
            for t in range(1, QT):
                for h in range(4):
                    k = 4 * (t - 1) + h
                    at_least(pe, i_relu, k - 1)
                    nc.tensor.matmul(bank[:, 6 + k % 2, 0:P * (t + 1)], idx_q[:, h // 2, h % 2, t * P:(t + 1) * P],
                                     idx_k[:, 0:P * (t + 1)], start=True, stop=True).then_inc(i_z.sem, 1)
            pe.wait_ge(*i_kn.at(1))
            rotate(K_A, 3)

        @block.scalar
        def _(act):
            v = bank[:, 2].rearrange("p (t c) -> p t c", t=QT)
            act.wait_ge(*i_turned.at(1))
            act.wait_ge(*i_zeroed.at(2))
            nc.scalar.copy(dsa_v[:, :, 0:HD], v[:, :, 0:HD]).then_inc(i_v.sem, 1)
            nc.scalar.copy(dsa_v[:, :, 2 * HD:], v[:, :, 0:HD]).then_inc(i_v.sem, 1)
            nc.scalar.activation(idx_w[:], v[:, :, HD:HD + 4], ACT.Copy, scale=1.0 / 16).then_inc(i_v.sem, 1)
            act.wait_ge(*i_taken.at(5))
            nc.scalar.activation(square[:], idx_tmp[:, K_A], ACT.Square).then_inc(i_sq.sem, 1)
            act.wait_ge(*i_stat.at(1))
            nc.scalar.activation(sumsq[:], bank[:, 4], ACT.Ln, bias=eps_c[:], scale=1.0 / HD).then_inc(i_ln.sem, 1)
            act.wait_ge(*i_ln.at(1))
            nc.scalar.activation(sumsq[:], sumsq[:], ACT.Exp, scale=-0.5).then_inc(i_rn.sem, 1)
            for t in range(1, QT):
                for h in range(4):
                    k = 4 * (t - 1) + h
                    act.wait_ge(*i_z.at(k + 1))
                    at_least(act, i_sum, k - 1)
                    nc.scalar.activation(relu[:, k % 2, 0:P * (t + 1)], bank[:, 6 + k % 2, 0:P * (t + 1)], ACT.Relu
                                         ).then_inc(i_relu.sem, 1)

        rotary_extra = {"perm": perm, "sin": sin_t, "cos": cos_t, "swap": swap}
        areas[0] = after_index

        def turn_choice(pe, part):
            if part == 0:
                pe.wait_ge(*i_mask.at(2))
            at_least(pe, i_copied, part)
            for j in GROUPS[part][2]:
                for t in range(j, QT):
                    c = COL[j] - GROUPS[part][0] + (t - j) * P
                    last = nc.tensor.transpose(bank[:, 7, c:c + P],
                                               chosen[:, NOFF[t] + j * P:NOFF[t] + (j + 1) * P].bitcast(F32), ident[:])
            last.then_inc(i_maskt.sem, 1)

        def copy_choice(act, part):
            c, width, _ = GROUPS[part]
            act.wait_ge(*i_maskt.at(part + 1))
            nc.scalar.copy(chosen_t[:, c:c + width], bank[:, 7, 0:width]).then_inc(i_copied.sem, 1)

        diff = softmax_attention("diff", "diff", 4, U_DIFF, layer1, (IN_hi, IN_lo), H_KB,
                                 extra=rotary_extra | {"gq": gq_b, "neg_lam": neg_lam, "before": i_relu, "before_count": 12,
                                                       "last_pair": turn_choice, "last_pair_act": copy_choice,
                                                       "meanwhile": lambda p, part: choose(4 + 15 * p + CHOICE_STEPS[part],
                                                                                        4 + 15 * p + CHOICE_STEPS[part + 1])})

        areas[0] = after_index
        dsa = softmax_attention("dsa", "dsa", 4, U_QA, layer1, None, None, shared={"K": dsa_k, "V": dsa_v},
                                extra=rotary_extra | {"gq": gq_a, "mask": chosen, "maskT": chosen_t,
                                                      "before": i_copied, "before_count": NG})

        XHEADS = 4
        areas[0] = area0
        mem_hi, mem_lo = (area(f"mem_{x}", [P, DT, M], F32R) for x in ("hi", "lo"))
        cross_k = area("cross_k", [P, DT, M], F32)
        cross_v = area("cross_v", [P, MT, D], F32)
        cross_q = area("cross_q", [P, 2, 2, S], F32)
        cross_w = area("cross_w", [P, MT, S], F32)
        cross_sq_at = areas[0]
        cross_sq = area("cross_sq", [P, DT, M], F32)
        mem_squares = tmp_c[:, 0, 0:M]
        mem_rstd = area("mem_rstd", [P, M + MT], F32)
        cross_diag = nc.alloc_sbuf_tensor_at("cross_diag", [P, S], F32R, offset=place_used["tmp_a"])
        cross_max = area("cross_max", [P, QT], F32)
        cross_qh = area("cross_qh", [P, 2, S], F32R)
        cross_kh = nc.alloc_sbuf_tensor_at("cross_kh", [P, DT, M], F32R, offset=cross_sq_at)
        assert areas[0] <= nc.sbuf_usable_end
        c_hi, c_lo, c_sq, c_sum, c_stat, c_ln, c_rstd = (
            sem("mem_" + x) for x in "hi lo sq sum stat ln rstd".split())
        k_out, k_sq, k_stat, k_ln, k_rn, k_done, v_out = (
            again("soft_" + x, n) for x, n in (("yk", DT), ("sqk", 1), ("statk", 1), ("lnk", 2), ("rnk", 1),
                                               ("kn", DT), ("v", MT * DT)))
        q_out, q_sq, q_stat, q_ln, q_rn, q_done = (
            again("soft_" + x, n * XHEADS) for x, n in (("yq", 2), ("sqq", 1), ("statq", 1), ("lnq", 1), ("rnq", 1),
                                                        ("qn", 2)))
        x_qh, x_ln = again("soft_qh", 1 + XHEADS), again("soft_lns", XHEADS)
        x_nat, x_max, x_diag, x_st, x_p, x_o, x_rc, x_od, x_hi, x_lo = (
            again("soft_" + x, n * XHEADS) for x, n in (("nat", 2), ("max", QT), ("diag", QT), ("st", MT), ("p", MT),
                                                        ("o", 3), ("rc", 1), ("od", 2), ("hi", 2), ("lo", 2)))

        @block.scalar
        def _(act):
            act.wait_ge(*m_loaded.at(16))
            act.wait_ge(*dsa["lo"].at(4))
            for c in range(DT):
                nc.scalar.activation(mem_hi[:, c], mem_in[:, c], ACT.Copy, scale=column(gains, G_MEM * DT + c)
                                     ).then_inc(c_hi.sem, 1)
            nc.scalar.activation(cross_sq[:], mem_in[:], ACT.Square).then_inc(c_sq.sem, 1)

        @block.vector
        def _(dve):
            for c in range(DT):
                dve.wait_ge(*c_hi.at(c + 1))
                nc.vector.scalar_tensor_tensor(mem_lo[:, c], mem_in[:, c], column(gains, G_MEM * DT + c),
                                               mem_hi[:, c].bitcast(F32), ALU.mult, ALU.subtract).then_inc(c_lo.sem, 1)
            dve.wait_ge(*c_sq.at(1))
            nc.vector.tensor_reduce(mem_squares, cross_sq[:].rearrange("p c m -> p m c"), AX.X, ALU.add
                                    ).then_inc(c_sum.sem, 1)

        mix_op = Operand("mix", [(G_XATTN, IN_hi, IN_lo)], None)
        def mixed(pe, t):
            pe.wait_ge(*(dsa["lo"].at(t + 1) if t < 4 else diff["lo"].at(t - 3)))

        tile_by_tile("mix", U_OUT2, MID_hi, MID_lo, mixed, mix_op,
                     order=(4, 5, 6, 7, 0, 1, 2, 3))

        @block.tensor
        def _(pe):
            pe.wait_ge(*c_sum.at(1))
            pe.wait_ge(*c_lo.at(DT))
            nc.tensor.matmul(bank[:, 0, 0:M], ones[:], mem_squares, start=True, stop=True)
            for m in range(MT):
                last = nc.tensor.matmul(bank[:, 0, M + m:M + m + 1], mem_squares[:, m * P:(m + 1) * P], ones[:, 0:1],
                                        start=True, stop=True)
            last.then_inc(c_stat.sem, 1)
            for c in range(DT):
                if c < 2:
                    pe.wait_ge(*mix_op.h_done.at(DT + c - 1))
                else:
                    pe.wait_ge(*k_out.at(c - 1))
                unit(pe, U_XK + c, (U_XK + c) % SLOTS, bank[:, 6 + c % 2, 0:M], mem_hi, mem_lo, width=M)

        @block.scalar
        def _(act):
            act.wait_ge(*c_stat.at(1))
            nc.scalar.activation(mem_rstd[:], bank[:, 0, 0:M + MT], ACT.Ln, bias=eps_c[:], scale=1.0 / D
                                 ).then_inc(c_ln.sem, 1)
            act.wait_ge(*c_ln.at(1))
            nc.scalar.activation(mem_rstd[:], mem_rstd[:], ACT.Exp, scale=-0.5).then_inc(c_rstd.sem, 1)

        @block.vector
        def _(dve):
            dve.wait_ge(*c_rstd.at(1))
            for c in range(DT):
                dve.wait_ge(*unit_done.at(U_XK + c + 1))
                nc.vector.tensor_tensor(cross_k[:, c], bank[:, 6 + c % 2, 0:M], mem_rstd[:, 0:M], ALU.mult
                                        ).then_inc(k_out.sem, 1)

        mix_op.stats(1)

        cross_sq_q = nc.alloc_sbuf_tensor_at("cross_sq_q", [P, 2, S], F32, offset=place_used["tmp_b"])
        V_BANKS = (2, 3, 0, 6)
        cross_rn, cross_rc = tmp_a[:, 1], square[:]
        cross_out = nc.alloc_sbuf_tensor_at("cross_out", [P, 2, S], F32, offset=place_used["tmp_c"])

        @block.tensor
        def _(pe):
            def project(h, k):
                at_least(pe, q_out, 2 * (h - 1) + k + 1)
                u = U_XQ0 + k if h == 0 else U_XQ + 2 * (h - 1) + k
                unit(pe, u, u % SLOTS, bank[:, 6 + k], IN_hi, IN_lo)

            def stat(h):
                pe.wait_ge(*q_sq.at(h + 1))
                at_least(pe, x_max, 4 * h)
                for k in range(2):
                    last = nc.tensor.matmul(bank[:, 1], ones[:], cross_sq_q[:, k], start=(k == 0), stop=(k == 1))
                last.then_inc(q_stat.sem, 1)

            def natural(h):
                pe.wait_ge(*x_qh.at(h + 2))
                at_least(pe, x_ln, h)
                for t in range(QT):
                    out = bank[:, t // 2, (t % 2) * M:(t % 2 + 1) * M]
                    for k in range(2):
                        last = nc.tensor.matmul(out, cross_qh[:, k, t * P:(t + 1) * P], cross_kh[:, 2 * h + k],
                                                start=(k == 0), stop=(k == 1))
                    if t % 2 == 1:
                        last.then_inc(x_nat.sem, 1)

            def transposed(h):
                pe.wait_ge(*x_diag.at(4 * h + 4))
                at_least(pe, x_p, 2 * h)
                for m in range(MT):
                    out = bank[:, 2 + m]
                    for k in range(2):
                        nc.tensor.matmul(out, cross_k[:, 2 * h + k, m * P:(m + 1) * P], cross_q[:, h % 2, k],
                                         start=(k == 0), stop=False)
                    nc.tensor.matmul(out, ones_r[:], cross_diag[:], start=False, stop=True).then_inc(x_st.sem, 1)

            def output(h, parts):
                pe.wait_ge(*x_p.at(2 * h + 2))
                at_least(pe, x_od, 2 * h)
                if 0 in parts:
                    for m in range(MT):
                        last = nc.tensor.matmul(bank[:, 0], ones[:], cross_w[:, m], start=(m == 0), stop=(m == MT - 1))
                    last.then_inc(x_o.sem, 1)
                for k in [n - 1 for n in parts if n]:
                    for m in range(MT):
                        c = 2 * h + k
                        last = nc.tensor.matmul(bank[:, 4 + k], cross_v[:, m, c * P:(c + 1) * P], cross_w[:, m],
                                                start=(m == 0), stop=(m == MT - 1))
                    last.then_inc(x_o.sem, 1)

            def key_stats():
                pe.wait_ge(*k_sq.at(1))
                for h in range(XHEADS):
                    out = bank[:, 4 + h // 2, (h % 2) * M:(h % 2 + 1) * M]
                    for k in range(2):
                        last = nc.tensor.matmul(out, ones[:], cross_sq[:, 2 * h + k], start=(k == 0), stop=(k == 1))
                last.then_inc(k_stat.sem, 1)

            def values(c):
                u = U_XV + c
                pe.wait_ge(*w_split.at(u + 1))
                at_least(pe, v_out, 2 * (c - len(V_BANKS) + 1))
                for m in range(MT):
                    out = bank[:, V_BANKS[c % 4], m * P:(m + 1) * P]
                    n = 0
                    for t in range(DT):
                        x = slice(m * P, (m + 1) * P)
                        for a, w in ((mem_hi, w_hi), (mem_hi, w_lo), (mem_lo, w_hi)):
                            last = nc.tensor.matmul(out, a[:, t, x], w[:, u % SLOTS, t * P:(t + 1) * P], start=(n == 0),
                                                    stop=(n == 3 * DT - 1))
                            n += 1
                last.then_inc(unit_done.sem, 1)

            mix_op.add_up(pe)
            pe.wait_ge(*k_out.at(DT))
            project(0, 0)
            project(0, 1)
            key_stats()
            stat(0)
            for c in range(DT):
                values(c)
            pe.wait_ge(*k_done.at(DT))
            pe.wait_ge(*v_out.at(2 * DT))
            for h in range(XHEADS):
                natural(h)
                if h + 1 < XHEADS:
                    project(h + 1, 0)
                transposed(h)
                if h + 1 < XHEADS:
                    project(h + 1, 1)
                output(h, (0,))
                if h + 1 < XHEADS:
                    stat(h + 1)
                output(h, (1, 2))

        @block.scalar
        def _(act):
            def squares(h):
                act.wait_ge(*q_out.at(2 * h + 2))
                at_least(act, q_stat, h)
                nc.scalar.activation(cross_sq_q[:], cross_q[:, h % 2], ACT.Square).then_inc(q_sq.sem, 1)

            def norms(h):
                act.wait_ge(*q_stat.at(h + 1))
                at_least(act, q_done, 2 * h)
                nc.scalar.activation(cross_rn, bank[:, 1], ACT.Ln, bias=eps_c[:], scale=1.0 / M).then_inc(q_ln.sem, 1)
                act.wait_ge(*q_ln.at(h + 1))
                nc.scalar.activation(cross_rn, cross_rn, ACT.Exp, scale=-0.5).then_inc(q_rn.sem, 1)

            def round_q(h):
                act.wait_ge(*q_done.at(2 * h + 2))
                at_least(act, x_nat, 2 * h)
                nc.scalar.copy(cross_qh[:], cross_q[:, h % 2]).then_inc(x_qh.sem, 1)

            act.wait_ge(*k_out.at(DT))
            nc.scalar.activation(cross_sq[:], cross_k[:], ACT.Square).then_inc(k_sq.sem, 1)
            squares(0)
            act.wait_ge(*k_stat.at(1))
            for g in range(2):
                nc.scalar.activation(tmp_c[:, g], bank[:, 4 + g], ACT.Ln, bias=eps_c[:], scale=1.0 / M
                                     ).then_inc(k_ln.sem, 1)
            act.wait_ge(*k_ln.at(2))
            nc.scalar.activation(tmp_c[:], tmp_c[:], ACT.Exp, scale=-0.5).then_inc(k_rn.sem, 1)
            norms(0)
            act.wait_ge(*k_done.at(DT))
            nc.scalar.copy(cross_kh[:], cross_k[:]).then_inc(x_qh.sem, 1)
            round_q(0)
            for c in range(DT):
                act.wait_ge(*unit_done.at(U_XV + c + 1))
                for m in range(MT):
                    nc.scalar.activation(cross_v[:, m, c * P:(c + 1) * P], bank[:, V_BANKS[c % 4], m * P:(m + 1) * P],
                                         ACT.Copy, scale=mem_rstd[:, M + m:M + m + 1]).then_inc(v_out.sem, 1)
            for h in range(XHEADS):
                at_least(act, x_o, 3 * h)
                for m in range(MT):
                    act.wait_ge(*x_st.at(2 * h + m + 1))
                    nc.scalar.activation(cross_w[:, m], bank[:, 2 + m], ACT.Exp).then_inc(x_p.sem, 1)
                if h + 1 < XHEADS:
                    squares(h + 1)
                act.wait_ge(*x_o.at(3 * h + 1))
                at_least(act, x_od, 2 * h)
                nc.scalar.activation(cross_rc, bank[:, 0], ACT.Ln).then_inc(x_ln.sem, 1)
                act.wait_ge(*x_ln.at(h + 1))
                nc.scalar.activation(cross_rc, cross_rc, ACT.Exp, scale=-1.0).then_inc(x_rc.sem, 1)
                if h + 1 < XHEADS:
                    norms(h + 1)
                    round_q(h + 1)
                for k in range(2):
                    act.wait_ge(*x_od.at(2 * h + k + 1))
                    nc.scalar.copy(MID_hi[:, 2 * h + k], cross_out[:, k]).then_inc(x_hi.sem, 1)

        @block.vector
        def _(dve):
            def take(h, k):
                dve.wait_ge(*unit_done.at((U_XQ0 if h == 0 else U_XQ + 2 * (h - 1)) + k + 1))
                at_least(dve, x_st, 2 * (h - 1))
                nc.vector.tensor_tensor(cross_q[:, h % 2, k], bank[:, 6 + k], rstd[:], ALU.mult).then_inc(q_out.sem, 1)

            def finish(h):
                dve.wait_ge(*q_rn.at(h + 1))
                dve.wait_ge(*q_out.at(2 * h + 2))
                for k in range(2):
                    nc.vector.scalar_tensor_tensor(cross_q[:, h % 2, k], cross_q[:, h % 2, k], gq_x[:, k:k + 1], cross_rn,
                                                   ALU.mult, ALU.mult).then_inc(q_done.sem, 1)

            dve.wait_ge(*mix_op.rstd_done.at(1))
            take(0, 0)
            take(0, 1)
            dve.wait_ge(*k_rn.at(1))
            for c in range(DT):
                h = c // 2
                nc.vector.scalar_tensor_tensor(cross_k[:, c], cross_k[:, c], xgains[:, 2 + c % 2:3 + c % 2],
                                               tmp_c[:, h // 2, (h % 2) * M:(h % 2 + 1) * M], ALU.mult, ALU.mult
                                               ).then_inc(k_done.sem, 1)
            finish(0)
            for h in range(XHEADS):
                at_least(dve, x_st, 2 * h)
                for t in range(QT):
                    dve.wait_ge(*x_nat.at(2 * h + t // 2 + 1))
                    nc.vector.tensor_reduce(cross_max[:, t:t + 1], bank[:, t // 2, (t % 2) * M:(t % 2 + 1) * M], AX.X,
                                            ALU.max, negate=True).then_inc(x_max.sem, 1)
                    dve.wait_ge(*x_max.at(4 * h + t + 1))
                    nc.vector.tensor_scalar(cross_diag[:, t * P:(t + 1) * P], ident[:], cross_max[:, t:t + 1], None,
                                            ALU.mult).then_inc(x_diag.sem, 1)
                if h + 1 < XHEADS:
                    take(h + 1, 0)
                    take(h + 1, 1)
                    finish(h + 1)
                dve.wait_ge(*x_rc.at(h + 1))
                at_least(dve, x_lo, 2 * h)
                for k in range(2):
                    dve.wait_ge(*x_o.at(3 * h + k + 2))
                    nc.vector.tensor_tensor(cross_out[:, k], bank[:, 4 + k], cross_rc, ALU.mult).then_inc(x_od.sem, 1)
                for k in range(2):
                    dve.wait_ge(*x_hi.at(2 * h + k + 1))
                    nc.vector.tensor_tensor(MID_lo[:, 2 * h + k], cross_out[:, k], MID_hi[:, 2 * h + k].bitcast(F32),
                                            ALU.subtract).then_inc(x_lo.sem, 1)

        cross_op = Operand("cross", [(G_FFN2, IN_hi, IN_lo)], mix_op)
        tile_by_tile("cross", U_XO, MID_hi, MID_lo, lambda pe, t: pe.wait_ge(*x_lo.at(t + 1)), cross_op)
        cross_op.stats(0)
        feed_forward("conv", U_FFN2, cross_op, None, conv=True)

        stored = sem("stored")

        @block.sync
        def _(sp):
            for c in range(DT):
                sp.wait_ge(*h_final.at(c + 1))
                sp.dma_start(OUT[:, c], hT[:, c]).then_inc(stored.sem, 16)
            sp.wait_ge(*stored.at(16 * DT))


def feature_tiles(a):
    a = a.reshape(a.shape[:-2] + (a.shape[-2] // P, P, a.shape[-1]))
    return np.ascontiguousarray(np.swapaxes(a, -3, -2))


def column_units(w):
    return w.reshape(DT, P, -1, P).transpose(2, 1, 0, 3).reshape(-1, P, UNIT)


def row_units(w):
    return w.reshape(-1, 2, P, 2, 4, P).transpose(3, 0, 2, 1, 4, 5).reshape(-1, P, UNIT)


def ffn_units(w_gu, w_d):
    gate_up = column_units(w_gu).reshape(2, FT, P, UNIT).transpose(1, 0, 2, 3)
    return [gate_up[:FA].reshape(-1, P, UNIT), row_units(w_d[:FA * P]),
            gate_up[FA:].reshape(-1, P, UNIT), column_units(w_d[FA * P:])]


def ple_units(w_gate, w_proj):
    g, p = column_units(w_gate), row_units(w_proj)
    return [p[0:1], g[0:4], p[1:2], g[4:8]]


def interleaved(*ws):
    return np.stack([column_units(w) for w in ws], 1).reshape(-1, P, UNIT)


def padded(w):
    return np.pad(w, ((0, 0), (0, P - w.shape[1])))


def weight_stream(i):
    qkv = i["sb_w_qkv"][0]
    kvf = i["shared_w_kvf"]
    w_in = i["w_in_2"][0]
    qa, ka, va, qi, ki, wi, qb, kb, vb = np.split(w_in, np.cumsum([512, 64, 64, 256, 64, 4, 512, 512])
                                                  .tolist(), axis=1)
    xq = column_units(i["w_xq_2"][0])
    twice = lambda w: np.concatenate([w, w], axis=1)
    units = [interleaved(qkv[:, 0:D], qkv[:, D:2 * D], qkv[:, 2 * D:]), column_units(i["sb_w_o"][0]),
             *ffn_units(i["ffn_w_gu"][0], i["ffn_w_d"][0]), *ple_units(i["ple_w_gate"][0], i["ple_w_proj"][0]),
             column_units(padded(kvf[:, 2 * D:])),
             interleaved(i["fox_w_q"][0], kvf[:, 0:D], kvf[:, D:2 * D]), column_units(i["fox_w_o"][0]),
             *ffn_units(i["ffn_w_gu"][1], i["ffn_w_d"][1]), *ple_units(i["ple_w_gate"][1], i["ple_w_proj"][1]),
             column_units(twice(ki)), column_units(padded(np.concatenate([va, wi], axis=1))), column_units(qi),
             column_units(twice(ka)), interleaved(qb, kb, vb), column_units(qa), column_units(i["w_out_2"][0]),
             column_units(i["w_xk_2"][0]), xq[:2], column_units(i["w_xv_2"][0]), xq[2:],
             column_units(i["w_xo_2"][0]), *ffn_units(i["w_ffn_in_2"][0], i["w_ffn_out_2"][0])]
    return np.concatenate(units)


def kernel(**inputs):
    import concourse.bacc as bacc
    from concourse.bass_utils import run_bass_kernel_spmd

    i = {k: np.asarray(v) for k, v in inputs.items()}
    per_tile = lambda g: g.reshape(-1, P).T
    gains = [i["attn_norm_g"][0], i["ffn_norm_g"][0], i["ple_norm_g"][0], i["attn_norm_g"][1], i["shared_norm_g"],
             i["ffn_norm_g"][1], i["ple_norm_g"][1], i["g_mix_2"][0], i["g_xattn_2"][0], i["g_ffn_2"][0],
             i["g_mem_2"][0]]
    heads = [i["shared_k_norm_g"], i["fox_q_norm_g"][0], i["g_qa_2"][0], i["g_ka_2"][0], i["g_qb_2"][0],
             i["g_kb_2"][0]]
    half = HD // 2
    inv_freq = (1.0 / 10000.0 ** (np.arange(half, dtype=np.float32) / np.float32(half))).astype(np.float32)
    arrays = {
        "W": weight_stream(i),
        "XT": feature_tiles(i["x"][0].T),
        "PT": feature_tiles(np.swapaxes(i["p"][:, 0], 1, 2)),
        "MEMT": feature_tiles(i["mem_2"][0].T),
        "POS": i["positions_2"].astype(np.int32),
        "INVF": np.tile(inv_freq, 4).reshape(P, 1),
        "GAINS": np.concatenate([per_tile(g) for g in gains], axis=1),
        "HGAINS": np.stack([np.tile(g, 2) for g in heads], axis=1),
        "XGAINS": np.concatenate([per_tile(i["g_xq_2"][0]), per_tile(i["g_xk_2"][0])], axis=1),
        "BF": i["shared_b_f"].reshape(HEADS, 1),
        "LAM": np.concatenate([i["lam_q1_2"], i["lam_k1_2"], i["lam_q2_2"], i["lam_k2_2"]]).T,
        "CONV": np.stack([*i["conv_w_2"][0], i["conv_b_2"][0]]).reshape(4, FT, P).transpose(2, 1, 0)
                .reshape(P, 4 * FT),
    }
    arrays = {k: np.ascontiguousarray(a) for k, a in arrays.items()}
    nc = bacc.Bacc("TRN2", target_bir_lowering=False, num_devices=1)
    args = [nc.dram_tensor(k, a.shape, mybir.dt.from_np(a.dtype), kind="ExternalInput").ap()
            for k, a in arrays.items()]
    out = nc.dram_tensor("OUT", [P, DT, S], F32, kind="ExternalOutput").ap()
    build_program(nc, *args, out)
    r = run_bass_kernel_spmd(nc, [arrays], core_ids=[0])
    got = r.results[0]["OUT"]
    return np.ascontiguousarray(got.transpose(1, 0, 2).reshape(D, S).T)[None]
```
